# Optimizing a Trainium2 kernel written in Bass

```python
import jax, jax.numpy as jnp
from jax import lax
import numpy as np

D_MODEL = 1024
BATCH = 1
SEQ = 1024
DEPTH = 2

N_MIX = 2
N_RWKV = (DEPTH + 1) // 2
N_ATTN = DEPTH // 2
N_VRES = max(N_RWKV - 1, 0)
RWKV_HEAD = 64
RWKV_HEADS = D_MODEL // RWKV_HEAD
DECAY_LORA = 64
ICLR_LORA = 64
VRES_LORA = 32
GATE_LORA = 128
GN_EPS = 64e-5
HEAD_DIM = 64
N_Q_HEADS = D_MODEL // HEAD_DIM
N_KV_HEADS = 4
GROUP = N_Q_HEADS // N_KV_HEADS
QKV_DIM = (N_Q_HEADS + 2 * N_KV_HEADS) * HEAD_DIM
WINDOW = 128
BLOCK = 128
ROPE_THETA = 500000.0
ROPE_DIM = HEAD_DIM // 4
D_FF = ((8 * D_MODEL // 3 + 255) // 256) * 256
RMS_EPS = 1e-6

kernel_name = "hybrid_rwkv7_swa_sink_swiglu_sandwich"

def rmsnorm(x, g):
    xf = x.astype(jnp.float32)
    y = xf * lax.rsqrt(jnp.mean(xf * xf, axis=-1, keepdims=True) + RMS_EPS)
    return (y * g.astype(jnp.float32)).astype(x.dtype)

def wkv7_scan(r, decay, k, v, a, b):
    Bsz, _, H, N = r.shape
    xs = tuple(jnp.moveaxis(t, 1, 0) for t in (r, decay, k, v, a, b))

    def step(S, inp):
        r_t, w_t, k_t, v_t, a_t, b_t = inp
        sa = jnp.einsum('bhvk,bhk->bhv', S, a_t)
        S = S * w_t[:, :, None, :] + sa[..., None] * b_t[:, :, None, :] + v_t[..., None] * k_t[:, :, None, :]
        y = jnp.einsum('bhvk,bhk->bhv', S, r_t)
        return S, y

    S0 = jnp.zeros((Bsz, H, N, N), jnp.float32)
    _, ys = lax.scan(step, S0, xs)
    return jnp.moveaxis(ys, 0, 1)

def rwkv7_time_mix(x, v_first, x_mix, w_rkv, w0, w1, w2, a0, a1, a2, g1, g2,
                   k_k, k_a, r_k, lnx_w, lnx_b, w_o, vres):
    Bsz, T, C = x.shape
    H, N = RWKV_HEADS, RWKV_HEAD
    f32 = jnp.float32
    x_prev = jnp.pad(x, ((0, 0), (1, 0), (0, 0)))[:, :-1]
    xx = x_prev - x
    xm = x[:, :, None, :] + xx[:, :, None, :] * x_mix
    rkv = jnp.einsum('btjc,jcd->btjd', xm[:, :, :3], w_rkv)
    r, k, v = rkv[:, :, 0], rkv[:, :, 1], rkv[:, :, 2]
    xv, xw, xa, xg = xm[:, :, 2], xm[:, :, 3], xm[:, :, 4], xm[:, :, 5]

    w_log = -jax.nn.softplus(-(w0 + jnp.tanh(xw @ w1) @ w2).astype(f32)) - 0.5
    if vres is None:
        v_first = v
    else:
        v0, v1, v2 = vres
        v = v + (v_first - v) * jax.nn.sigmoid(v0 + (xv @ v1) @ v2)
    a = jax.nn.sigmoid(a0 + (xa @ a1) @ a2)
    g = jax.nn.sigmoid(xg @ g1) @ g2

    kk = (k * k_k).reshape(Bsz, T, H, N).astype(f32)
    kk = kk / jnp.maximum(jnp.sqrt(jnp.sum(kk * kk, -1, keepdims=True)), 1e-12)
    k = k * (1 + (a - 1) * k_a)

    rh = r.reshape(Bsz, T, H, N).astype(f32)
    kh = k.reshape(Bsz, T, H, N).astype(f32)
    vh = v.reshape(Bsz, T, H, N).astype(f32)
    ah = a.reshape(Bsz, T, H, N).astype(f32)
    decay = jnp.exp(-jnp.exp(w_log)).reshape(Bsz, T, H, N)
    y = wkv7_scan(rh, decay, kh, vh, -kk, kk * ah)

    mu = jnp.mean(y, -1, keepdims=True)
    var = jnp.mean(jnp.square(y - mu), -1, keepdims=True)
    y = ((y - mu) * lax.rsqrt(var + GN_EPS)).reshape(Bsz, T, C)
    y = y * lnx_w.astype(f32) + lnx_b.astype(f32)
    bonus = jnp.sum(rh * kh * r_k.astype(f32), -1, keepdims=True) * vh
    y = (y + bonus.reshape(Bsz, T, C)).astype(x.dtype)
    return (y * g) @ w_o, v_first

def rope_tables(T):
    pos = jnp.arange(T, dtype=jnp.float32)
    inv_freq = ROPE_THETA ** (-jnp.arange(0, ROPE_DIM, 2, dtype=jnp.float32) / ROPE_DIM)
    ang = pos[:, None] * inv_freq[None, :]
    return jnp.cos(ang), jnp.sin(ang)

def apply_partial_rope(t, cos, sin):
    tr = t[..., :ROPE_DIM].astype(jnp.float32)
    t1, t2 = tr[..., :ROPE_DIM // 2], tr[..., ROPE_DIM // 2:]
    c, s = cos[None, :, None, :], sin[None, :, None, :]
    rot = jnp.concatenate([t1 * c - t2 * s, t2 * c + t1 * s], axis=-1)
    return jnp.concatenate([rot.astype(t.dtype), t[..., ROPE_DIM:]], axis=-1)

def swa_sink_attention(x, w_qkv, b_qkv, sinks, w_o, b_o, cos, sin):
    Bsz, T, C = x.shape
    nb = T // BLOCK
    qkv = x @ w_qkv + b_qkv
    q = qkv[..., :N_Q_HEADS * HEAD_DIM].reshape(Bsz, T, N_Q_HEADS, HEAD_DIM)
    k = qkv[..., N_Q_HEADS * HEAD_DIM:(N_Q_HEADS + N_KV_HEADS) * HEAD_DIM].reshape(Bsz, T, N_KV_HEADS, HEAD_DIM)
    v = qkv[..., (N_Q_HEADS + N_KV_HEADS) * HEAD_DIM:].reshape(Bsz, T, N_KV_HEADS, HEAD_DIM)
    q = apply_partial_rope(q, cos, sin)
    k = apply_partial_rope(k, cos, sin)

    q = q.reshape(Bsz, nb, BLOCK, N_KV_HEADS, GROUP, HEAD_DIM)
    k = k.reshape(Bsz, nb, BLOCK, N_KV_HEADS, HEAD_DIM)
    v = v.reshape(Bsz, nb, BLOCK, N_KV_HEADS, HEAD_DIM)

    def with_prev(t):
        prev = jnp.pad(t, ((0, 0), (1, 0), (0, 0), (0, 0), (0, 0)))[:, :-1]
        return jnp.concatenate([prev, t], axis=2)

    kb, vb = with_prev(k), with_prev(v)
    s = jnp.einsum('bnqhgd,bnkhd->bnhgqk', q, kb).astype(jnp.float32) * (HEAD_DIM ** -0.5)

    qi = jnp.arange(BLOCK)[:, None]
    kj = jnp.arange(2 * BLOCK)[None, :]
    rel = qi + BLOCK - kj
    band = (rel >= 0) & (rel < WINDOW)
    valid = band[None] & ((jnp.arange(nb)[:, None, None] > 0) | (kj[None] >= BLOCK))
    s = jnp.where(valid[None, :, None, None], s, -jnp.inf)

    sink = sinks.astype(jnp.float32).reshape(N_KV_HEADS, GROUP)[None, None, :, :, None, None]
    m = jnp.maximum(jnp.max(s, -1, keepdims=True), sink)
    p = jnp.exp(s - m)
    p = p / (jnp.sum(p, -1, keepdims=True) + jnp.exp(sink - m))
    o = jnp.einsum('bnhgqk,bnkhd->bnqhgd', p.astype(x.dtype), vb).reshape(Bsz, T, N_Q_HEADS * HEAD_DIM)
    return o @ w_o + b_o

def swiglu_ffn(x, w_gate_up, w_down):
    h = x @ w_gate_up
    gate, up = h[..., :D_FF], h[..., D_FF:]
    return (jax.nn.silu(gate) * up) @ w_down

def setup_inputs(seed: int = 0) -> dict:
    key = jax.random.key(seed)
    ks = iter(jax.random.split(key, 40))
    D, H, N = D_MODEL, RWKV_HEADS, RWKV_HEAD
    nrm = lambda shape, scale: scale * jax.random.normal(next(ks), shape, jnp.float32)
    return {
        "x": nrm((BATCH, SEQ, D), 1.0),
        "norm_g": 1.0 + nrm((DEPTH, 4, D), 0.05),
        "rwkv_x_mix": jax.random.uniform(next(ks), (N_RWKV, 6, D), jnp.float32),
        "rwkv_w_rkv": nrm((N_RWKV, 3, D, D), D ** -0.5),
        "rwkv_w0": jax.random.uniform(next(ks), (N_RWKV, D), jnp.float32, -6.5, -1.5),
        "rwkv_w1": nrm((N_RWKV, D, DECAY_LORA), D ** -0.5),
        "rwkv_w2": nrm((N_RWKV, DECAY_LORA, D), 0.1 * DECAY_LORA ** -0.5),
        "rwkv_a0": nrm((N_RWKV, D), 0.1),
        "rwkv_a1": nrm((N_RWKV, D, ICLR_LORA), D ** -0.5),
        "rwkv_a2": nrm((N_RWKV, ICLR_LORA, D), 0.5 * ICLR_LORA ** -0.5),
        "rwkv_v0": 1.0 + nrm((N_VRES, D), 0.1),
        "rwkv_v1": nrm((N_VRES, D, VRES_LORA), D ** -0.5),
        "rwkv_v2": nrm((N_VRES, VRES_LORA, D), 0.5 * VRES_LORA ** -0.5),
        "rwkv_g1": nrm((N_RWKV, D, GATE_LORA), D ** -0.5),
        "rwkv_g2": nrm((N_RWKV, GATE_LORA, D), GATE_LORA ** -0.5),
        "rwkv_k_k": 0.85 + nrm((N_RWKV, D), 0.05),
        "rwkv_k_a": 1.0 + nrm((N_RWKV, D), 0.05),
        "rwkv_r_k": -0.04 + nrm((N_RWKV, H, N), 0.05),
        "rwkv_lnx_w": 1.0 + nrm((N_RWKV, D), 0.05),
        "rwkv_lnx_b": nrm((N_RWKV, D), 0.02),
        "rwkv_w_o": nrm((N_RWKV, D, D), D ** -0.5),
        "attn_w_qkv": nrm((N_ATTN, D, QKV_DIM), D ** -0.5),
        "attn_b_qkv": nrm((N_ATTN, QKV_DIM), 0.02),
        "attn_sinks": nrm((N_ATTN, N_Q_HEADS), 1.0),
        "attn_w_o": nrm((N_ATTN, N_Q_HEADS * HEAD_DIM, D), (N_Q_HEADS * HEAD_DIM) ** -0.5),
        "attn_b_o": nrm((N_ATTN, D), 0.02),
        "ffn_w_gate_up": nrm((DEPTH, D, 2 * D_FF), D ** -0.5),
        "ffn_w_down": nrm((DEPTH, D_FF, D), D_FF ** -0.5),
    }

def reference(x, norm_g, rwkv_x_mix, rwkv_w_rkv, rwkv_w0, rwkv_w1, rwkv_w2, rwkv_a0, rwkv_a1,
              rwkv_a2, rwkv_v0, rwkv_v1, rwkv_v2, rwkv_g1, rwkv_g2, rwkv_k_k, rwkv_k_a, rwkv_r_k,
              rwkv_lnx_w, rwkv_lnx_b, rwkv_w_o, attn_w_qkv, attn_b_qkv, attn_sinks, attn_w_o,
              attn_b_o, ffn_w_gate_up, ffn_w_down):
    cos, sin = rope_tables(x.shape[1])
    v_first = None
    for i in range(DEPTH):
        j = i // N_MIX
        h = rmsnorm(x, norm_g[i, 0])
        if i % N_MIX == 0:
            vres = None if j == 0 else (rwkv_v0[j - 1], rwkv_v1[j - 1], rwkv_v2[j - 1])
            h, v_first = rwkv7_time_mix(
                h, v_first, rwkv_x_mix[j], rwkv_w_rkv[j], rwkv_w0[j], rwkv_w1[j], rwkv_w2[j],
                rwkv_a0[j], rwkv_a1[j], rwkv_a2[j], rwkv_g1[j], rwkv_g2[j], rwkv_k_k[j],
                rwkv_k_a[j], rwkv_r_k[j], rwkv_lnx_w[j], rwkv_lnx_b[j], rwkv_w_o[j], vres)
        else:
            h = swa_sink_attention(h, attn_w_qkv[j], attn_b_qkv[j], attn_sinks[j],
                                   attn_w_o[j], attn_b_o[j], cos, sin)
        x = x + rmsnorm(h, norm_g[i, 1])
        h = swiglu_ffn(rmsnorm(x, norm_g[i, 2]), ffn_w_gate_up[i], ffn_w_down[i])
        x = x + rmsnorm(h, norm_g[i, 3])
    return x


_drawn_inputs = setup_inputs


def setup_inputs(seed=0):
    import zlib

    import numpy as np

    out = dict(_drawn_inputs(seed))
    spreads = {}
    factors = {'rwkv_w1': 8.0, 'rwkv_w2': 8.0, 'attn_sinks': 6.84}
    for name, (base, spread) in spreads.items():
        noise = np.random.default_rng([zlib.crc32(name.encode()), seed]).standard_normal(out[name].shape)
        drawn = base * np.exp(spread * noise) if base else spread * noise
        out[name] = __import__('jax').numpy.asarray(drawn.astype(out[name].dtype))
    for name, factor in factors.items():
        out[name] = (out[name] * factor).astype(out[name].dtype)
    return out
```

```python
from contextlib import ExitStack

import numpy as np

import concourse.bass as bass
from concourse import mybir

F32 = mybir.dt.float32
F32R = mybir.dt.float32r
ALU = mybir.AluOpType
ACT = mybir.ActivationFunctionType
AX_X = mybir.AxisListType.X
LN_EXP = "natural_log_exp_and_others"

P = 128
D = 1024
T = 1024
KT = D // P
HALF = 512
D_FF = 2816
FG = D_FF // (2 * P)
HD = 64
C = 64
NHP = D // P
DECAY = float(np.exp(-0.5))
RMS_EPS = 1e-6
GN_EPS = 64e-5
SCALE = HD ** -0.5
NKV = 4
NB = T // P
LN_SHIFT = 17

N_RKV, N_LORA, N_WO = 0, 24, 27
N_F0 = N_WO + 8
N_QKV = N_F0 + 6 * FG
N_AO = N_QKV + 12
N_F1 = N_AO + 8
N_ALL = N_F1 + 6 * FG

G0, MIX, W0, A0, KK, KA, RK, LNW, LNB = 0, 64, 112, 120, 128, 136, 144, 152, 160
BQKV, BO, SINK, EPS_RMS, EPS_GN, KSH = 168, 180, 188, 204, 205, 206
NPAR = 207


def shape_constants():
    i = np.arange(P)
    same = lambda n: (i[:, None] // n) == (i[None, :] // n)
    up = i[None, :] > i[:, None]
    ident = np.eye(P)
    blk = same(HD)
    strict = same(C) & up
    incl = same(C) & (up | np.eye(P, dtype=bool))
    e = [same(2 * b) & ~same(b) & up for b in (8, 16, 32)]
    base = np.concatenate([ident, np.ones((P, P)), blk], 1).astype(np.float32)
    rst = np.tile((np.arange(HALF) % C != 0).astype(np.float32), (P, 1))
    rw = np.concatenate([rst, strict, incl, same(8) & up] + e, 1).astype(np.float32)
    rope = HD // 4
    inv = np.float32(500000.0) ** (-np.arange(0, rope, 2, dtype=np.float32) / np.float32(rope))
    ang = np.arange(T, dtype=np.float32)[:, None] * inv[None, :].astype(np.float32)
    cos, sin = np.ones((P, T), np.float32), np.zeros((P, T), np.float32)
    perm = np.zeros((P, P), np.float32)
    for h in (0, HD):
        for d in range(rope // 2):
            lo, hi = h + d, h + d + rope // 2
            cos[lo] = cos[hi] = np.cos(ang[:, d])
            sin[lo] = sin[hi] = np.sin(ang[:, d])
            perm[hi, lo] = -1.0
            perm[lo, hi] = 1.0
    qi, kj = np.arange(P)[:, None], np.arange(2 * P)[None, :]
    rel = qi + P - kj
    band = (rel >= 0) & (rel < P)
    far = np.float32(-1e30)
    m = np.where(band, 0, far).astype(np.float32)
    m0 = np.where(band & (kj >= P), 0, far).astype(np.float32)
    at = np.concatenate([cos, sin, perm, m0, m], 1).astype(np.float32)
    return base, rw, at


def build_program(nc, xT, wt, par, lora2, cbase, crw, cat, out):
    ctx = ExitStack()
    with ctx:
        def keep(stack, name, shape, dt=F32):
            return stack.enter_context(nc.sbuf_tensor(name, shape, dt))

        def sem(name):
            return ctx.enter_context(nc.semaphore(name))

        xh = keep(ctx, "xh", [P, KT, T], F32R)
        xl = keep(ctx, "xl", [P, KT, T], F32R)
        wst = keep(ctx, "wst", [P, 2, T])
        wh = keep(ctx, "wh", [P, 2, T], F32R)
        wl = keep(ctx, "wl", [P, 2, T], F32R)
        sqb = keep(ctx, "sqb", [P, 2, T])
        tmp = keep(ctx, "tmp", [P, 2, T])
        cb = keep(ctx, "cb", [P, 3 * P])
        pr = keep(ctx, "pr", [P, NPAR])
        ident, ones, blk = (cb[:, i * P:(i + 1) * P] for i in range(3))
        rstd = keep(ctx, "rstd", [P, T])
        ps = ctx.enter_context(nc.psum_tensor("ps", [P, 4, T], F32))

        s_n = ExitStack()
        x = keep(s_n, "x", [P, KT, T])
        y = keep(s_n, "y", [P, KT, T])
        hidh = keep(s_n, "hidh", [P, 2, 2, T], F32R)
        hidl = keep(s_n, "hidl", [P, 2, 2, T], F32R)
        s_n.close()
        s_ab = ExitStack()
        lor = keep(s_ab, "lor", [P, 3, T])
        s_a = ExitStack()
        h = keep(s_a, "h", [P, KT, T + 1])
        xx = keep(s_a, "xx", [P, KT, T])
        ost = keep(s_a, "ost", [P, 2, T])
        s_a.close()
        s_b = ExitStack()
        cr = keep(s_b, "cr", [P, 512 + 6 * P])
        rst, m_si, mu8 = cr[:, 0:512], cr[:, 512:768], cr[:, 768:896]
        me = [cr[:, 896 + P * i:1024 + P * i] for i in range(3)]
        l2 = keep(s_b, "l2", [P, 2, P])
        l2g = keep(s_b, "l2g", [P, P])
        rin = keep(s_b, "rin", [P, HALF])
        kin = keep(s_b, "kin", [P, HALF])
        vin = keep(s_b, "vin", [P, 2, HALF])
        At, Bt, Kt, Rt, bon = (keep(s_b, n, [P, 2, HALF]) for n in ("At", "Bt", "Kt", "Rt", "bon"))
        pend = keep(s_b, "pend", [P, 2, 8])
        pcp = keep(s_b, "pcp", [P, 6])
        pcq = keep(s_b, "pcq", [P, 2])
        Sm = [[keep(s_b, f"Sm{a}{g}", [P, 2, 4, P]) for g in range(2)] for a in range(2)]
        TT = [[keep(s_b, f"TT{a}{g}", [P, 2, 2, P]) for g in range(2)] for a in range(2)]
        tok = [[keep(s_b, f"tok{a}{g}", [P, 3, P]) for g in range(2)] for a in range(2)]
        Et = [keep(s_b, f"Et{g}", [P, 3, 2, P]) for g in range(2)]
        Dt = [keep(s_b, f"Dt{g}", [P, 2, P]) for g in range(2)]
        Dn = [keep(s_b, f"Dn{g}", [P, 2, P]) for g in range(2)]
        D2 = [keep(s_b, f"D2{g}", [P, 2, 2, P]) for g in range(2)]
        Wm = [keep(s_b, f"Wm{g}", [P, 2, P]) for g in range(2)]
        rhs_sb = keep(s_b, "rhs_sb", [P, P])
        SA = [keep(s_b, f"SA{g}", [P, P]) for g in range(2)]
        S = keep(s_b, "S", [P, P])
        SP = keep(s_b, "SP", [P, P])
        ysb = keep(s_b, "ysb", [P, HALF])
        psq, zt = rstd[:, 0:HALF], rstd[:, HALF:T]
        s_b.close()
        s_ab.close()
        s_c = ExitStack()
        q = keep(s_c, "q", [P, KT, T])
        kd = keep(s_c, "kd", [P, NKV, T + P])
        vt = keep(s_c, "vt", [P, NB + 1, NKV, HD])
        ca = keep(s_c, "ca", [P, 2 * T + P + 4 * P])
        cosT, sinT, perm = ca[:, 0:T], ca[:, T:2 * T], ca[:, 2 * T:2 * T + P]
        msk = [ca[:, 2 * T + P + 256 * i:2 * T + P + 256 * i + 256] for i in range(2)]
        sc = keep(s_c, "sc", [P, 2, T])
        pT = keep(s_c, "pT", [P, 2, 4 * P])
        st = keep(s_c, "st", [P, 2, 6, 4])
        s_c.close()

        T0, T1, T2, T3 = (sqb[:, i // 2, (i % 2) * HALF:(i % 2) * HALF + HALF] for i in range(4))
        T4, T5, T6, T7 = (tmp[:, i // 2, (i % 2) * HALF:(i % 2) * HALF + HALF] for i in range(4))

        rkv_d = nc.dram_tensor("rkv_scratch", [3, NHP, P, T], F32).ap()
        x_d = nc.dram_tensor("x_scratch", [P, KT, T], F32).ap()

        c_in, a_in = sem("const_loaded"), sem("phase_const_loaded")
        w_dma = [sem("w_loaded0"), sem("w_loaded1")]
        w_hi, w_split, w_used = sem("w_hi_ready"), sem("w_split_ready"), sem("w_tile_used")
        mm_evac = sem("tile_evacuated")
        x_in, x_out = sem("x_loaded"), sem("x_saved")
        sq_ready, sq_used, rs_ready = sem("square_ready"), sem("square_used"), sem("rstd_ready")
        xn_ready, xhi_ready, x_ready = sem("normed_ready"), sem("x_hi_ready"), sem("x_split_ready")
        act_own, dve_own, pool_own = sem("scalar_step"), sem("vector_step"), sem("pool_step")
        h_ready, xx_ready = sem("h_ready"), sem("shift_diff_ready")
        o_full, o_dma = [sem("spill0_full"), sem("spill1_full")], [sem("spill0_written"), sem("spill1_written")]
        lo_ready = sem("lora_ready")
        res_done = sem("residual_done")
        sg_ready, up_mul, hid_hi, hid_ready = (sem(n) for n in ("silu_ready", "hidden_ready", "hidden_hi_ready", "hidden_split"))
        dn_full, dn_evac, y_zero = sem("down_full"), sem("down_added"), sem("y_zeroed")
        st_full = [sem(f"st{i}_full") for i in range(14)]
        st_evac = [sem(f"st{i}_evac") for i in range(14)]
        dt_ready, x1_ready = sem("Dt_ready"), sem("X1_ready")
        e_ready = sem("E_ready")
        rhs_full, rhs_sbr, sa_full, sa_sbr, ds_full, s_ready = (sem(n) for n in (
            "rhs_full", "rhs_copied", "sa_full", "sa_copied", "chunk_done", "state_ready"))
        l_in, lg_in, r_in, k_in = sem("l2_loaded"), sem("l2g_loaded"), sem("r_loaded"), sem("k_loaded")
        v_in = [sem("v_loaded0"), sem("v_loaded1")]
        zw_f, za_f, mean_f, ss_f, var_f, g_f, bon_f = (sem(n + "_full") for n in ("zw", "za", "mean", "ss", "var", "g", "bonus"))
        zw_e, za_e, mean_e, ss_e, var_e, g_e, bon_e = (sem(n + "_read") for n in ("zw", "za", "mean", "ss", "var", "g", "bonus"))
        ksq_r, s_r, sm_r, P_r, ssm_r, rinv_r, prep_done, rk_r, sp_ready = (sem(n) for n in (
            "key_square", "decay_sum", "decay_sum_prev", "decays", "ss_clamped", "key_rnorm", "prep_done", "rk_ready", "state_decayed"))
        y_sb, yc_r, ysq_r, yrs_r, z_r, zhi_r, z_ready = (sem(n) for n in (
            "y_copied", "y_centred", "y_square", "y_rstd", "z_ready", "z_hi", "z_split"))
        pq_r = sem("post_params")
        y_tile, pp_r = sem("y_tile_done"), sem("prep_params")
        raw_r, rot_f, rot_r = sem("qkv_raw"), sem("rotated_full"), sem("rope_done")
        vtr_f, vtr_r, kd_r, pad_r = sem("v_transposed"), sem("v_tokens"), sem("keys_ready"), sem("kv_padded")
        s_f, sm_m, nm_r, p_r, p_n, pt_f, pt_r, o_f, o_r = (sem(n) for n in (
            "scores_full", "scores_masked", "max_ready", "probs_ready", "probs_normed",
            "pT_full", "pT_copied", "o_full", "o_hi"))
        oz_r = sem("o_split")
        st_out = sem("out_written")

        class Own:
            def __init__(self, eng, s):
                self.eng, self.s, self.n, self.r = eng, s, 0, 0

            def link(self, ins):
                self.n += 1
                ins.then_inc(self.s, 1)
                self.eng.wait_ge(self.s, self.r + self.n)

        def bank(b):
            return ps[:, b // 2, (b % 2) * HALF:(b % 2) * HALF + HALF]

        def halves():
            return [(0, HALF), (HALF, T)]

        def inv_bank(s, g):
            return (2 * s + g) % 3

        def prior(s, g):
            e = 2 * s + g
            if e >= 3:
                return (e - 3) // 2, (e - 3) % 2, 0
            e = {0: 27, 1: 25, 2: 26}[e]
            return e // 2, e % 2, 1

        B_SC, B_Y, B_AUX0, B_AUX1 = 3, 4, 5, 6
        block = ctx.enter_context(nc.Block())

        @block.sync
        def _(sp):
            sp.dma_start(cb[:], cbase).then_inc(c_in, 16)
            sp.dma_start(pr[:], par).then_inc(c_in, 16)
            sp.dma_start(wst[:, 0, :], wt[0]).then_inc(w_dma[0], 16)
            sp.dma_start(wst[:, 1, :], wt[1]).then_inc(w_dma[1], 16)
            with sp.Fori(0, (N_ALL - 3) // 2) as i:
                for u in range(2):
                    sp.wait_ge(w_split, 2 * i + u + 1)
                    sp.dma_start(wst[:, u, :], wt[2 * i + 2 + u]).then_inc(w_dma[u], 16)
            sp.wait_ge(w_split, N_ALL - 2)
            sp.dma_start(wst[:, 0, :], wt[N_ALL - 1]).then_inc(w_dma[0], 16)

        @block.gpsimd
        def _(pool):
            own = Own(pool, pool_own)
            pool.dma_start(h[:, :, 1:T + 1], xT).then_inc(x_in, 16)
            own.link(pool.memset(h[:, :, 0:1], 0.0))
            for kt in range(KT):
                pool.wait_ge(h_ready, kt + 1)
                pool.tensor_tensor(xx[:, kt, :], h[:, kt, 0:T], h[:, kt, 1:T + 1], ALU.subtract).then_inc(xx_ready, 1)
            with pool.Fori(0, 12) as i:
                for u in range(2):
                    pool.wait_ge(o_full[u], i + 1)
                    pool.dma_start(rkv_d.rearrange("a b p t -> (a b) p t")[2 * i + u], ost[:, u, :]).then_inc(o_dma[u], 16)
            pool.wait_ge(x_ready, 6 * KT)
            pool.wait_ge(o_dma[0], 16 * 12)
            pool.wait_ge(o_dma[1], 16 * 12)
            pool.dma_start(cr[:], crw).then_inc(a_in, 16)

            def load_piece(hp, pc, first):
                r = 2 * hp + pc
                if not first:
                    pool.wait_ge(prep_done, r)
                if pc == 0:
                    if not first:
                        pool.wait_ge(za_f, r)
                    pool.dma_start(l2[:], lora2[hp][:, 0:2, :]).then_inc(l_in, 16)
                if not first:
                    pool.wait_ge(bon_e, r)
                if not (first or (pc == 1 and type(hp) is int and hp == 0)):
                    pool.wait_ge(st_full[2], 8 * hp + 4 * pc - 4)
                cols = slice(pc * HALF, pc * HALF + HALF)
                pool.dma_start(rin[:], rkv_d[0, hp][:, cols]).then_inc(r_in, 16)
                pool.dma_start(kin[:], rkv_d[1, hp][:, cols]).then_inc(k_in, 16)
                pool.dma_start(vin[:, pc, :], rkv_d[2, hp][:, cols]).then_inc(v_in[pc], 16)

            def load_g(hp, first):
                if not first:
                    pool.wait_ge(g_f, 2 * hp)
                pool.dma_start(l2g[:], lora2[hp][:, 2, :]).then_inc(lg_in, 16)

            def merge_masks(k, a, nopr):
                for g in range(2):
                    pool.wait_ge(st_evac[1], 2 * k + g + 1)
                    if not nopr:
                        pool.wait_ge(st_full[12], 2 * k + g - 1)
                    for lv in range(3):
                        ins = pool.tensor_tensor(Et[g][:, lv], Sm[a][g][:, :, 0, :],
                                                 me[lv].unsqueeze(1).to_broadcast([P, 2, P]), ALU.mult)
                    ins.then_inc(e_ready, 1)

            def body(hp, first, last):
                load_piece(hp, 1, False)
                merge_masks(4 * hp + 1, 1, False)
                load_g(hp, first)
                merge_masks(4 * hp + 2, 0, False)
                if not last:
                    load_piece(hp + 1, 0, False)
                merge_masks(4 * hp + 3, 1, False)
                if not last:
                    merge_masks(4 * hp + 4, 0, False)

            load_piece(0, 0, True)
            pool.wait_ge(a_in, 16)
            merge_masks(0, 0, True)
            body(0, True, False)
            with pool.Fori(1, NHP - 1) as hp:
                body(hp, False, False)
            body(NHP - 1, False, True)

            pool.wait_ge(z_ready, 16)
            pool.wait_ge(ds_full, 16 * NHP)
            pool.wait_ge(e_ready, 2 * 32)
            pool.dma_start(x[:], xT).then_inc(x_in, 16)

            def ffn_zero(L):
                pool.wait_ge(res_done, KT * (2 * L + 1))
                pool.memset(y[:], 0.0).then_inc(y_zero, 1)

            ffn_zero(0)
            pool.wait_ge(res_done, KT * 2)
            pool.dma_start(x_d, x[:]).then_inc(x_out, 16)
            pool.wait_ge(x_out, 16)
            pool.wait_ge(xn_ready, KT * 2)
            pool.dma_start(ca[:], cat).then_inc(a_in, 16)
            pool.memset(kd[:, :, 0:P], 0.0)
            pool.memset(vt[:, 0, :, :], 0.0).then_inc(pad_r, 1)
            pool.wait_ge(oz_r, NB * NKV)
            pool.dma_start(x[:], x_d).then_inc(x_in, 16)
            ffn_zero(1)
            for kt in range(KT):
                pool.wait_ge(res_done, KT * 3 + kt + 1)
                pool.dma_start(out[:, kt, :], x[:, kt, :]).then_inc(st_out, 16)
            pool.wait_ge(st_out, 16 * KT)

        @block.tensor
        def _(pe):
            pe.wait_ge(c_in, 32)

            def dense(n, r, slot, free, xb):
                pe.wait_ge(w_split, n + r + 1)
                if free is not None:
                    pe.wait_ge(mm_evac, free + r)
                for kt in range(KT):
                    if xb is not None:
                        pe.wait_ge(x_ready, xb + kt + 1)
                    for j, (a, b) in enumerate(((wh, xh), (wh, xl), (wl, xh))):
                        for lo, hi in halves():
                            ins = pe.matmul(ps[:, slot, lo:hi], a[:, n % 2, kt * P:(kt + 1) * P],
                                            b[:, kt, lo:hi], start=(kt == 0 and j == 0),
                                            stop=(kt == KT - 1 and j == 2))
                ins.then_inc(w_used, 1)

            def stats(nn):
                for kt in range(KT):
                    pe.wait_ge(sq_ready, KT * nn + kt + 1)
                    for lo, hi in halves():
                        ins = pe.matmul(ps[:, 3, lo:hi], ones, sqb[:, kt % 2, lo:hi],
                                        start=(kt == 0), stop=(kt == KT - 1))
                    ins.then_inc(sq_used, 1)

            stats(0)
            def rkv(j, t, r):
                n = 8 * j + t
                if n >= 4:
                    pe.wait_ge(o_full[t % 2], (n - 4) // 2 + 1 + 2 * r)
                dense(n, 4 * r, t % 4, None, KT * j)

            for t in range(8):
                rkv(0, t, 0)
            for j in (1, 2):
                with pe.Fori(0, 2) as i:
                    for t in range(4):
                        rkv(j, t, i)
            for j in range(3):
                n = N_LORA + j
                pe.wait_ge(o_full[n % 2], (n - 4) // 2 + 1)
                dense(n, 0, n % 4, None, KT * (3 + j))

            def mm(o, a, b, start, stop=True):
                return pe.matmul(o, a, b, start=start, stop=stop, skip_group_check=True)

            def stage(s, g, k, a, nopr):
                b = bank(inv_bank(s, g))
                ps_, pg, back = prior(s, g)
                if not (back and nopr):
                    pe.wait_ge(st_evac[ps_], 2 * (k - back) + pg + 1)
                cols = slice(a * 256 + g * P, a * 256 + g * P + P)
                if s < 2:
                    hh = slice(HD * s, HD * s + HD)
                    for i, L in enumerate((Bt, Kt)):
                        for j, R in enumerate((At, Rt)):
                            ins = mm(b[:, (2 * i + j) * P:(2 * i + j + 1) * P], L[hh, pcs, cols], R[hh, pcs, cols], i + j == 0)
                elif s == 2:
                    for i, src in enumerate((vin, Bt, Kt)):
                        ins = pe.transpose(b[:, i * P:(i + 1) * P], src[:, pcs, cols], ident)
                elif s == 3:
                    pe.wait_ge(dt_ready, 2 * k + g + 1)
                    for i in range(2):
                        ins = pe.transpose(b[:, i * P:(i + 1) * P], Dt[g][:, i, :], ident)
                elif s == 4:
                    pe.wait_ge(st_evac[3], 2 * k + g + 1)
                    for i in range(2):
                        mm(b[:, i * P:(i + 1) * P], Dn[g][:, i, :], Dt[g][:, i, :], i == 0)
                        ins = mm(b[:, (2 + i) * P:(3 + i) * P], Dt[g][:, i, :], Dn[g][:, i, :], False)
                elif s == 5:
                    pe.wait_ge(st_evac[4], 2 * k + g + 1)
                    pe.wait_ge(x1_ready, 2 * k + g + 1)
                    for i in range(2):
                        mm(b[:, i * P:(i + 1) * P], D2[g][:, 1, i, :], TT[a][g][:, 0, i, :], i == 0)
                        ins = mm(b[:, (2 + i) * P:(3 + i) * P], D2[g][:, 0, i, :], D2[g][:, 1, i, :], False)
                elif s == 6:
                    pe.wait_ge(st_evac[5], 2 * k + g + 1)
                    for i in range(2):
                        ins = mm(b[:, i * P:(i + 1) * P], Dn[g][:, i, :], TT[a][g][:, 0, i, :], i == 0)
                elif s == 7:
                    pe.wait_ge(st_evac[6], 2 * k + g + 1)
                    for i in range(2):
                        ins = pe.transpose(b[:, i * P:(i + 1) * P], TT[a][g][:, 0, i, :], ident)
                elif s % 2 == 0:
                    pe.wait_ge(e_ready, 2 * k + g + 1)
                    pe.wait_ge(st_evac[s - 1], 2 * k + g + 1)
                    for i in range(2):
                        ins = mm(b[:, i * P:(i + 1) * P], Et[g][:, (s - 8) // 2, i, :], TT[a][g][:, 1, i, :], i == 0)
                else:
                    pe.wait_ge(st_evac[s - 1], 2 * k + g + 1)
                    for i in range(2):
                        ins = mm(b[:, i * P:(i + 1) * P], Wm[g][:, i, :], TT[a][g][:, 0, i, :], i == 0)
                        if s < 13:
                            ins = mm(b[:, (2 + i) * P:(3 + i) * P], TT[a][g][:, 0, i, :], Wm[g][:, i, :], False)
                ins.then_inc(st_full[s], 1)

            def scan(f, hp, u, first):
                c, ph = f // 3, f % 3
                g, p = c // 2, c % 2
                a, pc = u % 2, u // 2
                n = 16 * hp + 4 * u + c
                tp = slice(C * p, C * p + C)
                base = a * 256 + g * P
                cols = slice(base + C * p, base + C * p + C)
                sc, yb = bank(B_SC), bank(B_Y)
                sm, tk = Sm[a][g], tok[a][g]
                if ph == 0:
                    if c == 0:
                        pe.wait_ge(st_evac[13], 2 * (4 * hp + u) + 2)
                        if a == 0 and not (first and pc == 0):
                            pe.wait_ge(y_sb, 2 * hp + pc)
                    pe.wait_ge(s_ready, n + 1)
                    mm(sc[tp, 0:P], At[:, pc, cols], S[:], True)
                    for i in range(2):
                        hh = slice(HD * i, HD * i + HD)
                        ins = mm(sc[tp, hh], sm[:, i, 2, tp], tk[:, 0, hh], False)
                    ins.then_inc(rhs_full, 1)
                elif ph == 1:
                    mm(yb[:, cols], S[:], Rt[:, pc, cols], c == 0 and a == 0)
                    pe.wait_ge(rhs_sbr, n + 1)
                    for i in range(2):
                        ins = mm(sc[tp, P + HD * i:P + HD * i + HD], TT[a][g][:, 0, i, tp],
                                 rhs_sb[:, HD * i:HD * i + HD], i == 0)
                    ins.then_inc(sa_full, 1)
                else:
                    pe.wait_ge(sa_sbr, n + 1)
                    mm(sc[:, 2 * P:3 * P], tk[tp, 1, :], SA[g][tp, :], True)
                    mm(sc[:, 2 * P:3 * P], tk[tp, 2, :], tk[tp, 0, :], False).then_inc(ds_full, 1)
                    if p == 1:
                        for i in range(2):
                            hh = slice(HD * i, HD * i + HD)
                            mm(yb[hh, base:base + P], SA[g][:, hh], sm[:, i, 1, :], False)
                            ins = mm(yb[hh, base:base + P], tk[:, 0, hh], sm[:, i, 3, :], False)
                        ins.then_inc(y_tile, 1)

            def is0(v, below=1):
                return type(v) is int and v < below

            def prep(e, r, hp, pc):
                cols = slice(pc * HALF, pc * HALF + HALF)
                if e == 0:
                    if not is0(r):
                        pe.wait_ge(bon_e, r)
                    pe.wait_ge(l_in, 16 * (hp + 1))
                    mm(bank(B_AUX0), l2[:, 0, :], lor[:, 0, cols], True).then_inc(zw_f, 1)
                    if not is0(r):
                        pe.wait_ge(ss_e, r)
                    if not is0(r, 3):
                        pe.wait_ge(z_r, r - 2)
                    mm(bank(B_AUX1), l2[:, 1, :], lor[:, 1, cols], True).then_inc(za_f, 1)
                elif e == 1:
                    pe.wait_ge(za_e, r + 1)
                    pe.wait_ge(ksq_r, r + 1)
                    mm(bank(B_AUX1), blk, T6, True).then_inc(ss_f, 1)
                else:
                    pe.wait_ge(rk_r, r + 1)
                    mm(bank(B_AUX0), blk, T6, True).then_inc(bon_f, 1)

            def post(e, p, hp, pc, alone):
                cols = slice(pc * HALF, pc * HALF + HALF)
                if e == 0:
                    if alone == 0:
                        pe.wait_ge(zw_e, p + 3)
                    elif alone == 1:
                        pe.wait_ge(bon_e, 16)
                    else:
                        pe.wait_ge(var_e, p)
                    pe.wait_ge(y_sb, p + 1)
                    mm(bank(B_AUX0), blk, ysb[:], True).then_inc(mean_f, 1)
                elif e == 1:
                    pe.wait_ge(ysq_r, p + 1)
                    mm(bank(B_AUX0), blk, psq, True).then_inc(var_f, 1)
                else:
                    pe.wait_ge(ss_e, p + 3 if alone == 0 else 16)
                    if not is0(p):
                        pe.wait_ge(z_r, p)
                    pe.wait_ge(lg_in, 16 * (hp + 1))
                    mm(bank(B_AUX1), l2g[:], lor[:, 2, cols], True).then_inc(g_f, 1)

            def rounds(inv, sc, busy):
                nonlocal pcs
                if inv:
                    k, u, nopr, need = inv
                    pcs = u // 2
                    pe.wait_ge(prep_done, need)
                    pe.wait_ge(bon_e, need)
                for s in range(14):
                    if inv:
                        stage(s, 0, k, u % 2, nopr)
                        stage(s, 1, k, u % 2, nopr)
                    if sc and 1 <= s <= 12:
                        scan(s - 1, *sc)
                    if busy:
                        pp, qq, alone = busy
                        if pp and s == 0:
                            prep(0, *pp)
                        if qq and s == 2:
                            post(0, *qq, alone)
                        if pp and s == 3:
                            prep(1, *pp)
                        if qq and s == 6:
                            post(1, *qq, alone)
                        if qq and s == 8:
                            post(2, *qq, alone)
                        if pp and s == 10:
                            if qq:
                                pe.wait_ge(var_e, pp[0] - 1)
                            prep(2, *pp)

            pcs = 0

            def body(hp, first, last):
                rounds((4 * hp + 1, 1, False, 2 * hp + 1), (hp, 0, first),
                       ((2 * hp + 1, hp, 1), None if first else (2 * hp - 1, hp - 1, 1), 0))
                rounds((4 * hp + 2, 2, False, 2 * hp + 2), (hp, 1, first), None)
                rounds((4 * hp + 3, 3, False, 2 * hp + 2), (hp, 2, first),
                       (None if last else (2 * hp + 2, hp + 1, 0), (2 * hp, hp, 0), 1 if last else 0))
                rounds(None if last else (4 * hp + 4, 0, False, 2 * hp + 3), (hp, 3, first), None)

            pe.wait_ge(lo_ready, 3)
            pe.wait_ge(a_in, 16)
            for e in range(3):
                prep(e, 0, 0, 0)
            rounds((0, 0, True, 1), None, None)
            body(0, True, False)
            with pe.Fori(1, NHP - 1) as hp:
                body(hp, False, False)
            body(NHP - 1, False, True)
            for e in range(3):
                post(e, 15, NHP - 1, 1, 2)

            def project(n0, m0):
                for t in range(8):
                    dense(n0 + t, 0, t % 4, m0 + t - 3 if t >= 4 else None, None)

            pe.wait_ge(z_ready, 16)
            project(N_WO, 0)
            stats(1)
            stats(2)

            def ffn(L, n0, xb):
                s0 = n0 % 2

                def gate_up(n, ws, t):
                    pe.wait_ge(w_split, n + 1)
                    for kt in range(KT):
                        pe.wait_ge(x_ready, xb + kt + 1)
                        for j, (a, b) in enumerate(((wh, xh), (wh, xl), (wl, xh))):
                            for lo, hi in halves():
                                ins = pe.matmul(ps[:, t, lo:hi], a[:, ws, kt * P:(kt + 1) * P], b[:, kt, lo:hi],
                                                start=(kt == 0 and j == 0), stop=(kt == KT - 1 and j == 2))
                    ins.then_inc(w_used, 1)

                def down(G, n, ws, cc, buf, gated):
                    pe.wait_ge(w_split, n + 1)
                    for m in range(4):
                        if cc == 0 and gated:
                            pe.wait_ge(sg_ready if m % 2 == 0 else up_mul, 2 * (G + 1) + m // 2 + 1)
                        else:
                            pe.wait_ge(dn_evac, 8 * G + 4 * cc + m - 3)
                        for kk in range(2):
                            pe.wait_ge(hid_ready, 2 * G + kk + 1)
                            for j, (a, b) in enumerate(((wh, hidh), (wh, hidl), (wl, hidh))):
                                for lo, hi in halves():
                                    ins = pe.matmul(ps[:, m, lo:hi], a[:, ws, kk * HALF + m * P:kk * HALF + (m + 1) * P],
                                                    b[:, buf, kk, lo:hi], start=(kk == 0 and j == 0),
                                                    stop=(kk == 1 and j == 2))
                        ins.then_inc(dn_full, 1)

                G = FG * L
                for t in range(4):
                    gate_up(n0 + t, (s0 + t) % 2, t)
                for t in range(4):
                    pe.wait_ge(sg_ready if t % 2 == 0 else up_mul, 2 * G + t // 2 + 1)
                    gate_up(n0 + 4 + t, (s0 + t) % 2, t)
                down(G, n0 + 8, s0, 0, 0, True)
                down(G, n0 + 9, 1 - s0, 1, 0, True)

                def group(g, n, buf):
                    for t in range(4):
                        pe.wait_ge(dn_evac, 8 * (g - 2) + 4 + t + 1)
                        gate_up(n + t, (s0 + t) % 2, t)
                    down(g - 1, n + 4, s0, 0, 1 - buf, True)
                    down(g - 1, n + 5, 1 - s0, 1, 1 - buf, True)

                with pe.Fori(0, (FG - 3) // 2) as i:
                    for v in range(2):
                        group(2 * i + G + 2 + v, 12 * i + n0 + 10 + 6 * v, v)
                group(G + FG - 1, n0 + 4 + 6 * (FG - 2), 0)
                down(G + FG - 1, n0 + 6 * FG - 2, s0, 0, 0, False)
                down(G + FG - 1, n0 + 6 * FG - 1, 1 - s0, 1, 0, False)

            ffn(0, N_F0, 6 * KT)
            stats(3)
            stats(4)

            def qkv(l):
                if l >= 2:
                    pe.wait_ge(mm_evac, 8 + l - 1)
                n = N_QKV + l
                dense(n, 0, l % 2, None, 7 * KT)

            def turn(l):
                sl = 2 + l % 2
                pe.wait_ge(mm_evac, 8 + l + 1)
                if l >= 2:
                    pe.wait_ge(rot_r, l - 1)
                if l < 10:
                    for lo, hi in halves():
                        ins = mm(ps[:, sl, lo:hi], perm, tmp[:, l % 2, lo:hi], True)
                else:
                    for n in range(NB):
                        ins = pe.transpose(ps[:, sl, n * P:(n + 1) * P], tmp[:, l % 2, n * P:(n + 1) * P], ident)
                ins.then_inc(rot_f, 1)

            pe.wait_ge(a_in, 32)
            for l in range(12):
                qkv(l)
                if l >= 1:
                    turn(l - 1)
            turn(11)
            pe.wait_ge(rot_r, 12)
            pe.wait_ge(kd_r, 3)
            pe.wait_ge(pad_r, 1)

            def scores(it):
                n, kv = it // NKV, it % NKV
                if it >= 2:
                    pe.wait_ge(sm_m, it - 1)
                for i in range(4):
                    hh = slice(HD * (i % 2), HD * (i % 2) + HD)
                    o = (i % 2) * HALF + (i // 2) * 2 * P
                    ins = mm(ps[:, it % 2, o:o + 2 * P], q[hh, 2 * kv + i // 2, n * P:(n + 1) * P],
                             kd[hh, kv, n * P:(n + 2) * P], i < 2)
                ins.then_inc(s_f, 1)

            def probs(it):
                pe.wait_ge(p_n, it + 1)
                if it >= 1:
                    pe.wait_ge(pt_r, it)
                for kk in range(2):
                    for i in range(4):
                        ins = pe.transpose(bank(4 + kk)[:, i * P:(i + 1) * P],
                                           sc[:, it % 2, i * 2 * P + kk * P:i * 2 * P + (kk + 1) * P], ident)
                ins.then_inc(pt_f, 1)

            def values(it):
                n, kv = it // NKV, it % NKV
                pe.wait_ge(pt_r, it + 1)
                if it >= 2:
                    pe.wait_ge(oz_r, it - 1)
                o = bank(6 + it % 2)
                for odd in range(2):
                    for kk in range(2):
                        ins = mm(o[HD * odd:HD * odd + HD, 0:2 * P], vt[:, n + kk, kv, :],
                                 pT[:, kk, odd * 2 * P:(odd + 1) * 2 * P], kk == 0)
                ins.then_inc(o_f, 1)

            IT = NB * NKV
            scores(0)
            for it in range(IT):
                if it + 1 < IT:
                    scores(it + 1)
                if it >= 1:
                    values(it - 1)
                probs(it)
            values(IT - 1)
            pe.wait_ge(oz_r, IT)
            project(N_AO, 20)
            stats(5)
            stats(6)
            ffn(1, N_F1, 8 * KT)
            stats(7)

        @block.scalar
        def _(act):
            own = Own(act, act_own)

            def w_round(n, r, after):
                act.wait_ge(w_dma[n % 2], 8 * r + 16 * (n // 2 + 1))
                if after:
                    act.wait_ge(*after)
                act.activation(wh[:, n % 2, :], wst[:, n % 2, :], ACT.Copy).then_inc(w_hi, 1)

            def squares(nn, src, ready):
                for kt in range(KT):
                    if ready:
                        act.wait_ge(ready[0], ready[1] + (kt + 1 if ready[2] else 0))
                    if KT * nn + kt >= 2:
                        act.wait_ge(sq_used, KT * nn + kt - 1)
                    act.activation(sqb[:, kt % 2, :], src(kt), ACT.Square).then_inc(sq_ready, 1)

            def root(nn, after):
                act.preload_act_table_set(LN_EXP)
                act.wait_ge(sq_used, KT * nn + KT)
                if after:
                    act.wait_ge(*after)
                own.link(act.activation(rstd[:], ps[:, 3, :], ACT.Ln, bias=pr[:, EPS_RMS:EPS_RMS + 1], scale=1.0 / D))
                act.activation(rstd[:], rstd[:], ACT.Exp, scale=-0.5).then_inc(rs_ready, 1)

            def x_round(b):
                for kt in range(KT):
                    act.wait_ge(xn_ready, b + kt + 1)
                    act.activation(xh[:, kt, :], tmp[:, kt % 2, :], ACT.Copy).then_inc(xhi_ready, 1)

            act.wait_ge(c_in, 32)
            w_round(0, 0, None)
            squares(0, lambda kt: h[:, kt, 1:T + 1], (x_in, 16, False))
            root(0, None)

            def spill(n, r):
                w_round(n + 1, 4 * r, (w_used, n + 4 * r) if n >= 1 else None)
                act.wait_ge(w_used, n + 4 * r + 1)
                if n >= 2:
                    act.wait_ge(o_dma[n % 2], 32 * r + 16 * (n // 2))
                act.activation(ost[:, n % 2, :], ps[:, n % 4, :], ACT.Copy).then_inc(o_full[n % 2], 1)

            x_round(0)
            for t in range(8):
                spill(t, 0)
            for j in (1, 2):
                x_round(KT * j)
                with act.Fori(0, 2) as i:
                    for t in range(4):
                        spill(8 * j + t, i)
            for j, f in enumerate((ACT.Tanh, ACT.Copy, ACT.Sigmoid)):
                n = N_LORA + j
                x_round(KT * (3 + j))
                w_round(n + 1, 0, (w_used, n))
                act.wait_ge(w_used, n + 1)
                act.activation(lor[:, j, :], ps[:, n % 4, :], f).then_inc(lo_ready, 1)

            def evac(s, g, k, a):
                if s not in (2, 3, 4, 7, 8, 10, 12):
                    return
                b = bank(inv_bank(s, g))
                act.wait_ge(st_full[s], 2 * k + g + 1)
                if s == 2:
                    if not (type(k) is int and k < 2):
                        act.wait_ge(y_tile, 2 * k - 3 + g)
                    dst, n = tok[a][g][:].rearrange("p a b -> p (a b)"), 3 * P
                elif s == 3:
                    dst, n = Dn[g][:].rearrange("p a b -> p (a b)"), 2 * P
                elif s == 4:
                    dst, n = D2[g][:].rearrange("p a b c -> p (a b c)"), 4 * P
                elif s == 7:
                    dst, n = TT[a][g][:, 1].rearrange("p a b -> p (a b)"), 2 * P
                else:
                    dst, n = Wm[g][:].rearrange("p a b -> p (a b)"), 2 * P
                act.activation(dst, b[:, 0:n], ACT.Copy).then_inc(st_evac[s], 1)

            def scan(f, hp, u, first):
                c, ph = f // 3, f % 3
                g, p = c // 2, c % 2
                n, k = 16 * hp + 4 * u + c, 4 * hp + u
                tp = slice(C * p, C * p + C)
                b = bank(B_SC)
                if ph == 0:
                    act.wait_ge(rhs_full, n + 1)
                    act.activation(rhs_sb[tp, :], b[tp, 0:P], ACT.Copy).then_inc(rhs_sbr, 1)
                elif ph == 1:
                    act.wait_ge(sa_full, n + 1)
                    if p == 0 and not (type(k) is int and k == 0):
                        act.wait_ge(y_tile, 2 * k + g - 1)
                    act.activation(SA[g][tp, :], b[tp, P:2 * P], ACT.Copy).then_inc(sa_sbr, 1)

            def prep(e, r, hp, pc):
                if e == 0:
                    if pc == 0:
                        act.wait_ge(pp_r, hp + 1)
                    if not (type(r) is int and r == 0):
                        act.wait_ge(prep_done, r)
                        act.wait_ge(bon_f, r)
                    act.wait_ge(zw_f, r + 1)
                    act.activation(T0, bank(B_AUX0), ACT.Sigmoid, bias=pcp[:, 0:1]).then_inc(zw_e, 1)
                    act.wait_ge(za_f, r + 1)
                    act.activation(T5, bank(B_AUX1), ACT.Sigmoid, bias=pcp[:, 1:2]).then_inc(za_e, 1)
                    act.preload_act_table_set(LN_EXP)
                    act.wait_ge(k_in, 16 * (r + 1))
                    act.activation(T6, kin[:], ACT.Square, scale=pcp[:, 2:3]).then_inc(ksq_r, 1)
                elif e == 1:
                    act.wait_ge(s_r, r + 1)
                    act.activation(T2, T1, ACT.Exp, scale=-DECAY)
                    act.activation(T3, T1, ACT.Exp, scale=DECAY)
                    act.wait_ge(sm_r, r + 1)
                    act.activation(T4, T0, ACT.Exp, scale=-DECAY).then_inc(P_r, 1)
                else:
                    act.wait_ge(ss_e, r + 1)
                    own.link(act.activation(T6, T6, ACT.Ln, scale=float(2 ** LN_SHIFT)))
                    act.activation(T6, T6, ACT.Exp, scale=-0.5, bias=pr[:, KSH:KSH + 1]).then_inc(rinv_r, 1)

            def post(e, p, hp, pc):
                if e == 0:
                    act.wait_ge(y_tile, 4 * (p + 1))
                    act.activation(ysb[:], bank(B_Y), ACT.Copy).then_inc(y_sb, 1)
                elif e == 1:
                    act.wait_ge(yc_r, p + 1)
                    act.activation(psq, ysb[:], ACT.Square).then_inc(ysq_r, 1)
                elif e == 2:
                    act.wait_ge(var_f, p + 1)
                    own.link(act.activation(psq, bank(B_AUX0), ACT.Ln, bias=pr[:, EPS_GN:EPS_GN + 1], scale=1.0 / HD))
                    act.activation(psq, psq, ACT.Exp, scale=-0.5).then_inc(var_e, 1)
                else:
                    act.wait_ge(z_r, p + 1)
                    act.activation(xh[:, hp, pc * HALF:(pc + 1) * HALF], zt, ACT.Copy).then_inc(zhi_r, 1)

            def rounds(inv, sc, busy):
                for s in range(14):
                    if busy:
                        pp, qq = busy
                        if qq and s == 0:
                            post(0, *qq)
                    if inv:
                        evac(s, 0, inv[0], inv[1] % 2)
                        evac(s, 1, inv[0], inv[1] % 2)
                    if sc and 1 <= s <= 12:
                        scan(s - 1, *sc)
                    if busy:
                        if pp and s == 0:
                            prep(0, *pp)
                        if pp and s == 2:
                            prep(1, *pp)
                        if qq and s == 4:
                            post(1, *qq)
                        if pp and s == 5:
                            prep(2, *pp)
                        if qq and s == 7:
                            post(2, *qq)
                        if qq and s == 10:
                            post(3, *qq)

            def body(hp, first, last):
                rounds((4 * hp + 1, 1), (hp, 0, first), ((2 * hp + 1, hp, 1), None if first else (2 * hp - 1, hp - 1, 1)))
                rounds((4 * hp + 2, 2), (hp, 1, first), None)
                rounds((4 * hp + 3, 3), (hp, 2, first), (None if last else (2 * hp + 2, hp + 1, 0), (2 * hp, hp, 0)))
                rounds(None if last else (4 * hp + 4, 0), (hp, 3, first), None)

            for e in range(3):
                prep(e, 0, 0, 0)
            rounds((0, 0), None, None)
            body(0, True, False)
            n, per = own.n, 4
            with act.Fori(1, NHP - 1) as hp:
                own.r = per * hp - per
                body(hp, False, False)
            assert own.n == n + per
            own.n, own.r = n + per * (NHP - 2), 0
            body(NHP - 1, False, True)
            for e in range(4):
                post(e, 15, NHP - 1, 1)

            def project(n0, m0, used, bias):
                for t in range(8):
                    w_round(n0 + t + 1, 0, (w_used, used + t))
                    act.wait_ge(w_used, used + t + 1)
                    if bias is None:
                        ins = act.activation(y[:, t, :], ps[:, t % 4, :], ACT.Copy)
                    else:
                        ins = act.activation(y[:, t, :], ps[:, t % 4, :], ACT.Identity, bias=pr[:, bias + t:bias + t + 1])
                    ins.then_inc(mm_evac, 1)

            project(N_WO, 0, N_WO, None)
            squares(1, lambda kt: y[:, kt, :], (mm_evac, 0, True))
            root(1, None)
            squares(2, lambda kt: x[:, kt, :], (res_done, 0, True))
            root(2, (res_done, KT))
            x_round(6 * KT)

            def ffn(L, n0, used):
                s0 = n0 % 2

                def silu(g, i, count):
                    act.wait_ge(w_used, count)
                    if not (type(g) is int and g == 0):
                        act.wait_ge(up_mul, 2 * g + i - 1)
                    act.activation(sqb[:, i, :], ps[:, 2 * i, :], ACT.Silu).then_inc(sg_ready, 1)

                def hidden(g, i, buf):
                    act.wait_ge(up_mul, 2 * g + i + 1)
                    act.activation(hidh[:, buf, i, :], tmp[:, i, :], ACT.Copy).then_inc(hid_hi, 1)

                G = FG * L
                w_round(n0 + 1, 0, (w_used, used))
                silu(G, 0, used + 1)
                w_round(n0 + 2, 0, (w_used, used + 1))
                w_round(n0 + 3, 0, (w_used, used + 2))
                hidden(G, 0, 0)
                silu(G, 1, used + 3)
                w_round(n0 + 4, 0, (w_used, used + 3))
                hidden(G, 1, 0)

                def group(g, n, r, u, prev, buf):
                    w_round(n + 1, r, prev)
                    silu(g, 0, u + 1)
                    w_round(n + 2, r, (w_used, u + 1))
                    w_round(n + 3, r, (w_used, u + 2))
                    hidden(g, 0, buf)
                    silu(g, 1, u + 3)
                    w_round(n + 4, r, (w_used, u + 3))
                    w_round(n + 5, r, (w_used, u + 4))
                    hidden(g, 1, buf)
                    w_round(n + 6, r, (dn_full, 8 * (g - 1) + 4))

                group(G + 1, n0 + 4, 0, used + 4, (w_used, used + 4), 1)
                with act.Fori(0, (FG - 3) // 2) as i:
                    for v in range(2):
                        g = 2 * i + G + 2 + v
                        group(g, n0 + 10 + 6 * v, 12 * i, 8 * i + used + 8 + 4 * v, (dn_full, 8 * (g - 2) + 8), v)
                g = G + FG - 1
                group(g, n0 + 4 + 6 * (FG - 2), 0, used + 4 * (FG - 1), (dn_full, 8 * (g - 2) + 8), 0)
                w_round(n0 + 6 * FG - 1, 0, (dn_full, 8 * (g - 1) + 8))
                if L == 0:
                    w_round(n0 + 6 * FG, 0, (dn_full, 8 * g + 4))

            U0 = N_F0 + 4 * FG
            ffn(0, N_F0, N_F0)
            squares(3, lambda kt: y[:, kt, :], (dn_evac, 8 * FG, False))
            root(3, (xn_ready, 7 * KT))
            squares(4, lambda kt: x[:, kt, :], (res_done, KT, True))
            root(4, (res_done, 2 * KT))
            x_round(7 * KT)

            def heads_in(l):
                w_round(N_QKV + l + 1, 0, (w_used, U0 + l) if l >= 1 else (dn_full, 8 * FG))
                act.wait_ge(w_used, U0 + l + 1)
                if l >= 2:
                    act.wait_ge(rot_r, l - 1)
                act.activation(tmp[:, l % 2, :], ps[:, l % 2, :], ACT.Identity,
                               bias=pr[:, BQKV + l:BQKV + l + 1]).then_inc(mm_evac, 1)

            def v_out(l):
                act.wait_ge(rot_f, l + 1)
                kv = 2 * (l - 10)
                act.activation(vt[:, 1:NB + 1, kv:kv + 2, :].rearrange("p n a b -> p n (a b)"),
                               ps[:, 2 + l % 2, :].rearrange("p (n c) -> p n c", c=P), ACT.Copy).then_inc(rot_r, 1)

            for l in range(12):
                heads_in(l)
                if l == 11:
                    v_out(10)
            v_out(11)
            act.wait_ge(kd_r, 2)
            for i in range(2):
                act.activation(kd[HD:P, 2 * i, P:], kd[0:HD, 2 * i, P:], ACT.Copy)
                ins = act.activation(kd[0:HD, 2 * i + 1, P:], kd[HD:P, 2 * i + 1, P:], ACT.Copy)
            ins.then_inc(kd_r, 1)

            def soft(it):
                act.wait_ge(nm_r, it + 1)
                b = it % 2
                act.activation(st[:, b, 3, :], st[:, b, 3, :], ACT.Exp)
                for i in range(4):
                    ins = act.activation(sc[:, b, i * 2 * P:(i + 1) * 2 * P], sc[:, b, i * 2 * P:(i + 1) * 2 * P], ACT.Exp,
                                         bias=st[:, b, 1, i:i + 1], accum_out=st[:, b, 2, i:i + 1])
                ins.then_inc(p_r, 1)

            def turned(it):
                act.wait_ge(pt_f, it + 1)
                if it >= 1:
                    act.wait_ge(o_f, it)
                act.activation(pT[:].rearrange("p a b -> p (a b)"), ps[:, 2, :], ACT.Copy).then_inc(pt_r, 1)

            def o_hi(it):
                n, kv = it // NKV, it % NKV
                act.wait_ge(o_f, it + 1)
                act.activation(xh[:, 2 * kv:2 * kv + 2, n * P:(n + 1) * P],
                               bank(6 + it % 2)[:, 0:2 * P].rearrange("p (a b) -> p a b", b=P), ACT.Copy).then_inc(o_r, 1)

            IT = NB * NKV
            act.preload_act_table_set(LN_EXP)
            for it in range(IT):
                soft(it)
                if it >= 1:
                    turned(it - 1)
                if it >= 2:
                    o_hi(it - 2)
            turned(IT - 1)
            o_hi(IT - 2)
            o_hi(IT - 1)
            act.wait_ge(oz_r, IT)
            project(N_AO, 20, U0 + 12, BO)
            squares(5, lambda kt: y[:, kt, :], (mm_evac, 20, True))
            root(5, None)
            squares(6, lambda kt: x[:, kt, :], (res_done, 2 * KT, True))
            root(6, (res_done, 3 * KT))
            x_round(8 * KT)
            ffn(1, N_F1, U0 + 20)
            squares(7, lambda kt: y[:, kt, :], (dn_evac, 16 * FG, False))
            root(7, (xn_ready, 9 * KT))

        @block.vector
        def _(dve):
            own = Own(dve, dve_own)
            stt = dve.scalar_tensor_tensor

            def w_lo(n, ws):
                dve.wait_ge(w_hi, n + 1)
                dve.tensor_tensor(wl[:, ws, :], wst[:, ws, :], wh[:, ws, :].bitcast(F32), ALU.subtract).then_inc(w_split, 1)

            def x_split(b, make, used):
                def lo(kt):
                    dve.wait_ge(xhi_ready, b + kt + 1)
                    dve.tensor_tensor(xl[:, kt, :], tmp[:, kt % 2, :], xh[:, kt, :].bitcast(F32), ALU.subtract).then_inc(x_ready, 1)
                if used:
                    dve.wait_ge(*used)
                for kt in range(KT):
                    if b + kt >= 2:
                        dve.wait_ge(x_ready, b + kt - 1)
                    make(kt).then_inc(xn_ready, 1)
                    if kt >= 1:
                        lo(kt - 1)
                lo(KT - 1)

            def g_col(c, kt):
                return pr[:, c + kt:c + kt + 1]

            def normed(gc):
                def make(kt):
                    return stt(out=tmp[:, kt % 2, :], in0=x[:, kt, :], scalar=g_col(gc, kt), in1=rstd[:], op0=ALU.mult, op1=ALU.mult)
                return make

            def residual(i, gc, nn, ready):
                dve.wait_ge(rs_ready, nn + 1)
                if ready:
                    dve.wait_ge(*ready)
                for kt in range(KT):
                    own.link(stt(out=y[:, kt, :], in0=y[:, kt, :], scalar=g_col(gc, kt), in1=rstd[:], op0=ALU.mult, op1=ALU.mult))
                    dve.tensor_tensor(x[:, kt, :], x[:, kt, :], y[:, kt, :], ALU.add).then_inc(res_done, 1)

            w_lo(0, 0)
            dve.wait_ge(rs_ready, 1)
            dve.wait_ge(pool_own, 1)
            for kt in range(KT):
                stt(out=h[:, kt, 1:T + 1], in0=h[:, kt, 1:T + 1], scalar=g_col(G0, kt), in1=rstd[:],
                    op0=ALU.mult, op1=ALU.mult).then_inc(h_ready, 1)

            def mixed(j):
                def make(kt):
                    dve.wait_ge(xx_ready, kt + 1)
                    return stt(out=tmp[:, kt % 2, :], in0=xx[:, kt, :], scalar=g_col(MIX + KT * j, kt), in1=h[:, kt, 1:T + 1],
                               op0=ALU.mult, op1=ALU.add)
                return make

            x_split(0, mixed(0), None)
            for t in range(8):
                w_lo(t + 1, (t + 1) % 2)
            for j in (1, 2):
                x_split(KT * j, mixed(j), (w_used, 8 * j))
                with dve.Fori(0, 2) as i:
                    for t in range(4):
                        w_lo(4 * i + 8 * j + t + 1, (t + 1) % 2)
            for j in range(3):
                x_split(KT * (3 + j), mixed(3 + j), (w_used, N_LORA + j))
                w_lo(N_LORA + j + 1, (N_LORA + j + 1) % 2)

            def evac(s, g, k, a):
                b = bank(inv_bank(s, g))
                tt0 = TT[a][g][:, 0].rearrange("p a b -> p (a b)")
                if s < 2:
                    dve.wait_ge(st_full[s], 2 * k + g + 1)
                    if s == 0 and not (type(k) is int and k < 2):
                        dve.wait_ge(y_tile, 2 * k - 3 + g)
                    dve.tensor_tensor(Sm[a][g][:, s].rearrange("p (i j) c -> p i (j c)", i=2),
                                      b.rearrange("p (i c) -> p i c", i=2),
                                      m_si.unsqueeze(1).to_broadcast([P, 2, 2 * P]), ALU.mult).then_inc(st_evac[s], 1)
                    if s == 1:
                        dve.wait_ge(st_evac[0], 2 * k + g + 1)
                        dve.wait_ge(st_evac[1], 2 * k + g + 1)
                        dve.tensor_tensor(Dt[g][:], Sm[a][g][:, :, 0, :], mu8.unsqueeze(1).to_broadcast([P, 2, P]),
                                          ALU.mult).then_inc(dt_ready, 1)
                        dve.wait_ge(dt_ready, 2 * k + g + 1)
                        dve.tensor_tensor(TT[a][g][:, 0], Dt[g][:], ident.unsqueeze(1).to_broadcast([P, 2, P]),
                                          ALU.add).then_inc(x1_ready, 1)
                elif s == 5:
                    dve.wait_ge(st_full[5], 2 * k + g + 1)
                    dve.tensor_tensor(tt0, tt0, b[:, 0:2 * P], ALU.add)
                    dve.tensor_copy(Dn[g][:].rearrange("p a b -> p (a b)"), b[:, 2 * P:4 * P]).then_inc(st_evac[5], 1)
                elif s in (6, 13):
                    dve.wait_ge(st_full[s], 2 * k + g + 1)
                    dve.tensor_tensor(tt0, tt0, b[:, 0:2 * P], ALU.add).then_inc(st_evac[s], 1)
                elif s in (9, 11):
                    dve.wait_ge(st_full[s], 2 * k + g + 1)
                    tt = TT[a][g][:].rearrange("p a b c -> p (a b c)")
                    dve.tensor_tensor(tt, tt, b, ALU.add).then_inc(st_evac[s], 1)

            def scan(f, hp, u, first):
                c, ph = f // 3, f % 3
                a, pc = u % 2, u // 2
                n = 16 * hp + 4 * u + c
                pe_col = pend[:, pc, 4 * a + c:4 * a + c + 1]
                if ph == 0:
                    if u == 0 and c == 0:
                        if not first:
                            dve.wait_ge(ds_full, 16 * hp)
                            dve.memset(S[:], 0.0).then_inc(s_ready, 1)
                        else:
                            dve.memset(rhs_sb[:], 0.0)
                            dve.memset(S[:], 0.0).then_inc(s_ready, 1)
                    dve.wait_ge(s_ready, n + 1)
                    dve.tensor_scalar(SP[:], S[:], pe_col, None, ALU.mult).then_inc(sp_ready, 1)
                elif ph == 2 and not (u == 3 and c == 3):
                    dve.wait_ge(ds_full, n + 1)
                    dve.wait_ge(sp_ready, n + 1)
                    b = bank(B_SC)
                    for i in range(2):
                        hh = slice(HD * i, HD * i + HD)
                        ins = stt(out=S[hh, hh], in0=b[hh, 2 * P + HD * i:2 * P + HD * i + HD], scalar=pe_col[hh, :], in1=SP[hh, hh],
                                  op0=ALU.mult, op1=ALU.add)
                    ins.then_inc(s_ready, 1)

            def prep(e, r, hp, pc, after):
                if e == 0:
                    if pc == 0:
                        src = pr[:, W0:W0 + 40].rearrange("p (v h) -> p v h", h=NHP)[:, :, hp:hp + 1] if type(hp) is int else \
                            pr[:, W0:W0 + 40].rearrange("p (v h) -> p v h", h=NHP)[:, :, bass.ds(hp, 1)]
                        own.link(dve.tensor_copy(pcp[:, 0:5].unsqueeze(2), src))
                        dve.tensor_scalar(pcp[:, 5:6], pcp[:, 3:4], -1.0, 1.0, ALU.mult, ALU.add).then_inc(pp_r, 1)
                elif e == 1:
                    dve.wait_ge(zw_e, r + 1)
                    dve.tensor_tensor_scan(T1, rst, T0, 0.0, ALU.mult, ALU.add).then_inc(s_r, 1)
                    dve.wait_ge(s_r, r + 1)
                    dve.tensor_tensor(T0, T1, T0, ALU.subtract).then_inc(sm_r, 1)
                elif e == 2:
                    dve.wait_ge(ss_f, r + 1)
                    dve.tensor_scalar(T6, bank(B_AUX1), 1e-24, None, ALU.max).then_inc(ss_e, 1)
                elif e == 3:
                    dve.wait_ge(P_r, r + 1)
                    dve.wait_ge(rinv_r, r + 1)
                    dve.wait_ge(r_in, 16 * (r + 1))
                    dve.wait_ge(za_e, r + 1)
                    if after is not None:
                        dve.wait_ge(y_tile, after)
                    own.link(stt(out=T7, in0=kin[:], scalar=pcp[:, 2:3], in1=T6, op0=ALU.mult, op1=ALU.mult))
                    stt(out=At[:, pc, :], in0=T7, scalar=-1.0, in1=T4, op0=ALU.mult, op1=ALU.mult)
                    own.link(dve.tensor_tensor(T7, T7, T5, ALU.mult))
                    dve.tensor_tensor(Bt[:, pc, :], T7, T3, ALU.mult)
                    own.link(dve.tensor_scalar(T5, T5, pcp[:, 3:4], pcp[:, 5:6], ALU.mult, ALU.add))
                    own.link(dve.tensor_tensor(T5, T5, kin[:], ALU.mult))
                    dve.tensor_tensor(Kt[:, pc, :], T5, T3, ALU.mult)
                    dve.tensor_tensor(Rt[:, pc, :], rin[:], T2, ALU.mult)
                    stt(out=T6, in0=rin[:], scalar=pcp[:, 4:5], in1=T5, op0=ALU.mult, op1=ALU.mult).then_inc(rk_r, 1)
                    dve.tensor_copy(pend[:, pc, :], T2.rearrange("p (n c) -> p n c", c=C)[:, :, C - 1]).then_inc(prep_done, 1)
                else:
                    dve.wait_ge(bon_f, r + 1)
                    dve.wait_ge(v_in[pc], 16 * (hp + 1))
                    dve.tensor_tensor(bon[:, pc, :], bank(B_AUX0), vin[:, pc, :], ALU.mult).then_inc(bon_e, 1)

            def post(e, p, hp, pc):
                if e == 0:
                    if pc == 0:
                        src = pr[:, LNW:LNW + 16].rearrange("p (v h) -> p v h", h=NHP)
                        src = src[:, :, hp:hp + 1] if type(hp) is int else src[:, :, bass.ds(hp, 1)]
                        dve.tensor_copy(pcq[:].unsqueeze(2), src).then_inc(pq_r, 1)
                    dve.wait_ge(mean_f, p + 1)
                    stt(out=ysb[:], in0=bank(B_AUX0), scalar=-1.0 / HD, in1=ysb[:], op0=ALU.mult, op1=ALU.add).then_inc(yc_r, 1)
                elif e == 1:
                    dve.wait_ge(var_e, p + 1)
                    dve.wait_ge(g_f, p + 1)
                    dve.wait_ge(pq_r, hp + 1)
                    own.link(stt(out=zt, in0=ysb[:], scalar=pcq[:, 0:1], in1=psq, op0=ALU.mult, op1=ALU.mult))
                    own.link(stt(out=zt, in0=zt, scalar=pcq[:, 1:2], in1=bon[:, pc, :], op0=ALU.add, op1=ALU.add))
                    dve.tensor_tensor(zt, zt, bank(B_AUX1), ALU.mult).then_inc(z_r, 1)
                else:
                    dve.wait_ge(zhi_r, p + 1)
                    cols = slice(pc * HALF, pc * HALF + HALF)
                    dve.tensor_tensor(xl[:, hp, cols], zt, xh[:, hp, cols].bitcast(F32), ALU.subtract).then_inc(z_ready, 1)

            def rounds(inv, sc, busy):
                for s in range(14):
                    if inv:
                        evac(s, 0, inv[0], inv[1] % 2)
                        evac(s, 1, inv[0], inv[1] % 2)
                    if sc and 1 <= s <= 12:
                        scan(s - 1, *sc)
                    if busy:
                        pp, qq = busy
                        if pp and s == 0:
                            prep(0, *pp)
                        if pp and s == 1:
                            prep(1, *pp)
                        if qq and s == 2:
                            post(0, *qq)
                        if pp and s == 4:
                            prep(2, *pp)
                        if pp and s == 6:
                            prep(3, *pp)
                        if qq and s == 9:
                            post(1, *qq)
                        if pp and s == 11:
                            prep(4, *pp)
                        if qq and s == 12:
                            post(2, *qq)

            own.n = own.r = 0
            dve.wait_ge(a_in, 16)
            dve.wait_ge(lo_ready, 3)
            for e in range(5):
                prep(e, 0, 0, 0, None)
            rounds((0, 0), None, None)

            def body(hp, first, last):
                rounds((4 * hp + 1, 1), (hp, 0, first),
                       ((2 * hp + 1, hp, 1, None if first else 8 * hp), None if first else (2 * hp - 1, hp - 1, 1)))
                rounds((4 * hp + 2, 2), (hp, 1, first), None)
                rounds((4 * hp + 3, 3), (hp, 2, first),
                       (None if last else (2 * hp + 2, hp + 1, 0, 8 * hp + 4), (2 * hp, hp, 0)))
                rounds(None if last else (4 * hp + 4, 0), (hp, 3, first), None)

            body(0, True, False)
            n = own.n
            per = 13
            with dve.Fori(1, NHP - 1) as hp:
                own.r = per * hp - per
                body(hp, False, False)
            assert own.n == n + per, own.n - n
            own.n, own.r = n + per * (NHP - 2), 0
            body(NHP - 1, False, True)
            for e in range(3):
                post(e, 15, NHP - 1, 1)

            for t in range(8):
                w_lo(N_WO + t + 1, (N_WO + t + 1) % 2)
            residual(0, G0 + KT, 1, (x_in, 32))
            dve.wait_ge(rs_ready, 3)
            x_split(6 * KT, normed(G0 + 2 * KT), None)

            def ffn(L, n0):
                s0 = n0 % 2
                G = FG * L

                def hidden(g, i):
                    dve.wait_ge(sg_ready, 2 * g + i + 1)
                    dve.wait_ge(w_used, used(g, i))
                    dve.tensor_tensor(tmp[:, i, :], sqb[:, i, :], ps[:, 2 * i + 1, :], ALU.mult).then_inc(up_mul, 1)

                def hidden_lo(g, i, buf):
                    dve.wait_ge(hid_hi, 2 * g + i + 1)
                    dve.tensor_tensor(hidl[:, buf, i, :], tmp[:, i, :], hidh[:, buf, i, :].bitcast(F32),
                                      ALU.subtract).then_inc(hid_ready, 1)

                def used(g, i):
                    return (N_F0 if L == 0 else N_F0 + 4 * FG + 20) + 4 * (g - G) + 2 * i + 2

                def add(g, m):
                    dve.wait_ge(dn_full, 8 * g + m + 1)
                    dve.tensor_tensor(y[:, m, :], y[:, m, :], ps[:, m % 4, :], ALU.add).then_inc(dn_evac, 1)

                for t in (1, 2, 3):
                    w_lo(n0 + t, (s0 + t) % 2)
                hidden(G, 0)
                hidden_lo(G, 0, 0)
                w_lo(n0 + 4, s0)
                hidden(G, 1)
                hidden_lo(G, 1, 0)
                dve.wait_ge(y_zero, L + 1)

                def group(g, n, buf):
                    for t in (1, 2, 3):
                        w_lo(n + t, (s0 + t) % 2)
                    hidden(g, 0)
                    hidden_lo(g, 0, buf)
                    w_lo(n + 4, s0)
                    w_lo(n + 5, 1 - s0)
                    hidden(g, 1)
                    hidden_lo(g, 1, buf)
                    for m in range(4):
                        add(g - 1, m)
                    w_lo(n + 6, s0)
                    for m in range(4, 8):
                        add(g - 1, m)

                group(G + 1, n0 + 4, 1)
                with dve.Fori(0, (FG - 3) // 2) as i:
                    for v in range(2):
                        group(2 * i + G + 2 + v, 12 * i + n0 + 10 + 6 * v, v)
                group(G + FG - 1, n0 + 4 + 6 * (FG - 2), 0)
                w_lo(n0 + 6 * FG - 1, 1 - s0)
                for m in range(4):
                    add(G + FG - 1, m)
                if L == 0:
                    w_lo(n0 + 6 * FG, s0)
                for m in range(4, 8):
                    add(G + FG - 1, m)

            ffn(0, N_F0)
            residual(1, G0 + 3 * KT, 3, None)
            dve.wait_ge(rs_ready, 5)
            x_split(7 * KT, normed(G0 + 4 * KT), None)

            def rotate(l):
                raw, rot, b = tmp[:, l % 2, :], ps[:, 2 + l % 2, :], sqb[:, l % 2, :]
                dve.wait_ge(mm_evac, 8 + l + 1)
                dve.wait_ge(rot_f, l + 1)
                own.link(dve.tensor_tensor(b, rot, sinT, ALU.mult))
                own.link(dve.tensor_tensor(raw, raw, cosT, ALU.mult))
                if l < 8:
                    own.link(dve.tensor_tensor(raw, raw, b, ALU.add))
                    dve.tensor_scalar(q[:, l, :], raw, SCALE, None, ALU.mult).then_inc(rot_r, 1)
                else:
                    kv = 2 * (l - 8)
                    dve.tensor_tensor(kd[0:HD, kv, P:], raw[0:HD, :], b[0:HD, :], ALU.add).then_inc(kd_r, 1)
                    dve.tensor_tensor(kd[HD:P, kv + 1, P:], raw[HD:P, :], b[HD:P, :], ALU.add).then_inc(rot_r, 1)

            dve.wait_ge(a_in, 32)
            dve.wait_ge(pad_r, 1)
            for l in range(12):
                w_lo(N_QKV + l + 1, (N_QKV + l + 1) % 2)
                if 1 <= l <= 10:
                    rotate(l - 1)

            def masked(it):
                n, kv = it // NKV, it % NKV
                b = it % 2
                dve.wait_ge(s_f, it + 1)
                if it >= 2:
                    dve.wait_ge(pt_f, it - 1)
                s3 = sc[:, b, :].rearrange("p (i c) -> p i c", c=2 * P)
                dve.tensor_tensor(s3, ps[:, b, :].rearrange("p (i c) -> p i c", c=2 * P),
                                  msk[min(n, 1)].unsqueeze(1).to_broadcast([P, 4, 2 * P]), ALU.add).then_inc(sm_m, 1)
                dve.wait_ge(sm_m, it + 1)
                own.link(dve.tensor_reduce(st[:, b, 0, :], s3, AX_X, ALU.max))
                sk = pr[:, SINK + 4 * kv:SINK + 4 * kv + 4]
                own.link(dve.tensor_tensor(st[:, b, 0, :], st[:, b, 0, :], sk, ALU.max))
                own.link(dve.tensor_scalar(st[:, b, 1, :], st[:, b, 0, :], -1.0, None, ALU.mult))
                dve.tensor_tensor(st[:, b, 3, :], st[:, b, 1, :], sk, ALU.add).then_inc(nm_r, 1)

            def denominators(it):
                b = it % 2
                dve.wait_ge(p_r, it + 1)
                own.link(dve.tensor_tensor(st[:, b, 4, :], st[:, b, 2, :], st[:, b, 3, :], ALU.add))
                own.link(dve.reciprocal(st[:, b, 5, :], st[:, b, 4, :]))
                s3 = sc[:, b, :].rearrange("p (i c) -> p i c", c=2 * P)
                dve.tensor_tensor(s3, s3, st[:, b, 5, :].unsqueeze(2).to_broadcast([P, 4, 2 * P]), ALU.mult).then_inc(p_n, 1)

            def o_lo(it):
                n, kv = it // NKV, it % NKV
                dve.wait_ge(o_r, it + 1)
                dst = slice(n * P, (n + 1) * P)
                dve.tensor_tensor(xl[:, 2 * kv:2 * kv + 2, dst], bank(6 + it % 2)[:, 0:2 * P].rearrange("p (a b) -> p a b", b=P),
                                  xh[:, 2 * kv:2 * kv + 2, dst].bitcast(F32), ALU.subtract).then_inc(oz_r, 1)

            IT = NB * NKV
            masked(0)
            for it in range(IT):
                if it + 1 < IT:
                    masked(it + 1)
                denominators(it)
                if it >= 2:
                    o_lo(it - 2)
            o_lo(IT - 2)
            o_lo(IT - 1)
            for t in range(8):
                w_lo(N_AO + t + 1, (N_AO + t + 1) % 2)
            residual(2, G0 + 5 * KT, 5, (x_in, 48))
            dve.wait_ge(rs_ready, 7)
            x_split(8 * KT, normed(G0 + 6 * KT), None)
            ffn(1, N_F1)
            residual(3, G0 + 7 * KT, 7, None)


def lay_out(i):
    f = {k: np.asarray(v) for k, v in i.items()}

    def tiles(w):
        k, n = w.shape
        return w.reshape(k // P, P, n // P, P).transpose(2, 1, 0, 3).reshape(n // P, P, -1)

    def wide(w):
        return np.concatenate([w, np.zeros((w.shape[0], P - w.shape[1]), w.dtype)], 1)

    def ffn(L):
        gu, dn = tiles(f["ffn_w_gate_up"][L]), f["ffn_w_down"][L]
        dn = dn.reshape(FG, 2, P, 2, HALF).transpose(0, 3, 2, 1, 4).reshape(FG, 2, P, T)
        seq = []
        for g in range(FG + 1):
            if g < FG:
                for t in (2 * g, 2 * g + 1):
                    seq += [gu[t], gu[D_FF // P + t]]
            if g >= 1:
                seq += [dn[g - 1, 0], dn[g - 1, 1]]
        return np.stack(seq)

    wt = np.concatenate([
        tiles(f["rwkv_w_rkv"][0, 0]), tiles(f["rwkv_w_rkv"][0, 1]), tiles(f["rwkv_w_rkv"][0, 2]),
        tiles(wide(f["rwkv_w1"][0])), tiles(wide(f["rwkv_a1"][0])), tiles(f["rwkv_g1"][0]),
        tiles(f["rwkv_w_o"][0]), ffn(0), tiles(f["attn_w_qkv"][0]), tiles(f["attn_w_o"][0]), ffn(1)])

    def cols(v):
        return v.reshape(-1, P).T

    sinks = f["attn_sinks"][0].reshape(NKV, 2, 2).transpose(0, 2, 1).reshape(1, -1)
    one = np.ones((P, 1), np.float32)
    par = np.concatenate([
        cols(f["norm_g"]), cols(f["rwkv_x_mix"]), cols(f["rwkv_w0"]), cols(f["rwkv_a0"]), cols(f["rwkv_k_k"]),
        cols(f["rwkv_k_a"]), cols(f["rwkv_r_k"]), cols(f["rwkv_lnx_w"]), cols(f["rwkv_lnx_b"]),
        cols(f["attn_b_qkv"]), cols(f["attn_b_o"]), np.repeat(sinks, P, 0),
        np.full((P, 1), RMS_EPS, np.float32), np.full((P, 1), GN_EPS, np.float32),
        np.full((P, 1), 0.5 * LN_SHIFT * np.log(2.0), np.float32)], 1)

    def tall(w):
        w = np.concatenate([w, np.zeros((P - w.shape[0], D), w.dtype)], 0)
        return w.reshape(P, NHP, P).transpose(1, 0, 2)

    lora2 = np.stack([tall(f["rwkv_w2"][0]), tall(f["rwkv_a2"][0]), tall(f["rwkv_g2"][0])], 2)
    xT = f["x"][0].T.reshape(KT, P, T).transpose(1, 0, 2)
    base, rw, at = shape_constants()
    return [np.ascontiguousarray(a) for a in (xT, wt, par, lora2, base, rw, at)]


def kernel(**inputs):
    import concourse.bacc as bacc
    from concourse.bass_utils import run_bass_kernel_spmd

    nc = bacc.Bacc("TRN2", target_bir_lowering=False, num_devices=1)
    names = ("xT", "wt", "par", "lora2", "cbase", "crw", "cat")
    arrays = dict(zip(names, lay_out(inputs)))
    aps = [nc.dram_tensor(n, arrays[n].shape, F32, kind="ExternalInput").ap() for n in names]
    out = nc.dram_tensor("out", [P, KT, T], F32, kind="ExternalOutput").ap()
    build_program(nc, *aps, out)
    r = run_bass_kernel_spmd(nc, [arrays], core_ids=[0])
    got = r.results[0]["out"]
    return np.ascontiguousarray(got.transpose(1, 0, 2).reshape(1, D, T).transpose(0, 2, 1))
```

```python
from contextlib import ExitStack

import numpy as np

import concourse.bass as bass
from concourse import mybir

F32 = mybir.dt.float32
F32R = mybir.dt.float32r
ALU = mybir.AluOpType
ACT = mybir.ActivationFunctionType
AX_X = mybir.AxisListType.X
LN_EXP = "natural_log_exp_and_others"

P = 128
D = 1024
T = 1024
KT = D // P
HALF = 512
D_FF = 2816
FG = D_FF // (2 * P)
HD = 64
C = 64
NHP = D // P
DECAY = float(np.exp(-0.5))
RMS_EPS = 1e-6
GN_EPS = 64e-5
SCALE = HD ** -0.5
NKV = 4
NB = T // P
LN_SHIFT = 17

N_RKV, N_LORA, N_WO = 0, 24, 27
N_F0 = N_WO + 8
N_QKV = N_F0 + 6 * FG
N_AO = N_QKV + 12
N_F1 = N_AO + 8
N_ALL = N_F1 + 6 * FG
MIX_LAST = (7, 15, 23, 24, 25)

G0, MIX, W0, A0, KK, KA, RK, LNW, LNB = 0, 64, 112, 120, 128, 136, 144, 152, 160
BQKV, BO, SINK, EPS_RMS, EPS_GN, KSH = 168, 180, 188, 204, 205, 206
NPAR = 207


def shape_constants():
    i = np.arange(P)
    same = lambda n: (i[:, None] // n) == (i[None, :] // n)
    up = i[None, :] > i[:, None]
    ident = np.eye(P)
    blk = same(HD)
    strict = same(C) & up
    incl = same(C) & (up | np.eye(P, dtype=bool))
    e = [same(2 * b) & ~same(b) & up for b in (8, 16, 32)]
    base = np.concatenate([ident, np.ones((P, P)), blk], 1).astype(np.float32)
    rst = np.tile((np.arange(HALF) % C != 0).astype(np.float32), (P, 1))
    rw = np.concatenate([rst, strict, incl, same(8) & up] + e, 1).astype(np.float32)
    rope = HD // 4
    inv = np.float32(500000.0) ** (-np.arange(0, rope, 2, dtype=np.float32) / np.float32(rope))
    ang = np.arange(T, dtype=np.float32)[:, None] * inv[None, :].astype(np.float32)
    cos, sin = np.ones((P, T), np.float32), np.zeros((P, T), np.float32)
    perm = np.zeros((P, P), np.float32)
    for h in (0, HD):
        for d in range(rope // 2):
            lo, hi = h + d, h + d + rope // 2
            cos[lo] = cos[hi] = np.cos(ang[:, d])
            sin[lo] = sin[hi] = np.sin(ang[:, d])
            perm[hi, lo] = -1.0
            perm[lo, hi] = 1.0
    qi, kj = np.arange(P)[:, None], np.arange(2 * P)[None, :]
    rel = qi + P - kj
    band = (rel >= 0) & (rel < P)
    far = np.float32(-1e30)
    m = np.where(band, 0, far).astype(np.float32)
    m0 = np.where(band & (kj >= P), 0, far).astype(np.float32)
    at = np.concatenate([cos, sin, perm, m0, m], 1).astype(np.float32)
    return base, rw, at


def build_program(nc, xT, wt, par, lora2, cbase, crw, cat, out):
    ctx = ExitStack()
    with ctx:
        def keep(stack, name, shape, dt=F32):
            return stack.enter_context(nc.sbuf_tensor(name, shape, dt))

        def sem(name):
            return ctx.enter_context(nc.semaphore(name))

        xh = keep(ctx, "xh", [P, KT, T], F32R)
        xl = keep(ctx, "xl", [P, KT, T], F32R)
        wst = keep(ctx, "wst", [P, 2, T])
        wh = keep(ctx, "wh", [P, 2, T], F32R)
        wl = keep(ctx, "wl", [P, 2, T], F32R)
        sqb = keep(ctx, "sqb", [P, 2, T])
        tmp = keep(ctx, "tmp", [P, 2, T])
        cb = keep(ctx, "cb", [P, 3 * P])
        pr = keep(ctx, "pr", [P, NPAR])
        ident, ones, blk = (cb[:, i * P:(i + 1) * P] for i in range(3))
        rstd = keep(ctx, "rstd", [P, T])
        ps = ctx.enter_context(nc.psum_tensor("ps", [P, 4, T], F32))

        s_n = ExitStack()
        x = keep(s_n, "x", [P, KT, T])
        y = keep(s_n, "y", [P, KT, T])
        hidh = keep(s_n, "hidh", [P, 2, 2, T], F32R)
        hidl = keep(s_n, "hidl", [P, 2, 2, T], F32R)
        s_n.close()
        s_ab = ExitStack()
        lor = keep(s_ab, "lor", [P, 3, T])
        s_a = ExitStack()
        h = keep(s_a, "h", [P, KT, T + 1])
        xx = keep(s_a, "xx", [P, KT, T])
        ost = keep(s_a, "ost", [P, 2, T])
        s_a.close()
        s_b = ExitStack()
        cr = keep(s_b, "cr", [P, 512 + 6 * P])
        rst, m_si, mu8 = cr[:, 0:512], cr[:, 512:768], cr[:, 768:896]
        me = [cr[:, 896 + P * i:1024 + P * i] for i in range(3)]
        l2 = keep(s_b, "l2", [P, 2, P])
        l2g = keep(s_b, "l2g", [P, P])
        rin = keep(s_b, "rin", [P, HALF])
        kin = keep(s_b, "kin", [P, HALF])
        vin = keep(s_b, "vin", [P, 2, HALF])
        At, Bt, Kt, Rt, bon = (keep(s_b, n, [P, 2, HALF]) for n in ("At", "Bt", "Kt", "Rt", "bon"))
        pend = keep(s_b, "pend", [P, 2, 8])
        pcp = keep(s_b, "pcp", [P, 6])
        pcq = keep(s_b, "pcq", [P, 2])
        Sm = [[keep(s_b, f"Sm{a}{g}", [P, 2, 4, P]) for g in range(2)] for a in range(2)]
        TT = [[keep(s_b, f"TT{a}{g}", [P, 2, 2, P]) for g in range(2)] for a in range(2)]
        tok = [[keep(s_b, f"tok{a}{g}", [P, 3, P]) for g in range(2)] for a in range(2)]
        Et = [keep(s_b, f"Et{g}", [P, 3, 2, P]) for g in range(2)]
        Dt = [keep(s_b, f"Dt{g}", [P, 2, P]) for g in range(2)]
        Dn = [keep(s_b, f"Dn{g}", [P, 2, P]) for g in range(2)]
        D2 = [keep(s_b, f"D2{g}", [P, 2, 2, P]) for g in range(2)]
        Wm = [keep(s_b, f"Wm{g}", [P, 2, P]) for g in range(2)]
        rhs_sb = keep(s_b, "rhs_sb", [P, P])
        SA = [keep(s_b, f"SA{g}", [P, P]) for g in range(2)]
        S = keep(s_b, "S", [P, P])
        SP = keep(s_b, "SP", [P, P])
        ysb = keep(s_b, "ysb", [P, HALF])
        psq, zt = rstd[:, 0:HALF], rstd[:, HALF:T]
        s_b.close()
        s_ab.close()
        s_c = ExitStack()
        q = keep(s_c, "q", [P, KT, T])
        kd = keep(s_c, "kd", [P, NKV, T + P])
        vt = keep(s_c, "vt", [P, NB + 1, NKV, HD])
        ca = keep(s_c, "ca", [P, 2 * T + P + 4 * P])
        cosT, sinT, perm = ca[:, 0:T], ca[:, T:2 * T], ca[:, 2 * T:2 * T + P]
        msk = [ca[:, 2 * T + P + 256 * i:2 * T + P + 256 * i + 256] for i in range(2)]
        sc = keep(s_c, "sc", [P, 3, T])
        pT = keep(s_c, "pT", [P, 2, 4 * P])
        st = keep(s_c, "st", [P, 3, 6, 4])
        s_c.close()

        T0, T1, T2, T3 = (sqb[:, i // 2, (i % 2) * HALF:(i % 2) * HALF + HALF] for i in range(4))
        T4, T5, T6, T7 = (tmp[:, i // 2, (i % 2) * HALF:(i % 2) * HALF + HALF] for i in range(4))

        rkv_d = nc.dram_tensor("rkv_scratch", [3, NHP, P, T], F32).ap()
        x_d = nc.dram_tensor("x_scratch", [P, KT, T], F32).ap()

        c_in, a_in = sem("const_loaded"), sem("phase_const_loaded")
        w_dma = [sem("w_loaded0"), sem("w_loaded1")]
        w_hi, w_split, w_used = sem("w_hi_ready"), sem("w_split_ready"), sem("w_tile_used")
        mm_evac = sem("tile_evacuated")
        x_first = [sem(f"x_part{i}_loaded") for i in range(4)]
        x_in, x_out = sem("x_loaded"), sem("x_saved")
        x_odd, x_used, xx_odd = sem("x_odd_split_ready"), sem("x_tile_used"), sem("shift_diff_odd_ready")
        acc_sq, acc_done, sum_full = sem("y_square_ready"), sem("y_squares_added"), sem("y_sum_full")
        scaled, res_odd = sem("y_scaled"), sem("residual_odd_done")
        sq_ready, sq_used, rs_ready = sem("square_ready"), sem("square_used"), sem("rstd_ready")
        xn_ready, xhi_ready, x_ready = sem("normed_ready"), sem("x_hi_ready"), sem("x_split_ready")
        act_own, dve_own, pool_own = sem("scalar_step"), sem("vector_step"), sem("pool_step")
        h_ready, xx_ready = sem("h_ready"), sem("shift_diff_ready")
        o_full, o_dma = [sem("spill0_full"), sem("spill1_full")], [sem("spill0_written"), sem("spill1_written")]
        lo_ready = sem("lora_ready")
        res_done = sem("residual_done")
        sg_ready, up_mul, hid_hi, hid_ready = (sem(n) for n in ("silu_ready", "hidden_ready", "hidden_hi_ready", "hidden_split"))
        dn_full, dn_evac, y_zero = sem("down_full"), sem("down_added"), sem("y_zeroed")
        st_full = [sem(f"st{i}_full") for i in range(14)]
        st_evac = [sem(f"st{i}_evac") for i in range(14)]
        dt_ready, x1_ready = sem("Dt_ready"), sem("X1_ready")
        e_ready = sem("E_ready")
        rhs_full, rhs_sbr, sa_full, sa_sbr, ds_full, s_ready = (sem(n) for n in (
            "rhs_full", "rhs_copied", "sa_full", "sa_copied", "chunk_done", "state_ready"))
        l_in, lg_in, r_in, k_in = sem("l2_loaded"), sem("l2g_loaded"), sem("r_loaded"), sem("k_loaded")
        v_in = [sem("v_loaded0"), sem("v_loaded1")]
        zw_f, za_f, mean_f, ss_f, var_f, g_f, bon_f = (sem(n + "_full") for n in ("zw", "za", "mean", "ss", "var", "g", "bonus"))
        zw_e, za_e, mean_e, ss_e, var_e, g_e, bon_e = (sem(n + "_read") for n in ("zw", "za", "mean", "ss", "var", "g", "bonus"))
        ksq_r, s_r, sm_r, P_r, ssm_r, rinv_r, prep_done, rk_r, sp_ready = (sem(n) for n in (
            "key_square", "decay_sum", "decay_sum_prev", "decays", "ss_clamped", "key_rnorm", "prep_done", "rk_ready", "state_decayed"))
        y_sb, yc_r, ysq_r, yrs_r, z_r, zhi_r, z_ready = (sem(n) for n in (
            "y_copied", "y_centred", "y_square", "y_rstd", "z_ready", "z_hi", "z_split"))
        pq_r = sem("post_params")
        y_tile, pp_r = sem("y_tile_done"), sem("prep_params")
        raw_r, rot_f, rot_r = sem("qkv_raw"), sem("rotated_full"), sem("rope_done")
        vtr_f, vtr_r, kd_r, pad_r = sem("v_transposed"), sem("v_tokens"), sem("keys_ready"), sem("kv_padded")
        s_f, sm_m, nm_r, p_r, p_n, pt_f, pt_r, o_f, o_r = (sem(n) for n in (
            "scores_full", "scores_masked", "max_ready", "probs_ready", "probs_normed",
            "pT_full", "pT_copied", "o_full", "o_hi"))
        oz_r, den_r = sem("o_split"), sem("denominators_ready")
        st_out = sem("out_written")

        class Own:
            def __init__(self, eng, s):
                self.eng, self.s, self.n, self.r = eng, s, 0, 0

            def link(self, ins):
                self.n += 1
                ins.then_inc(self.s, 1)
                self.eng.wait_ge(self.s, self.r + self.n)

        def bank(b):
            return ps[:, b // 2, (b % 2) * HALF:(b % 2) * HALF + HALF]

        def halves():
            return [(0, HALF), (HALF, T)]

        def inv_bank(s, g):
            return (2 * s + g) % 3

        def prior(s, g):
            e = 2 * s + g
            if e >= 3:
                return (e - 3) // 2, (e - 3) % 2, 0
            e = {0: 27, 1: 25, 2: 26}[e]
            return e // 2, e % 2, 1

        def xs(kt):
            return (tmp if kt % 4 < 2 else sqb)[:, kt % 2, :]

        def wait_x(eng, n):
            eng.wait_ge(x_odd if n % 2 else x_ready, n // 2 + 1)

        B_SC, B_Y, B_AUX0, B_AUX1 = 3, 4, 5, 6
        block = ctx.enter_context(nc.Block())

        @block.sync
        def _(sp):
            sp.dma_start(cb[:], cbase).then_inc(c_in, 16)
            sp.dma_start(pr[:], par).then_inc(c_in, 16)
            sp.dma_start(wst[:, 0, :], wt[0]).then_inc(w_dma[0], 16)
            sp.dma_start(wst[:, 1, :], wt[1]).then_inc(w_dma[1], 16)
            with sp.Fori(0, (N_ALL - 3) // 2) as i:
                for u in range(2):
                    sp.wait_ge(w_split, 2 * i + u + 1)
                    sp.dma_start(wst[:, u, :], wt[2 * i + 2 + u]).then_inc(w_dma[u], 16)
            sp.wait_ge(w_split, N_ALL - 2)
            sp.dma_start(wst[:, 0, :], wt[N_ALL - 1]).then_inc(w_dma[0], 16)
            for kt in range(KT):
                sp.wait_ge(res_odd if kt % 2 else res_done, KT // 2 * 3 + kt // 2 + 1)
                sp.dma_start(out[:, kt, :], x[:, kt, :]).then_inc(st_out, 16)
            sp.wait_ge(st_out, 16 * KT)

        @block.gpsimd
        def _(pool):
            own = Own(pool, pool_own)
            for i in range(4):
                pool.dma_start(h[:, 2 * i:2 * i + 2, 1:T + 1], xT[:, 2 * i:2 * i + 2, :]).then_inc(x_first[i], 16)
            own.link(pool.memset(h[:, :, 0:1], 0.0))

            def lo_part(b, kt):
                pool.wait_ge(xhi_ready, b + kt + 1)
                pool.tensor_tensor(xl[:, kt, :], xs(kt), xh[:, kt, :].bitcast(F32), ALU.subtract).then_inc(x_odd, 1)

            def lo_odd(b):
                for kt in range(1, KT, 2):
                    lo_part(b, kt)

            for kt in range(1, KT, 2):
                pool.wait_ge(h_ready, kt + 1)
                pool.tensor_tensor(xx[:, kt, :], h[:, kt, 0:T], h[:, kt, 1:T + 1], ALU.subtract).then_inc(xx_odd, 1)
                if kt >= 3:
                    lo_part(0, kt - 2)
            lo_part(0, KT - 1)
            for j in range(3):
                def spill(i, u):
                    pool.wait_ge(o_full[u], i + 4 * j + 1)
                    pool.dma_start(rkv_d[j][2 * i + u], ost[:, u, :]).then_inc(o_dma[u], 16)
                with pool.Fori(0, 3) as i:
                    for u in range(2):
                        spill(i, u)
                spill(3, 0)
                lo_odd(KT * (j + 1))
                spill(3, 1)
            for j in (4, 5):
                lo_odd(KT * j)
            wait_x(pool, 6 * KT - 2)
            wait_x(pool, 6 * KT - 1)
            pool.wait_ge(o_dma[0], 16 * 12)
            pool.wait_ge(o_dma[1], 16 * 12)
            pool.dma_start(cr[:], crw).then_inc(a_in, 16)

            def load_piece(hp, pc, first):
                r = 2 * hp + pc
                if not first:
                    pool.wait_ge(prep_done, r)
                if pc == 0:
                    if not first:
                        pool.wait_ge(za_f, r)
                    pool.dma_start(l2[:], lora2[hp][:, 0:2, :]).then_inc(l_in, 16)
                if not first:
                    pool.wait_ge(bon_e, r)
                if not (first or (pc == 1 and type(hp) is int and hp == 0)):
                    pool.wait_ge(st_full[2], 8 * hp + 4 * pc - 4)
                cols = slice(pc * HALF, pc * HALF + HALF)
                pool.dma_start(rin[:], rkv_d[0, hp][:, cols]).then_inc(r_in, 16)
                pool.dma_start(kin[:], rkv_d[1, hp][:, cols]).then_inc(k_in, 16)
                pool.dma_start(vin[:, pc, :], rkv_d[2, hp][:, cols]).then_inc(v_in[pc], 16)

            def load_g(hp, first):
                if not first:
                    pool.wait_ge(g_f, 2 * hp)
                pool.dma_start(l2g[:], lora2[hp][:, 2, :]).then_inc(lg_in, 16)

            def merge_masks(k, a, nopr):
                for g in range(2):
                    pool.wait_ge(st_evac[1], 2 * k + g + 1)
                    if not nopr:
                        pool.wait_ge(st_full[12], 2 * k + g - 1)
                    for lv in range(3):
                        ins = pool.tensor_tensor(Et[g][:, lv], Sm[a][g][:, :, 0, :],
                                                 me[lv].unsqueeze(1).to_broadcast([P, 2, P]), ALU.mult)
                    ins.then_inc(e_ready, 1)

            def body(hp, first, last):
                load_piece(hp, 1, False)
                merge_masks(4 * hp + 1, 1, False)
                load_g(hp, first)
                merge_masks(4 * hp + 2, 0, False)
                if not last:
                    load_piece(hp + 1, 0, False)
                merge_masks(4 * hp + 3, 1, False)
                if not last:
                    merge_masks(4 * hp + 4, 0, False)

            load_piece(0, 0, True)
            pool.wait_ge(a_in, 16)
            merge_masks(0, 0, True)
            body(0, True, False)
            with pool.Fori(1, NHP - 1) as hp:
                body(hp, False, False)
            body(NHP - 1, False, True)

            pool.wait_ge(z_ready, 16)
            pool.wait_ge(ds_full, 16 * NHP)
            pool.wait_ge(e_ready, 2 * 32)
            pool.dma_start(x[:], xT).then_inc(x_in, 16)

            def residual_odd(i):
                for kt in range(1, KT, 2):
                    pool.wait_ge(scaled, KT * i + kt)
                    pool.tensor_tensor(x[:, kt, :], x[:, kt, :], y[:, kt, :], ALU.add).then_inc(res_odd, 1)

            def ffn_zero(i):
                pool.wait_ge(res_done, KT // 2 * (i + 1))
                pool.wait_ge(res_odd, KT // 2 * (i + 1))
                pool.memset(y[:], 0.0).then_inc(y_zero, 1)

            pool.wait_ge(x_in, 16)
            residual_odd(0)
            lo_odd(6 * KT)
            ffn_zero(0)
            residual_odd(1)
            pool.wait_ge(res_done, KT // 2 * 2)
            pool.wait_ge(res_odd, KT // 2 * 2)
            pool.dma_start(x_d, x[:]).then_inc(x_out, 16)
            lo_odd(7 * KT)
            pool.wait_ge(x_out, 16)
            pool.wait_ge(xn_ready, KT * 2)
            pool.dma_start(ca[:], cat).then_inc(a_in, 16)
            pool.memset(kd[:, :, 0:P], 0.0)
            pool.memset(vt[:, 0, :, :], 0.0).then_inc(pad_r, 1)
            for it in range(NB * NKV):
                pool.wait_ge(den_r, it + 1)
                for i in range(4):
                    p_i = sc[:, it % 3, i * 2 * P:(i + 1) * 2 * P]
                    ins = pool.tensor_scalar(p_i, p_i, st[:, it % 3, 5, i:i + 1], None, ALU.mult)
                ins.then_inc(p_n, 1)
            pool.wait_ge(oz_r, NB * NKV)
            pool.dma_start(x[:], x_d).then_inc(x_in, 16)
            pool.wait_ge(x_in, 32)
            residual_odd(2)
            lo_odd(8 * KT)
            ffn_zero(2)
            residual_odd(3)

        @block.tensor
        def _(pe):
            pe.wait_ge(c_in, 32)

            def dense(n, r, slot, free, xb, count_x=False):
                pe.wait_ge(w_split, n + r + 1)
                if free is not None:
                    pe.wait_ge(mm_evac, free + r)
                for kt in range(KT):
                    if xb is not None:
                        wait_x(pe, xb + kt)
                    for j, (a, b) in enumerate(((wh, xh), (wh, xl), (wl, xh))):
                        for lo, hi in halves():
                            ins = pe.matmul(ps[:, slot, lo:hi], a[:, n % 2, kt * P:(kt + 1) * P],
                                            b[:, kt, lo:hi], start=(kt == 0 and j == 0),
                                            stop=(kt == KT - 1 and j == 2))
                    if count_x and kt < KT - 1:
                        ins.then_inc(x_used, 1)
                ins.then_inc(w_used, 1)

            def stats_y(i):
                pe.wait_ge(acc_done, (KT - 1) * (i + 1))
                for lo, hi in halves():
                    ins = pe.matmul(ps[:, 3, lo:hi], ones, rstd[:, lo:hi], start=True, stop=True)
                ins.then_inc(sum_full, 1)

            def stats(nn):
                for kt in range(KT):
                    pe.wait_ge(sq_ready, KT * nn + kt + 1)
                    for lo, hi in halves():
                        ins = pe.matmul(ps[:, 3, lo:hi], ones, sqb[:, kt % 2, lo:hi],
                                        start=(kt == 0), stop=(kt == KT - 1))
                    ins.then_inc(sq_used, 1)

            stats(0)
            def rkv(j, t, r):
                n = 8 * j + t
                if n >= 4:
                    pe.wait_ge(o_full[t % 2], (n - 4) // 2 + 1 + 2 * r)
                dense(n, 4 * r, t % 4, None, KT * j, True)

            for t in range(8):
                rkv(0, t, 0)
            for j in (1, 2):
                with pe.Fori(0, 2) as i:
                    for t in range(4):
                        rkv(j, t, i)
            for j in range(3):
                n = N_LORA + j
                pe.wait_ge(o_full[n % 2], (n - 4) // 2 + 1)
                dense(n, 0, n % 4, None, KT * (3 + j), True)

            def mm(o, a, b, start, stop=True):
                return pe.matmul(o, a, b, start=start, stop=stop, skip_group_check=True)

            def stage(s, g, k, a, nopr):
                b = bank(inv_bank(s, g))
                ps_, pg, back = prior(s, g)
                if not (back and nopr):
                    pe.wait_ge(st_evac[ps_], 2 * (k - back) + pg + 1)
                cols = slice(a * 256 + g * P, a * 256 + g * P + P)
                if s < 2:
                    hh = slice(HD * s, HD * s + HD)
                    for i, L in enumerate((Bt, Kt)):
                        for j, R in enumerate((At, Rt)):
                            ins = mm(b[:, (2 * i + j) * P:(2 * i + j + 1) * P], L[hh, pcs, cols], R[hh, pcs, cols], i + j == 0)
                elif s == 2:
                    for i, src in enumerate((vin, Bt, Kt)):
                        ins = pe.transpose(b[:, i * P:(i + 1) * P], src[:, pcs, cols], ident)
                elif s == 3:
                    pe.wait_ge(dt_ready, 2 * k + g + 1)
                    for i in range(2):
                        ins = pe.transpose(b[:, i * P:(i + 1) * P], Dt[g][:, i, :], ident)
                elif s == 4:
                    pe.wait_ge(st_evac[3], 2 * k + g + 1)
                    for i in range(2):
                        mm(b[:, i * P:(i + 1) * P], Dn[g][:, i, :], Dt[g][:, i, :], i == 0)
                        ins = mm(b[:, (2 + i) * P:(3 + i) * P], Dt[g][:, i, :], Dn[g][:, i, :], False)
                elif s == 5:
                    pe.wait_ge(st_evac[4], 2 * k + g + 1)
                    pe.wait_ge(x1_ready, 2 * k + g + 1)
                    for i in range(2):
                        mm(b[:, i * P:(i + 1) * P], D2[g][:, 1, i, :], TT[a][g][:, 0, i, :], i == 0)
                        ins = mm(b[:, (2 + i) * P:(3 + i) * P], D2[g][:, 0, i, :], D2[g][:, 1, i, :], False)
                elif s == 6:
                    pe.wait_ge(st_evac[5], 2 * k + g + 1)
                    for i in range(2):
                        ins = mm(b[:, i * P:(i + 1) * P], Dn[g][:, i, :], TT[a][g][:, 0, i, :], i == 0)
                elif s == 7:
                    pe.wait_ge(st_evac[6], 2 * k + g + 1)
                    for i in range(2):
                        ins = pe.transpose(b[:, i * P:(i + 1) * P], TT[a][g][:, 0, i, :], ident)
                elif s % 2 == 0:
                    pe.wait_ge(e_ready, 2 * k + g + 1)
                    pe.wait_ge(st_evac[s - 1], 2 * k + g + 1)
                    for i in range(2):
                        ins = mm(b[:, i * P:(i + 1) * P], Et[g][:, (s - 8) // 2, i, :], TT[a][g][:, 1, i, :], i == 0)
                else:
                    pe.wait_ge(st_evac[s - 1], 2 * k + g + 1)
                    for i in range(2):
                        ins = mm(b[:, i * P:(i + 1) * P], Wm[g][:, i, :], TT[a][g][:, 0, i, :], i == 0)
                        if s < 13:
                            ins = mm(b[:, (2 + i) * P:(3 + i) * P], TT[a][g][:, 0, i, :], Wm[g][:, i, :], False)
                ins.then_inc(st_full[s], 1)

            def scan(f, hp, u, first):
                c, ph = f // 3, f % 3
                g, p = c // 2, c % 2
                a, pc = u % 2, u // 2
                n = 16 * hp + 4 * u + c
                tp = slice(C * p, C * p + C)
                base = a * 256 + g * P
                cols = slice(base + C * p, base + C * p + C)
                sc, yb = bank(B_SC), bank(B_Y)
                sm, tk = Sm[a][g], tok[a][g]
                if ph == 0:
                    if c == 0:
                        pe.wait_ge(st_evac[13], 2 * (4 * hp + u) + 2)
                        if a == 0 and not (first and pc == 0):
                            pe.wait_ge(y_sb, 2 * hp + pc)
                    pe.wait_ge(s_ready, n + 1)
                    mm(sc[tp, 0:P], At[:, pc, cols], S[:], True)
                    for i in range(2):
                        hh = slice(HD * i, HD * i + HD)
                        ins = mm(sc[tp, hh], sm[:, i, 2, tp], tk[:, 0, hh], False)
                    ins.then_inc(rhs_full, 1)
                elif ph == 1:
                    mm(yb[:, cols], S[:], Rt[:, pc, cols], c == 0 and a == 0)
                    pe.wait_ge(rhs_sbr, n + 1)
                    for i in range(2):
                        ins = mm(sc[tp, P + HD * i:P + HD * i + HD], TT[a][g][:, 0, i, tp],
                                 rhs_sb[:, HD * i:HD * i + HD], i == 0)
                    ins.then_inc(sa_full, 1)
                else:
                    pe.wait_ge(sa_sbr, n + 1)
                    mm(sc[:, 2 * P:3 * P], tk[tp, 1, :], SA[g][tp, :], True)
                    mm(sc[:, 2 * P:3 * P], tk[tp, 2, :], tk[tp, 0, :], False).then_inc(ds_full, 1)
                    if p == 1:
                        for i in range(2):
                            hh = slice(HD * i, HD * i + HD)
                            mm(yb[hh, base:base + P], SA[g][:, hh], sm[:, i, 1, :], False)
                            ins = mm(yb[hh, base:base + P], tk[:, 0, hh], sm[:, i, 3, :], False)
                        ins.then_inc(y_tile, 1)

            def is0(v, below=1):
                return type(v) is int and v < below

            def prep(e, r, hp, pc):
                cols = slice(pc * HALF, pc * HALF + HALF)
                if e == 0:
                    if not is0(r):
                        pe.wait_ge(bon_e, r)
                    pe.wait_ge(l_in, 16 * (hp + 1))
                    mm(bank(B_AUX0), l2[:, 0, :], lor[:, 0, cols], True).then_inc(zw_f, 1)
                    if not is0(r):
                        pe.wait_ge(ss_e, r)
                    if not is0(r, 3):
                        pe.wait_ge(z_r, r - 2)
                    mm(bank(B_AUX1), l2[:, 1, :], lor[:, 1, cols], True).then_inc(za_f, 1)
                elif e == 1:
                    pe.wait_ge(za_e, r + 1)
                    pe.wait_ge(ksq_r, r + 1)
                    mm(bank(B_AUX1), blk, T6, True).then_inc(ss_f, 1)
                else:
                    pe.wait_ge(rk_r, r + 1)
                    mm(bank(B_AUX0), blk, T6, True).then_inc(bon_f, 1)

            def post(e, p, hp, pc, alone):
                cols = slice(pc * HALF, pc * HALF + HALF)
                if e == 0:
                    if alone == 0:
                        pe.wait_ge(zw_e, p + 3)
                    elif alone == 1:
                        pe.wait_ge(bon_e, 16)
                    else:
                        pe.wait_ge(var_e, p)
                    pe.wait_ge(y_sb, p + 1)
                    mm(bank(B_AUX0), blk, ysb[:], True).then_inc(mean_f, 1)
                elif e == 1:
                    pe.wait_ge(ysq_r, p + 1)
                    mm(bank(B_AUX0), blk, psq, True).then_inc(var_f, 1)
                else:
                    pe.wait_ge(ss_e, p + 3 if alone == 0 else 16)
                    if not is0(p):
                        pe.wait_ge(z_r, p)
                    pe.wait_ge(lg_in, 16 * (hp + 1))
                    mm(bank(B_AUX1), l2g[:], lor[:, 2, cols], True).then_inc(g_f, 1)

            def rounds(inv, sc, busy):
                nonlocal pcs
                if inv:
                    k, u, nopr, need = inv
                    pcs = u // 2
                    pe.wait_ge(prep_done, need)
                    pe.wait_ge(bon_e, need)
                for s in range(14):
                    if inv:
                        stage(s, 0, k, u % 2, nopr)
                        stage(s, 1, k, u % 2, nopr)
                    if sc and 1 <= s <= 12:
                        scan(s - 1, *sc)
                    if busy:
                        pp, qq, alone = busy
                        if pp and s == 0:
                            prep(0, *pp)
                        if qq and s == 2:
                            post(0, *qq, alone)
                        if pp and s == 3:
                            prep(1, *pp)
                        if qq and s == 6:
                            post(1, *qq, alone)
                        if qq and s == 8:
                            post(2, *qq, alone)
                        if pp and s == 10:
                            if qq:
                                pe.wait_ge(var_e, pp[0] - 1)
                            prep(2, *pp)

            pcs = 0

            def body(hp, first, last):
                rounds((4 * hp + 1, 1, False, 2 * hp + 1), (hp, 0, first),
                       ((2 * hp + 1, hp, 1), None if first else (2 * hp - 1, hp - 1, 1), 0))
                rounds((4 * hp + 2, 2, False, 2 * hp + 2), (hp, 1, first), None)
                rounds((4 * hp + 3, 3, False, 2 * hp + 2), (hp, 2, first),
                       (None if last else (2 * hp + 2, hp + 1, 0), (2 * hp, hp, 0), 1 if last else 0))
                rounds(None if last else (4 * hp + 4, 0, False, 2 * hp + 3), (hp, 3, first), None)

            pe.wait_ge(lo_ready, 3)
            pe.wait_ge(a_in, 16)
            for e in range(3):
                prep(e, 0, 0, 0)
            rounds((0, 0, True, 1), None, None)
            body(0, True, False)
            with pe.Fori(1, NHP - 1) as hp:
                body(hp, False, False)
            body(NHP - 1, False, True)
            for e in range(3):
                post(e, 15, NHP - 1, 1, 2)

            def project(n0, m0):
                for t in range(8):
                    dense(n0 + t, 0, t % 4, m0 + t - 3 if t >= 4 else None, None)

            pe.wait_ge(z_ready, 16)
            project(N_WO, 0)
            stats_y(0)
            stats(1)

            def ffn(L, n0, xb):
                s0 = n0 % 2

                def gate_up(n, ws, t):
                    pe.wait_ge(w_split, n + 1)
                    for kt in range(KT):
                        wait_x(pe, xb + kt)
                        for j, (a, b) in enumerate(((wh, xh), (wh, xl), (wl, xh))):
                            for lo, hi in halves():
                                ins = pe.matmul(ps[:, t, lo:hi], a[:, ws, kt * P:(kt + 1) * P], b[:, kt, lo:hi],
                                                start=(kt == 0 and j == 0), stop=(kt == KT - 1 and j == 2))
                    ins.then_inc(w_used, 1)

                def down(G, n, ws, cc, buf, gated):
                    pe.wait_ge(w_split, n + 1)
                    for m in range(4):
                        if cc == 0 and gated:
                            pe.wait_ge(sg_ready if m % 2 == 0 else up_mul, 2 * (G + 1) + m // 2 + 1)
                        else:
                            pe.wait_ge(dn_evac, 8 * G + 4 * cc + m - 3)
                        for kk in range(2):
                            pe.wait_ge(hid_ready, 2 * G + kk + 1)
                            for j, (a, b) in enumerate(((wh, hidh), (wh, hidl), (wl, hidh))):
                                for lo, hi in halves():
                                    ins = pe.matmul(ps[:, m, lo:hi], a[:, ws, kk * HALF + m * P:kk * HALF + (m + 1) * P],
                                                    b[:, buf, kk, lo:hi], start=(kk == 0 and j == 0),
                                                    stop=(kk == 1 and j == 2))
                        ins.then_inc(dn_full, 1)

                G = FG * L
                for t in range(4):
                    gate_up(n0 + t, (s0 + t) % 2, t)
                for t in range(4):
                    pe.wait_ge(sg_ready if t % 2 == 0 else up_mul, 2 * G + t // 2 + 1)
                    gate_up(n0 + 4 + t, (s0 + t) % 2, t)
                down(G, n0 + 8, s0, 0, 0, True)
                down(G, n0 + 9, 1 - s0, 1, 0, True)

                def group(g, n, buf):
                    for t in range(4):
                        pe.wait_ge(dn_evac, 8 * (g - 2) + 4 + t + 1)
                        gate_up(n + t, (s0 + t) % 2, t)
                    down(g - 1, n + 4, s0, 0, 1 - buf, True)
                    down(g - 1, n + 5, 1 - s0, 1, 1 - buf, True)

                with pe.Fori(0, (FG - 3) // 2) as i:
                    for v in range(2):
                        group(2 * i + G + 2 + v, 12 * i + n0 + 10 + 6 * v, v)
                group(G + FG - 1, n0 + 4 + 6 * (FG - 2), 0)
                down(G + FG - 1, n0 + 6 * FG - 2, s0, 0, 0, False)
                down(G + FG - 1, n0 + 6 * FG - 1, 1 - s0, 1, 0, False)

            ffn(0, N_F0, 6 * KT)
            stats_y(1)
            stats(2)

            def qkv(l):
                if l >= 2:
                    pe.wait_ge(mm_evac, 8 + l - 1)
                n = N_QKV + l
                dense(n, 0, l % 2, None, 7 * KT)

            def turn(l):
                sl = 2 + l % 2
                pe.wait_ge(mm_evac, 8 + l + 1)
                if l >= 2:
                    pe.wait_ge(rot_r, l - 1)
                if l < 10:
                    for lo, hi in halves():
                        ins = mm(ps[:, sl, lo:hi], perm, tmp[:, l % 2, lo:hi], True)
                else:
                    for n in range(NB):
                        ins = pe.transpose(ps[:, sl, n * P:(n + 1) * P], tmp[:, l % 2, n * P:(n + 1) * P], ident)
                ins.then_inc(rot_f, 1)

            pe.wait_ge(a_in, 32)
            for l in range(12):
                qkv(l)
                if l >= 1:
                    turn(l - 1)
            turn(11)
            pe.wait_ge(rot_r, 12)
            pe.wait_ge(kd_r, 3)
            pe.wait_ge(pad_r, 1)

            def scores(it):
                n, kv = it // NKV, it % NKV
                if it >= 2:
                    pe.wait_ge(sm_m, it - 1)
                for i in range(4):
                    hh = slice(HD * (i % 2), HD * (i % 2) + HD)
                    o = (i % 2) * HALF + (i // 2) * 2 * P
                    ins = mm(ps[:, it % 2, o:o + 2 * P], q[hh, 2 * kv + i // 2, n * P:(n + 1) * P],
                             kd[hh, kv, n * P:(n + 2) * P], i < 2)
                ins.then_inc(s_f, 1)

            def probs(it):
                pe.wait_ge(p_n, it + 1)
                if it >= 1:
                    pe.wait_ge(pt_r, it)
                for kk in range(2):
                    for i in range(4):
                        ins = pe.transpose(bank(4 + kk)[:, i * P:(i + 1) * P],
                                           sc[:, it % 3, i * 2 * P + kk * P:i * 2 * P + (kk + 1) * P], ident)
                ins.then_inc(pt_f, 1)

            def values(it):
                n, kv = it // NKV, it % NKV
                pe.wait_ge(pt_r, it + 1)
                if it >= 2:
                    pe.wait_ge(oz_r, it - 1)
                o = bank(6 + it % 2)
                for odd in range(2):
                    for kk in range(2):
                        ins = mm(o[HD * odd:HD * odd + HD, 0:2 * P], vt[:, n + kk, kv, :],
                                 pT[:, kk, odd * 2 * P:(odd + 1) * 2 * P], kk == 0)
                ins.then_inc(o_f, 1)

            IT = NB * NKV
            scores(0)
            scores(1)
            for it in range(IT):
                if it + 2 < IT:
                    scores(it + 2)
                if it >= 1:
                    values(it - 1)
                probs(it)
            values(IT - 1)
            pe.wait_ge(oz_r, IT)
            project(N_AO, 20)
            stats_y(2)
            stats(3)
            ffn(1, N_F1, 8 * KT)
            stats_y(3)

        @block.scalar
        def _(act):
            own = Own(act, act_own)

            def w_round(n, r, after):
                act.wait_ge(w_dma[n % 2], 8 * r + 16 * (n // 2 + 1))
                if after:
                    act.wait_ge(*after)
                act.activation(wh[:, n % 2, :], wst[:, n % 2, :], ACT.Copy).then_inc(w_hi, 1)

            def squares(nn, src):
                for kt in range(KT):
                    if nn == 0:
                        act.wait_ge(x_first[kt // 2], 16)
                    else:
                        act.wait_ge(res_odd if kt % 2 else res_done, KT // 2 * (nn - 1) + kt // 2 + 1)
                    if KT * nn + kt >= 2:
                        act.wait_ge(sq_used, KT * nn + kt - 1)
                    act.activation(sqb[:, kt % 2, :], src(kt), ACT.Square).then_inc(sq_ready, 1)

            def square_y(i, t, ready):
                act.wait_ge(*ready)
                if t >= 3:
                    act.wait_ge(acc_done, (KT - 1) * i + t - 2)
                act.activation(sqb[:, t % 2, :] if t else rstd[:], y[:, t, :], ACT.Square).then_inc(acc_sq, 1)

            def root(summed, after):
                act.preload_act_table_set(LN_EXP)
                act.wait_ge(*summed)
                if after:
                    act.wait_ge(*after)
                own.link(act.activation(rstd[:], ps[:, 3, :], ACT.Ln, bias=pr[:, EPS_RMS:EPS_RMS + 1], scale=1.0 / D))
                act.activation(rstd[:], rstd[:], ACT.Exp, scale=-0.5).then_inc(rs_ready, 1)

            def x_round(b, used=None):
                for kt in range(KT):
                    act.wait_ge(xn_ready, b + kt + 1)
                    if used is not None:
                        act.wait_ge(*((x_used, (KT - 1) * (used - 1) + kt + 1) if kt < KT - 1 else (w_used, used)))
                    act.activation(xh[:, kt, :], xs(kt), ACT.Copy).then_inc(xhi_ready, 1)

            act.wait_ge(c_in, 32)
            w_round(0, 0, None)
            squares(0, lambda kt: h[:, kt, 1:T + 1])
            root((sq_used, KT), None)
            x_round(0)
            for n in range(N_LORA + 3):
                w_round(n + 1, 0, (w_used, n) if n >= 1 else None)
                if n in MIX_LAST:
                    x_round(KT * (MIX_LAST.index(n) + 1), n + 1)
                act.wait_ge(w_used, n + 1)
                if n < N_LORA:
                    if n >= 2:
                        act.wait_ge(o_dma[n % 2], 16 * (n // 2))
                    act.activation(ost[:, n % 2, :], ps[:, n % 4, :], ACT.Copy).then_inc(o_full[n % 2], 1)
                else:
                    f = (ACT.Tanh, ACT.Copy, ACT.Sigmoid)[n - N_LORA]
                    act.activation(lor[:, n - N_LORA, :], ps[:, n % 4, :], f).then_inc(lo_ready, 1)

            def evac(s, g, k, a):
                if s not in (2, 3, 4, 7, 8, 10, 12):
                    return
                b = bank(inv_bank(s, g))
                act.wait_ge(st_full[s], 2 * k + g + 1)
                if s == 2:
                    if not (type(k) is int and k < 2):
                        act.wait_ge(y_tile, 2 * k - 3 + g)
                    dst, n = tok[a][g][:].rearrange("p a b -> p (a b)"), 3 * P
                elif s == 3:
                    dst, n = Dn[g][:].rearrange("p a b -> p (a b)"), 2 * P
                elif s == 4:
                    dst, n = D2[g][:].rearrange("p a b c -> p (a b c)"), 4 * P
                elif s == 7:
                    dst, n = TT[a][g][:, 1].rearrange("p a b -> p (a b)"), 2 * P
                else:
                    dst, n = Wm[g][:].rearrange("p a b -> p (a b)"), 2 * P
                act.activation(dst, b[:, 0:n], ACT.Copy).then_inc(st_evac[s], 1)

            def scan(f, hp, u, first):
                c, ph = f // 3, f % 3
                g, p = c // 2, c % 2
                n, k = 16 * hp + 4 * u + c, 4 * hp + u
                tp = slice(C * p, C * p + C)
                b = bank(B_SC)
                if ph == 0:
                    act.wait_ge(rhs_full, n + 1)
                    act.activation(rhs_sb[tp, :], b[tp, 0:P], ACT.Copy).then_inc(rhs_sbr, 1)
                elif ph == 1:
                    act.wait_ge(sa_full, n + 1)
                    if p == 0 and not (type(k) is int and k == 0):
                        act.wait_ge(y_tile, 2 * k + g - 1)
                    act.activation(SA[g][tp, :], b[tp, P:2 * P], ACT.Copy).then_inc(sa_sbr, 1)

            def prep(e, r, hp, pc):
                if e == 0:
                    if pc == 0:
                        act.wait_ge(pp_r, hp + 1)
                    if not (type(r) is int and r == 0):
                        act.wait_ge(prep_done, r)
                        act.wait_ge(bon_f, r)
                    act.wait_ge(zw_f, r + 1)
                    act.activation(T0, bank(B_AUX0), ACT.Sigmoid, bias=pcp[:, 0:1]).then_inc(zw_e, 1)
                    act.wait_ge(za_f, r + 1)
                    act.activation(T5, bank(B_AUX1), ACT.Sigmoid, bias=pcp[:, 1:2]).then_inc(za_e, 1)
                    act.preload_act_table_set(LN_EXP)
                    act.wait_ge(k_in, 16 * (r + 1))
                    act.activation(T6, kin[:], ACT.Square, scale=pcp[:, 2:3]).then_inc(ksq_r, 1)
                elif e == 1:
                    act.wait_ge(s_r, r + 1)
                    act.activation(T2, T1, ACT.Exp, scale=-DECAY)
                    act.activation(T3, T1, ACT.Exp, scale=DECAY)
                    act.wait_ge(sm_r, r + 1)
                    act.activation(T4, T0, ACT.Exp, scale=-DECAY).then_inc(P_r, 1)
                else:
                    act.wait_ge(ss_e, r + 1)
                    own.link(act.activation(T6, T6, ACT.Ln, scale=float(2 ** LN_SHIFT)))
                    act.activation(T6, T6, ACT.Exp, scale=-0.5, bias=pr[:, KSH:KSH + 1]).then_inc(rinv_r, 1)

            def post(e, p, hp, pc):
                if e == 0:
                    act.wait_ge(y_tile, 4 * (p + 1))
                    act.activation(ysb[:], bank(B_Y), ACT.Copy).then_inc(y_sb, 1)
                elif e == 1:
                    act.wait_ge(yc_r, p + 1)
                    act.activation(psq, ysb[:], ACT.Square).then_inc(ysq_r, 1)
                elif e == 2:
                    act.wait_ge(var_f, p + 1)
                    own.link(act.activation(psq, bank(B_AUX0), ACT.Ln, bias=pr[:, EPS_GN:EPS_GN + 1], scale=1.0 / HD))
                    act.activation(psq, psq, ACT.Exp, scale=-0.5).then_inc(var_e, 1)
                else:
                    act.wait_ge(z_r, p + 1)
                    act.activation(xh[:, hp, pc * HALF:(pc + 1) * HALF], zt, ACT.Copy).then_inc(zhi_r, 1)

            def rounds(inv, sc, busy):
                for s in range(14):
                    if busy:
                        pp, qq = busy
                        if qq and s == 0:
                            post(0, *qq)
                    if inv:
                        evac(s, 0, inv[0], inv[1] % 2)
                        evac(s, 1, inv[0], inv[1] % 2)
                    if sc and 1 <= s <= 12:
                        scan(s - 1, *sc)
                    if busy:
                        if pp and s == 0:
                            prep(0, *pp)
                        if pp and s == 2:
                            prep(1, *pp)
                        if qq and s == 4:
                            post(1, *qq)
                        if pp and s == 5:
                            prep(2, *pp)
                        if qq and s == 7:
                            post(2, *qq)
                        if qq and s == 10:
                            post(3, *qq)

            def body(hp, first, last):
                rounds((4 * hp + 1, 1), (hp, 0, first), ((2 * hp + 1, hp, 1), None if first else (2 * hp - 1, hp - 1, 1)))
                rounds((4 * hp + 2, 2), (hp, 1, first), None)
                rounds((4 * hp + 3, 3), (hp, 2, first), (None if last else (2 * hp + 2, hp + 1, 0), (2 * hp, hp, 0)))
                rounds(None if last else (4 * hp + 4, 0), (hp, 3, first), None)

            for e in range(3):
                prep(e, 0, 0, 0)
            rounds((0, 0), None, None)
            body(0, True, False)
            n, per = own.n, 4
            with act.Fori(1, NHP - 1) as hp:
                own.r = per * hp - per
                body(hp, False, False)
            assert own.n == n + per
            own.n, own.r = n + per * (NHP - 2), 0
            body(NHP - 1, False, True)
            for e in range(4):
                post(e, 15, NHP - 1, 1)

            def project(i, n0, m0, used, bias):
                for t in range(8):
                    w_round(n0 + t + 1, 0, (w_used, used + t))
                    act.wait_ge(w_used, used + t + 1)
                    if bias is None:
                        ins = act.activation(y[:, t, :], ps[:, t % 4, :], ACT.Copy)
                    else:
                        ins = act.activation(y[:, t, :], ps[:, t % 4, :], ACT.Identity, bias=pr[:, bias + t:bias + t + 1])
                    ins.then_inc(mm_evac, 1)
                    square_y(i, t, (mm_evac, m0 + t + 1))

            project(0, N_WO, 0, N_WO, None)
            root((sum_full, 1), None)
            squares(1, lambda kt: x[:, kt, :])
            root((sq_used, 2 * KT), (scaled, KT))
            x_round(6 * KT)

            def ffn(L, n0, used):
                s0 = n0 % 2

                def silu(g, i, count):
                    act.wait_ge(w_used, count)
                    if not (type(g) is int and g == 0):
                        act.wait_ge(up_mul, 2 * g + i - 1)
                    act.activation(sqb[:, i, :], ps[:, 2 * i, :], ACT.Silu).then_inc(sg_ready, 1)

                def hidden(g, i, buf):
                    act.wait_ge(up_mul, 2 * g + i + 1)
                    act.activation(hidh[:, buf, i, :], tmp[:, i, :], ACT.Copy).then_inc(hid_hi, 1)

                G = FG * L
                w_round(n0 + 1, 0, (w_used, used))
                silu(G, 0, used + 1)
                w_round(n0 + 2, 0, (w_used, used + 1))
                w_round(n0 + 3, 0, (w_used, used + 2))
                hidden(G, 0, 0)
                silu(G, 1, used + 3)
                w_round(n0 + 4, 0, (w_used, used + 3))
                hidden(G, 1, 0)

                def group(g, n, r, u, prev, buf):
                    w_round(n + 1, r, prev)
                    silu(g, 0, u + 1)
                    w_round(n + 2, r, (w_used, u + 1))
                    w_round(n + 3, r, (w_used, u + 2))
                    hidden(g, 0, buf)
                    silu(g, 1, u + 3)
                    w_round(n + 4, r, (w_used, u + 3))
                    w_round(n + 5, r, (w_used, u + 4))
                    hidden(g, 1, buf)
                    w_round(n + 6, r, (dn_full, 8 * (g - 1) + 4))

                group(G + 1, n0 + 4, 0, used + 4, (w_used, used + 4), 1)
                with act.Fori(0, (FG - 3) // 2) as i:
                    for v in range(2):
                        g = 2 * i + G + 2 + v
                        group(g, n0 + 10 + 6 * v, 12 * i, 8 * i + used + 8 + 4 * v, (dn_full, 8 * (g - 2) + 8), v)
                g = G + FG - 1
                group(g, n0 + 4 + 6 * (FG - 2), 0, used + 4 * (FG - 1), (dn_full, 8 * (g - 2) + 8), 0)
                w_round(n0 + 6 * FG - 1, 0, (dn_full, 8 * (g - 1) + 8))
                for m in range(8):
                    if m == 4 and L == 0:
                        w_round(n0 + 6 * FG, 0, (dn_full, 8 * g + 4))
                    square_y(2 * L + 1, m, (dn_evac, 8 * g + m + 1))

            U0 = N_F0 + 4 * FG
            ffn(0, N_F0, N_F0)
            root((sum_full, 2), None)
            squares(2, lambda kt: x[:, kt, :])
            root((sq_used, 3 * KT), (scaled, 2 * KT))
            x_round(7 * KT)

            def heads_in(l):
                w_round(N_QKV + l + 1, 0, (w_used, U0 + l) if l >= 1 else (dn_full, 8 * FG))
                act.wait_ge(w_used, U0 + l + 1)
                if l >= 2:
                    act.wait_ge(rot_r, l - 1)
                act.activation(tmp[:, l % 2, :], ps[:, l % 2, :], ACT.Identity,
                               bias=pr[:, BQKV + l:BQKV + l + 1]).then_inc(mm_evac, 1)

            def v_out(l):
                act.wait_ge(rot_f, l + 1)
                kv = 2 * (l - 10)
                act.activation(vt[:, 1:NB + 1, kv:kv + 2, :].rearrange("p n a b -> p n (a b)"),
                               ps[:, 2 + l % 2, :].rearrange("p (n c) -> p n c", c=P), ACT.Copy).then_inc(rot_r, 1)

            for l in range(12):
                heads_in(l)
                if l == 11:
                    v_out(10)
            v_out(11)
            act.wait_ge(kd_r, 2)
            for i in range(2):
                act.activation(kd[HD:P, 2 * i, P:], kd[0:HD, 2 * i, P:], ACT.Copy)
                ins = act.activation(kd[0:HD, 2 * i + 1, P:], kd[HD:P, 2 * i + 1, P:], ACT.Copy)
            ins.then_inc(kd_r, 1)

            def soft(it):
                act.wait_ge(nm_r, it + 1)
                b = it % 3
                act.activation(st[:, b, 3, :], st[:, b, 3, :], ACT.Exp)
                for i in range(4):
                    ins = act.activation(sc[:, b, i * 2 * P:(i + 1) * 2 * P], sc[:, b, i * 2 * P:(i + 1) * 2 * P], ACT.Exp,
                                         bias=st[:, b, 1, i:i + 1], accum_out=st[:, b, 2, i:i + 1])
                ins.then_inc(p_r, 1)

            def turned(it):
                act.wait_ge(pt_f, it + 1)
                if it >= 1:
                    act.wait_ge(o_f, it)
                act.activation(pT[:].rearrange("p a b -> p (a b)"), ps[:, 2, :], ACT.Copy).then_inc(pt_r, 1)

            def o_hi(it):
                n, kv = it // NKV, it % NKV
                act.wait_ge(o_f, it + 1)
                act.activation(xh[:, 2 * kv:2 * kv + 2, n * P:(n + 1) * P],
                               bank(6 + it % 2)[:, 0:2 * P].rearrange("p (a b) -> p a b", b=P), ACT.Copy).then_inc(o_r, 1)

            IT = NB * NKV
            act.preload_act_table_set(LN_EXP)
            soft(0)
            soft(1)
            for it in range(IT):
                if it >= 1:
                    o_hi(it - 1)
                turned(it)
                if it + 2 < IT:
                    soft(it + 2)
            o_hi(IT - 1)
            act.wait_ge(oz_r, IT)
            project(2, N_AO, 20, U0 + 12, BO)
            root((sum_full, 3), None)
            squares(3, lambda kt: x[:, kt, :])
            root((sq_used, 4 * KT), (scaled, 3 * KT))
            x_round(8 * KT)
            ffn(1, N_F1, U0 + 20)
            root((sum_full, 4), None)

        @block.vector
        def _(dve):
            own = Own(dve, dve_own)
            stt = dve.scalar_tensor_tensor

            def w_lo(n, ws):
                dve.wait_ge(w_hi, n + 1)
                dve.tensor_tensor(wl[:, ws, :], wst[:, ws, :], wh[:, ws, :].bitcast(F32), ALU.subtract).then_inc(w_split, 1)

            def x_split(b, make):
                def lo(kt):
                    dve.wait_ge(xhi_ready, b + kt + 1)
                    dve.tensor_tensor(xl[:, kt, :], xs(kt), xh[:, kt, :].bitcast(F32), ALU.subtract).then_inc(x_ready, 1)
                for kt in range(KT):
                    if b + kt >= 4:
                        wait_x(dve, b + kt - 4)
                    make(kt).then_inc(xn_ready, 1)
                    if kt >= 2 and kt % 2 == 0:
                        lo(kt - 2)
                lo(KT - 2)

            def g_col(c, kt):
                return pr[:, c + kt:c + kt + 1]

            def normed(gc):
                def make(kt):
                    return stt(out=xs(kt), in0=x[:, kt, :], scalar=g_col(gc, kt), in1=rstd[:], op0=ALU.mult, op1=ALU.mult)
                return make

            def add_square(i, t):
                dve.wait_ge(acc_sq, KT * i + t + 1)
                if t > 1:
                    dve.wait_ge(acc_done, (KT - 1) * i + t - 1)
                dve.tensor_tensor(rstd[:], rstd[:], sqb[:, t % 2, :], ALU.add).then_inc(acc_done, 1)

            def residual(i, gc, ready):
                dve.wait_ge(rs_ready, 2 * i + 2)
                if ready:
                    dve.wait_ge(*ready)
                for j in range(KT // 2):
                    for kt in (2 * j + 1, 2 * j):
                        stt(out=y[:, kt, :], in0=y[:, kt, :], scalar=g_col(gc, kt), in1=rstd[:], op0=ALU.mult, op1=ALU.mult).then_inc(scaled, 1)
                    dve.wait_ge(scaled, KT * i + 2 * j + 2)
                    dve.tensor_tensor(x[:, 2 * j, :], x[:, 2 * j, :], y[:, 2 * j, :], ALU.add).then_inc(res_done, 1)

            w_lo(0, 0)
            dve.wait_ge(rs_ready, 1)
            dve.wait_ge(pool_own, 1)

            def first_norm(kt):
                stt(out=h[:, kt, 1:T + 1], in0=h[:, kt, 1:T + 1], scalar=g_col(G0, kt), in1=rstd[:],
                    op0=ALU.mult, op1=ALU.mult).then_inc(h_ready, 1)
                if kt % 2 == 0:
                    dve.wait_ge(h_ready, kt + 1)
                    dve.tensor_tensor(xx[:, kt, :], h[:, kt, 0:T], h[:, kt, 1:T + 1], ALU.subtract).then_inc(xx_ready, 1)

            def mixed(j):
                def make(kt):
                    if j == 0 and kt + 2 < KT:
                        first_norm(kt + 2)
                    if j == 0:
                        dve.wait_ge(xx_odd if kt % 2 else xx_ready, kt // 2 + 1)
                        dve.wait_ge(h_ready, kt + 1)
                    return stt(out=xs(kt), in0=xx[:, kt, :], scalar=g_col(MIX + KT * j, kt), in1=h[:, kt, 1:T + 1],
                               op0=ALU.mult, op1=ALU.add)
                return make

            first_norm(0)
            first_norm(1)
            x_split(0, mixed(0))
            for n in range(N_LORA + 3):
                w_lo(n + 1, (n + 1) % 2)
                if n in MIX_LAST:
                    j = MIX_LAST.index(n) + 1
                    x_split(KT * j, mixed(j))

            def evac(s, g, k, a):
                b = bank(inv_bank(s, g))
                tt0 = TT[a][g][:, 0].rearrange("p a b -> p (a b)")
                if s < 2:
                    dve.wait_ge(st_full[s], 2 * k + g + 1)
                    if s == 0 and not (type(k) is int and k < 2):
                        dve.wait_ge(y_tile, 2 * k - 3 + g)
                    dve.tensor_tensor(Sm[a][g][:, s].rearrange("p (i j) c -> p i (j c)", i=2),
                                      b.rearrange("p (i c) -> p i c", i=2),
                                      m_si.unsqueeze(1).to_broadcast([P, 2, 2 * P]), ALU.mult).then_inc(st_evac[s], 1)
                    if s == 1:
                        dve.wait_ge(st_evac[0], 2 * k + g + 1)
                        dve.wait_ge(st_evac[1], 2 * k + g + 1)
                        dve.tensor_tensor(Dt[g][:], Sm[a][g][:, :, 0, :], mu8.unsqueeze(1).to_broadcast([P, 2, P]),
                                          ALU.mult).then_inc(dt_ready, 1)
                        dve.wait_ge(dt_ready, 2 * k + g + 1)
                        dve.tensor_tensor(TT[a][g][:, 0], Dt[g][:], ident.unsqueeze(1).to_broadcast([P, 2, P]),
                                          ALU.add).then_inc(x1_ready, 1)
                elif s == 5:
                    dve.wait_ge(st_full[5], 2 * k + g + 1)
                    dve.tensor_tensor(tt0, tt0, b[:, 0:2 * P], ALU.add)
                    dve.tensor_copy(Dn[g][:].rearrange("p a b -> p (a b)"), b[:, 2 * P:4 * P]).then_inc(st_evac[5], 1)
                elif s in (6, 13):
                    dve.wait_ge(st_full[s], 2 * k + g + 1)
                    dve.tensor_tensor(tt0, tt0, b[:, 0:2 * P], ALU.add).then_inc(st_evac[s], 1)
                elif s in (9, 11):
                    dve.wait_ge(st_full[s], 2 * k + g + 1)
                    tt = TT[a][g][:].rearrange("p a b c -> p (a b c)")
                    dve.tensor_tensor(tt, tt, b, ALU.add).then_inc(st_evac[s], 1)

            def scan(f, hp, u, first):
                c, ph = f // 3, f % 3
                a, pc = u % 2, u // 2
                n = 16 * hp + 4 * u + c
                pe_col = pend[:, pc, 4 * a + c:4 * a + c + 1]
                if ph == 0:
                    if u == 0 and c == 0:
                        if not first:
                            dve.wait_ge(ds_full, 16 * hp)
                            dve.memset(S[:], 0.0).then_inc(s_ready, 1)
                        else:
                            dve.memset(rhs_sb[:], 0.0)
                            dve.memset(S[:], 0.0).then_inc(s_ready, 1)
                    dve.wait_ge(s_ready, n + 1)
                    dve.tensor_scalar(SP[:], S[:], pe_col, None, ALU.mult).then_inc(sp_ready, 1)
                elif ph == 2 and not (u == 3 and c == 3):
                    dve.wait_ge(ds_full, n + 1)
                    dve.wait_ge(sp_ready, n + 1)
                    b = bank(B_SC)
                    for i in range(2):
                        hh = slice(HD * i, HD * i + HD)
                        ins = stt(out=S[hh, hh], in0=b[hh, 2 * P + HD * i:2 * P + HD * i + HD], scalar=pe_col[hh, :], in1=SP[hh, hh],
                                  op0=ALU.mult, op1=ALU.add)
                    ins.then_inc(s_ready, 1)

            def prep(e, r, hp, pc, after):
                if e == 0:
                    if pc == 0:
                        src = pr[:, W0:W0 + 40].rearrange("p (v h) -> p v h", h=NHP)[:, :, hp:hp + 1] if type(hp) is int else \
                            pr[:, W0:W0 + 40].rearrange("p (v h) -> p v h", h=NHP)[:, :, bass.ds(hp, 1)]
                        own.link(dve.tensor_copy(pcp[:, 0:5].unsqueeze(2), src))
                        dve.tensor_scalar(pcp[:, 5:6], pcp[:, 3:4], -1.0, 1.0, ALU.mult, ALU.add).then_inc(pp_r, 1)
                elif e == 1:
                    dve.wait_ge(zw_e, r + 1)
                    dve.tensor_tensor_scan(T1, rst, T0, 0.0, ALU.mult, ALU.add).then_inc(s_r, 1)
                    dve.wait_ge(s_r, r + 1)
                    dve.tensor_tensor(T0, T1, T0, ALU.subtract).then_inc(sm_r, 1)
                elif e == 2:
                    dve.wait_ge(ss_f, r + 1)
                    dve.tensor_scalar(T6, bank(B_AUX1), 1e-24, None, ALU.max).then_inc(ss_e, 1)
                elif e == 3:
                    dve.wait_ge(P_r, r + 1)
                    dve.wait_ge(rinv_r, r + 1)
                    dve.wait_ge(r_in, 16 * (r + 1))
                    dve.wait_ge(za_e, r + 1)
                    if after is not None:
                        dve.wait_ge(y_tile, after)
                    own.link(stt(out=T7, in0=kin[:], scalar=pcp[:, 2:3], in1=T6, op0=ALU.mult, op1=ALU.mult))
                    stt(out=At[:, pc, :], in0=T7, scalar=-1.0, in1=T4, op0=ALU.mult, op1=ALU.mult)
                    own.link(dve.tensor_tensor(T7, T7, T5, ALU.mult))
                    dve.tensor_tensor(Bt[:, pc, :], T7, T3, ALU.mult)
                    own.link(dve.tensor_scalar(T5, T5, pcp[:, 3:4], pcp[:, 5:6], ALU.mult, ALU.add))
                    own.link(dve.tensor_tensor(T5, T5, kin[:], ALU.mult))
                    dve.tensor_tensor(Kt[:, pc, :], T5, T3, ALU.mult)
                    dve.tensor_tensor(Rt[:, pc, :], rin[:], T2, ALU.mult)
                    stt(out=T6, in0=rin[:], scalar=pcp[:, 4:5], in1=T5, op0=ALU.mult, op1=ALU.mult).then_inc(rk_r, 1)
                    dve.tensor_copy(pend[:, pc, :], T2.rearrange("p (n c) -> p n c", c=C)[:, :, C - 1]).then_inc(prep_done, 1)
                else:
                    dve.wait_ge(bon_f, r + 1)
                    dve.wait_ge(v_in[pc], 16 * (hp + 1))
                    dve.tensor_tensor(bon[:, pc, :], bank(B_AUX0), vin[:, pc, :], ALU.mult).then_inc(bon_e, 1)

            def post(e, p, hp, pc):
                if e == 0:
                    if pc == 0:
                        src = pr[:, LNW:LNW + 16].rearrange("p (v h) -> p v h", h=NHP)
                        src = src[:, :, hp:hp + 1] if type(hp) is int else src[:, :, bass.ds(hp, 1)]
                        dve.tensor_copy(pcq[:].unsqueeze(2), src).then_inc(pq_r, 1)
                    dve.wait_ge(mean_f, p + 1)
                    stt(out=ysb[:], in0=bank(B_AUX0), scalar=-1.0 / HD, in1=ysb[:], op0=ALU.mult, op1=ALU.add).then_inc(yc_r, 1)
                elif e == 1:
                    dve.wait_ge(var_e, p + 1)
                    dve.wait_ge(g_f, p + 1)
                    dve.wait_ge(pq_r, hp + 1)
                    own.link(stt(out=zt, in0=ysb[:], scalar=pcq[:, 0:1], in1=psq, op0=ALU.mult, op1=ALU.mult))
                    own.link(stt(out=zt, in0=zt, scalar=pcq[:, 1:2], in1=bon[:, pc, :], op0=ALU.add, op1=ALU.add))
                    dve.tensor_tensor(zt, zt, bank(B_AUX1), ALU.mult).then_inc(z_r, 1)
                else:
                    dve.wait_ge(zhi_r, p + 1)
                    cols = slice(pc * HALF, pc * HALF + HALF)
                    dve.tensor_tensor(xl[:, hp, cols], zt, xh[:, hp, cols].bitcast(F32), ALU.subtract).then_inc(z_ready, 1)

            def rounds(inv, sc, busy):
                for s in range(14):
                    if inv:
                        evac(s, 0, inv[0], inv[1] % 2)
                        evac(s, 1, inv[0], inv[1] % 2)
                    if sc and 1 <= s <= 12:
                        scan(s - 1, *sc)
                    if busy:
                        pp, qq = busy
                        if pp and s == 0:
                            prep(0, *pp)
                        if pp and s == 1:
                            prep(1, *pp)
                        if qq and s == 2:
                            post(0, *qq)
                        if pp and s == 4:
                            prep(2, *pp)
                        if pp and s == 6:
                            prep(3, *pp)
                        if qq and s == 9:
                            post(1, *qq)
                        if pp and s == 11:
                            prep(4, *pp)
                        if qq and s == 12:
                            post(2, *qq)

            own.n = own.r = 0
            dve.wait_ge(a_in, 16)
            dve.wait_ge(lo_ready, 3)
            for e in range(5):
                prep(e, 0, 0, 0, None)
            rounds((0, 0), None, None)

            def body(hp, first, last):
                rounds((4 * hp + 1, 1), (hp, 0, first),
                       ((2 * hp + 1, hp, 1, None if first else 8 * hp), None if first else (2 * hp - 1, hp - 1, 1)))
                rounds((4 * hp + 2, 2), (hp, 1, first), None)
                rounds((4 * hp + 3, 3), (hp, 2, first),
                       (None if last else (2 * hp + 2, hp + 1, 0, 8 * hp + 4), (2 * hp, hp, 0)))
                rounds(None if last else (4 * hp + 4, 0), (hp, 3, first), None)

            body(0, True, False)
            n = own.n
            per = 13
            with dve.Fori(1, NHP - 1) as hp:
                own.r = per * hp - per
                body(hp, False, False)
            assert own.n == n + per, own.n - n
            own.n, own.r = n + per * (NHP - 2), 0
            body(NHP - 1, False, True)
            for e in range(3):
                post(e, 15, NHP - 1, 1)

            for t in range(8):
                w_lo(N_WO + t + 1, (N_WO + t + 1) % 2)
                if t >= 1:
                    add_square(0, t)
            residual(0, G0 + KT, (x_in, 16))
            dve.wait_ge(rs_ready, 3)
            x_split(6 * KT, normed(G0 + 2 * KT))

            def ffn(L, n0):
                s0 = n0 % 2
                G = FG * L

                def hidden(g, i):
                    dve.wait_ge(sg_ready, 2 * g + i + 1)
                    dve.wait_ge(w_used, used(g, i))
                    dve.tensor_tensor(tmp[:, i, :], sqb[:, i, :], ps[:, 2 * i + 1, :], ALU.mult).then_inc(up_mul, 1)

                def hidden_lo(g, i, buf):
                    dve.wait_ge(hid_hi, 2 * g + i + 1)
                    dve.tensor_tensor(hidl[:, buf, i, :], tmp[:, i, :], hidh[:, buf, i, :].bitcast(F32),
                                      ALU.subtract).then_inc(hid_ready, 1)

                def used(g, i):
                    return (N_F0 if L == 0 else N_F0 + 4 * FG + 20) + 4 * (g - G) + 2 * i + 2

                def add(g, m):
                    dve.wait_ge(dn_full, 8 * g + m + 1)
                    dve.tensor_tensor(y[:, m, :], y[:, m, :], ps[:, m % 4, :], ALU.add).then_inc(dn_evac, 1)

                for t in (1, 2, 3):
                    w_lo(n0 + t, (s0 + t) % 2)
                hidden(G, 0)
                hidden_lo(G, 0, 0)
                w_lo(n0 + 4, s0)
                hidden(G, 1)
                hidden_lo(G, 1, 0)
                dve.wait_ge(y_zero, L + 1)

                def group(g, n, buf):
                    for t in (1, 2, 3):
                        w_lo(n + t, (s0 + t) % 2)
                    hidden(g, 0)
                    hidden_lo(g, 0, buf)
                    w_lo(n + 4, s0)
                    w_lo(n + 5, 1 - s0)
                    hidden(g, 1)
                    hidden_lo(g, 1, buf)
                    for m in range(4):
                        add(g - 1, m)
                    w_lo(n + 6, s0)
                    for m in range(4, 8):
                        add(g - 1, m)

                group(G + 1, n0 + 4, 1)
                with dve.Fori(0, (FG - 3) // 2) as i:
                    for v in range(2):
                        group(2 * i + G + 2 + v, 12 * i + n0 + 10 + 6 * v, v)
                group(G + FG - 1, n0 + 4 + 6 * (FG - 2), 0)
                w_lo(n0 + 6 * FG - 1, 1 - s0)
                for m in range(8):
                    if m == 4 and L == 0:
                        w_lo(n0 + 6 * FG, s0)
                    add(G + FG - 1, m)
                    if m >= 2:
                        add_square(2 * L + 1, m - 1)
                add_square(2 * L + 1, 7)

            ffn(0, N_F0)
            residual(1, G0 + 3 * KT, None)
            dve.wait_ge(rs_ready, 5)
            x_split(7 * KT, normed(G0 + 4 * KT))

            def rotate(l):
                raw, rot, b = tmp[:, l % 2, :], ps[:, 2 + l % 2, :], sqb[:, l % 2, :]
                dve.wait_ge(mm_evac, 8 + l + 1)
                dve.wait_ge(rot_f, l + 1)
                own.link(dve.tensor_tensor(b, rot, sinT, ALU.mult))
                own.link(dve.tensor_tensor(raw, raw, cosT, ALU.mult))
                if l < 8:
                    own.link(dve.tensor_tensor(raw, raw, b, ALU.add))
                    dve.tensor_scalar(q[:, l, :], raw, SCALE, None, ALU.mult).then_inc(rot_r, 1)
                else:
                    kv = 2 * (l - 8)
                    dve.tensor_tensor(kd[0:HD, kv, P:], raw[0:HD, :], b[0:HD, :], ALU.add).then_inc(kd_r, 1)
                    dve.tensor_tensor(kd[HD:P, kv + 1, P:], raw[HD:P, :], b[HD:P, :], ALU.add).then_inc(rot_r, 1)

            dve.wait_ge(a_in, 32)
            dve.wait_ge(pad_r, 1)
            for l in range(12):
                w_lo(N_QKV + l + 1, (N_QKV + l + 1) % 2)
                if 1 <= l <= 10:
                    rotate(l - 1)

            def masked(it):
                n, kv = it // NKV, it % NKV
                b = it % 3
                dve.wait_ge(s_f, it + 1)
                if it >= 3:
                    dve.wait_ge(pt_f, it - 2)
                s3 = sc[:, b, :].rearrange("p (i c) -> p i c", c=2 * P)
                dve.tensor_tensor(s3, ps[:, it % 2, :].rearrange("p (i c) -> p i c", c=2 * P),
                                  msk[min(n, 1)].unsqueeze(1).to_broadcast([P, 4, 2 * P]), ALU.add).then_inc(sm_m, 1)
                dve.wait_ge(sm_m, it + 1)
                own.link(dve.tensor_reduce(st[:, b, 0, :], s3, AX_X, ALU.max))
                sk = pr[:, SINK + 4 * kv:SINK + 4 * kv + 4]
                own.link(dve.tensor_tensor(st[:, b, 0, :], st[:, b, 0, :], sk, ALU.max))
                own.link(dve.tensor_scalar(st[:, b, 1, :], st[:, b, 0, :], -1.0, None, ALU.mult))
                dve.tensor_tensor(st[:, b, 3, :], st[:, b, 1, :], sk, ALU.add).then_inc(nm_r, 1)

            def denominators(it):
                b = it % 3
                dve.wait_ge(p_r, it + 1)
                own.link(dve.tensor_tensor(st[:, b, 4, :], st[:, b, 2, :], st[:, b, 3, :], ALU.add))
                dve.reciprocal(st[:, b, 5, :], st[:, b, 4, :]).then_inc(den_r, 1)

            def o_lo(it):
                n, kv = it // NKV, it % NKV
                dve.wait_ge(o_r, it + 1)
                dst = slice(n * P, (n + 1) * P)
                dve.tensor_tensor(xl[:, 2 * kv:2 * kv + 2, dst], bank(6 + it % 2)[:, 0:2 * P].rearrange("p (a b) -> p a b", b=P),
                                  xh[:, 2 * kv:2 * kv + 2, dst].bitcast(F32), ALU.subtract).then_inc(oz_r, 1)

            IT = NB * NKV
            masked(0)
            masked(1)
            denominators(0)
            for it in range(IT):
                if it + 1 < IT:
                    denominators(it + 1)
                if it + 2 < IT:
                    masked(it + 2)
                if it >= 1:
                    o_lo(it - 1)
            o_lo(IT - 1)
            for t in range(8):
                w_lo(N_AO + t + 1, (N_AO + t + 1) % 2)
                if t >= 1:
                    add_square(2, t)
            residual(2, G0 + 5 * KT, (x_in, 32))
            dve.wait_ge(rs_ready, 7)
            x_split(8 * KT, normed(G0 + 6 * KT))
            ffn(1, N_F1)
            residual(3, G0 + 7 * KT, None)


def lay_out(i):
    f = {k: np.asarray(v) for k, v in i.items()}

    def tiles(w):
        k, n = w.shape
        return w.reshape(k // P, P, n // P, P).transpose(2, 1, 0, 3).reshape(n // P, P, -1)

    def wide(w):
        return np.concatenate([w, np.zeros((w.shape[0], P - w.shape[1]), w.dtype)], 1)

    def ffn(L):
        gu, dn = tiles(f["ffn_w_gate_up"][L]), f["ffn_w_down"][L]
        dn = dn.reshape(FG, 2, P, 2, HALF).transpose(0, 3, 2, 1, 4).reshape(FG, 2, P, T)
        seq = []
        for g in range(FG + 1):
            if g < FG:
                for t in (2 * g, 2 * g + 1):
                    seq += [gu[t], gu[D_FF // P + t]]
            if g >= 1:
                seq += [dn[g - 1, 0], dn[g - 1, 1]]
        return np.stack(seq)

    wt = np.concatenate([
        tiles(f["rwkv_w_rkv"][0, 0]), tiles(f["rwkv_w_rkv"][0, 1]), tiles(f["rwkv_w_rkv"][0, 2]),
        tiles(wide(f["rwkv_w1"][0])), tiles(wide(f["rwkv_a1"][0])), tiles(f["rwkv_g1"][0]),
        tiles(f["rwkv_w_o"][0]), ffn(0), tiles(f["attn_w_qkv"][0]), tiles(f["attn_w_o"][0]), ffn(1)])

    def cols(v):
        return v.reshape(-1, P).T

    sinks = f["attn_sinks"][0].reshape(NKV, 2, 2).transpose(0, 2, 1).reshape(1, -1)
    one = np.ones((P, 1), np.float32)
    par = np.concatenate([
        cols(f["norm_g"]), cols(f["rwkv_x_mix"]), cols(f["rwkv_w0"]), cols(f["rwkv_a0"]), cols(f["rwkv_k_k"]),
        cols(f["rwkv_k_a"]), cols(f["rwkv_r_k"]), cols(f["rwkv_lnx_w"]), cols(f["rwkv_lnx_b"]),
        cols(f["attn_b_qkv"]), cols(f["attn_b_o"]), np.repeat(sinks, P, 0),
        np.full((P, 1), RMS_EPS, np.float32), np.full((P, 1), GN_EPS, np.float32),
        np.full((P, 1), 0.5 * LN_SHIFT * np.log(2.0), np.float32)], 1)

    def tall(w):
        w = np.concatenate([w, np.zeros((P - w.shape[0], D), w.dtype)], 0)
        return w.reshape(P, NHP, P).transpose(1, 0, 2)

    lora2 = np.stack([tall(f["rwkv_w2"][0]), tall(f["rwkv_a2"][0]), tall(f["rwkv_g2"][0])], 2)
    xT = f["x"][0].T.reshape(KT, P, T).transpose(1, 0, 2)
    base, rw, at = shape_constants()
    return [np.ascontiguousarray(a) for a in (xT, wt, par, lora2, base, rw, at)]


def kernel(**inputs):
    import concourse.bacc as bacc
    from concourse.bass_utils import run_bass_kernel_spmd

    nc = bacc.Bacc("TRN2", target_bir_lowering=False, num_devices=1)
    names = ("xT", "wt", "par", "lora2", "cbase", "crw", "cat")
    arrays = dict(zip(names, lay_out(inputs)))
    aps = [nc.dram_tensor(n, arrays[n].shape, F32, kind="ExternalInput").ap() for n in names]
    out = nc.dram_tensor("out", [P, KT, T], F32, kind="ExternalOutput").ap()
    build_program(nc, *aps, out)
    r = run_bass_kernel_spmd(nc, [arrays], core_ids=[0])
    got = r.results[0]["out"]
    return np.ascontiguousarray(got.transpose(1, 0, 2).reshape(1, D, T).transpose(0, 2, 1))
```

```python
from contextlib import ExitStack

import numpy as np

import concourse.bass as bass
from concourse import mybir

F32 = mybir.dt.float32
F32R = mybir.dt.float32r
ALU = mybir.AluOpType
ACT = mybir.ActivationFunctionType
AX_X = mybir.AxisListType.X
LN_EXP = "natural_log_exp_and_others"

P = 128
D = 1024
T = 1024
KT = D // P
HALF = 512
D_FF = 2816
FG = D_FF // (2 * P)
HD = 64
C = 64
NHP = D // P
DECAY = float(np.exp(-0.5))
RMS_EPS = 1e-6
GN_EPS = 64e-5
SCALE = HD ** -0.5
NKV = 4
NB = T // P
LN_SHIFT = 17

N_RKV, N_LORA, N_WO = 0, 24, 27
N_F0 = N_WO + 8
N_QKV = N_F0 + 6 * FG
N_AO = N_QKV + 12
N_F1 = N_AO + 8
N_ALL = N_F1 + 6 * FG
MIX_LAST = (7, 15, 23, 24, 25)

G0, MIX, W0, A0, KK, KA, RK, LNW, LNB = 0, 64, 112, 120, 128, 136, 144, 152, 160
BQKV, BO, SINK, EPS_RMS, EPS_GN, KSH = 168, 180, 188, 204, 205, 206
NPAR = 207


def shape_constants():
    i = np.arange(P)
    same = lambda n: (i[:, None] // n) == (i[None, :] // n)
    up = i[None, :] > i[:, None]
    ident = np.eye(P)
    blk = same(HD)
    strict = same(C) & up
    incl = same(C) & (up | np.eye(P, dtype=bool))
    e = [same(2 * b) & ~same(b) & up for b in (8, 16, 32)]
    base = np.concatenate([ident, np.ones((P, P)), blk], 1).astype(np.float32)
    rst = np.tile((np.arange(HALF) % C != 0).astype(np.float32), (P, 1))
    rw = np.concatenate([rst, strict, incl, same(8) & up] + e, 1).astype(np.float32)
    rope = HD // 4
    inv = np.float32(500000.0) ** (-np.arange(0, rope, 2, dtype=np.float32) / np.float32(rope))
    ang = np.arange(T, dtype=np.float32)[:, None] * inv[None, :].astype(np.float32)
    cos, sin = np.ones((P, T), np.float32), np.zeros((P, T), np.float32)
    perm = np.zeros((P, P), np.float32)
    for h in (0, HD):
        for d in range(rope // 2):
            lo, hi = h + d, h + d + rope // 2
            cos[lo] = cos[hi] = np.cos(ang[:, d])
            sin[lo] = sin[hi] = np.sin(ang[:, d])
            perm[hi, lo] = -1.0
            perm[lo, hi] = 1.0
    qi, kj = np.arange(P)[:, None], np.arange(2 * P)[None, :]
    rel = qi + P - kj
    band = (rel >= 0) & (rel < P)
    far = np.float32(-1e30)
    m = np.where(band, 0, far).astype(np.float32)
    m0 = np.where(band & (kj >= P), 0, far).astype(np.float32)
    at = np.concatenate([cos, sin, perm, m0, m], 1).astype(np.float32)
    return base, rw, at


def build_program(nc, xT, wt, par, lora2, cbase, crw, cat, out):
    ctx = ExitStack()
    with ctx:
        def keep(stack, name, shape, dt=F32):
            return stack.enter_context(nc.sbuf_tensor(name, shape, dt))

        def sem(name):
            return ctx.enter_context(nc.semaphore(name))

        xh = keep(ctx, "xh", [P, KT, T], F32R)
        xl = keep(ctx, "xl", [P, KT, T], F32R)
        wst = keep(ctx, "wst", [P, 2, T])
        wh = keep(ctx, "wh", [P, 2, T], F32R)
        wl = keep(ctx, "wl", [P, 2, T], F32R)
        sqb = keep(ctx, "sqb", [P, 2, T])
        tmp = keep(ctx, "tmp", [P, 2, T])
        cb = keep(ctx, "cb", [P, 3 * P])
        pr = keep(ctx, "pr", [P, NPAR])
        ident, ones, blk = (cb[:, i * P:(i + 1) * P] for i in range(3))
        rstd = keep(ctx, "rstd", [P, T])
        ps = ctx.enter_context(nc.psum_tensor("ps", [P, 4, T], F32))

        s_n = ExitStack()
        x = keep(s_n, "x", [P, KT, T])
        y = keep(s_n, "y", [P, KT, T])
        hidh = keep(s_n, "hidh", [P, 2, 2, T], F32R)
        hidl = keep(s_n, "hidl", [P, 2, 2, T], F32R)
        s_n.close()
        s_q = ExitStack()
        keep(s_q, "below_squares", [P, 5, 4, T])
        sqx = keep(s_q, "sqx", [P, KT, HALF])
        s_q.close()
        s_ab = ExitStack()
        lor = keep(s_ab, "lor", [P, 3, T])
        s_a = ExitStack()
        h = keep(s_a, "h", [P, KT, T + 1])
        xx = keep(s_a, "xx", [P, KT, T])
        ost = keep(s_a, "ost", [P, 2, T])
        s_a.close()
        s_b = ExitStack()
        At, Bt, Kt, Rt, bon = (keep(s_b, n, [P, 2, HALF]) for n in ("At", "Bt", "Kt", "Rt", "bon"))
        pend = keep(s_b, "pend", [P, 2, 8])
        pcp = keep(s_b, "pcp", [P, 6])
        pcq = keep(s_b, "pcq", [P, 2])
        Sm = [[keep(s_b, f"Sm{a}{g}", [P, 2, 4, P]) for g in range(2)] for a in range(2)]
        TT = [[keep(s_b, f"TT{a}{g}", [P, 2, 2, P]) for g in range(2)] for a in range(2)]
        tok = [[keep(s_b, f"tok{a}{g}", [P, 3, P]) for g in range(2)] for a in range(2)]
        Et = [keep(s_b, f"Et{g}", [P, 3, 2, P]) for g in range(2)]
        Dt = [keep(s_b, f"Dt{g}", [P, 2, P]) for g in range(2)]
        Dn = [keep(s_b, f"Dn{g}", [P, 2, P]) for g in range(2)]
        D2 = [keep(s_b, f"D2{g}", [P, 2, 2, P]) for g in range(2)]
        Wm = [keep(s_b, f"Wm{g}", [P, 2, P]) for g in range(2)]
        rhs_sb = keep(s_b, "rhs_sb", [P, P])
        SA = [keep(s_b, f"SA{g}", [P, P]) for g in range(2)]
        S = keep(s_b, "S", [P, P])
        SP = keep(s_b, "SP", [P, P])
        ysb = keep(s_b, "ysb", [P, HALF])
        cr = keep(s_b, "cr", [P, 512 + 6 * P])
        rst, m_si, mu8 = cr[:, 0:512], cr[:, 512:768], cr[:, 768:896]
        me = [cr[:, 896 + P * i:1024 + P * i] for i in range(3)]
        l2 = keep(s_b, "l2", [P, 2, P])
        l2g = keep(s_b, "l2g", [P, P])
        rin = keep(s_b, "rin", [P, HALF])
        kin = keep(s_b, "kin", [P, HALF])
        vin = keep(s_b, "vin", [P, 2, HALF])
        psq, zt = rstd[:, 0:HALF], rstd[:, HALF:T]
        s_b.close()
        s_ab.close()
        s_c = ExitStack()
        q = keep(s_c, "q", [P, KT, T])
        kd = keep(s_c, "kd", [P, NKV, T + P])
        vt = keep(s_c, "vt", [P, NB + 1, NKV, HD])
        ca = keep(s_c, "ca", [P, 2 * T + P + 4 * P])
        cosT, sinT, perm = ca[:, 0:T], ca[:, T:2 * T], ca[:, 2 * T:2 * T + P]
        msk = [ca[:, 2 * T + P + 256 * i:2 * T + P + 256 * i + 256] for i in range(2)]
        sc = keep(s_c, "sc", [P, 3, T])
        pT = keep(s_c, "pT", [P, 2, 4 * P])
        st = keep(s_c, "st", [P, 3, 6, 4])
        s_c.close()

        T0, T1, T2, T3 = (sqb[:, i // 2, (i % 2) * HALF:(i % 2) * HALF + HALF] for i in range(4))
        T4, T5, T6, T7 = (tmp[:, i // 2, (i % 2) * HALF:(i % 2) * HALF + HALF] for i in range(4))

        rkv_d = nc.dram_tensor("rkv_scratch", [3, NHP, P, T], F32).ap()
        x_d = nc.dram_tensor("x_scratch", [P, KT, T], F32).ap()

        c_in, a_in = sem("const_loaded"), sem("phase_const_loaded")
        w_dma = [sem("w_loaded0"), sem("w_loaded1")]
        w_hi, w_split, w_used = sem("w_hi_ready"), sem("w_split_ready"), sem("w_tile_used")
        mm_evac = sem("tile_evacuated")
        x_first = [sem(f"x_part{i}_loaded") for i in range(4)]
        x_in, x_out = sem("x_loaded"), sem("x_saved")
        x_odd, x_used, xx_odd = sem("x_odd_split_ready"), sem("x_tile_used"), sem("shift_diff_odd_ready")
        acc_sq, acc_done, sum_full = sem("y_square_ready"), sem("y_squares_added"), sem("y_sum_full")
        x_sum_full = sem("x_sum_full")
        half_full = sem("last_tile_half_full")
        scaled, res_odd = sem("y_scaled"), sem("residual_odd_done")
        sq_ready, sq_used, rs_ready = sem("square_ready"), sem("square_used"), sem("rstd_ready")
        xn_ready, xhi_ready, x_ready = sem("normed_ready"), sem("x_hi_ready"), sem("x_split_ready")
        act_own, dve_own, pool_own = sem("scalar_step"), sem("vector_step"), sem("pool_step")
        h_ready, xx_ready = sem("h_ready"), sem("shift_diff_ready")
        o_full, o_dma = [sem("spill0_full"), sem("spill1_full")], [sem("spill0_written"), sem("spill1_written")]
        lo_ready = sem("lora_ready")
        res_done = sem("residual_done")
        sg_ready, up_mul, hid_hi, hid_ready = (sem(n) for n in ("silu_ready", "hidden_ready", "hidden_hi_ready", "hidden_split"))
        dn_full, dn_evac, y_zero = sem("down_full"), sem("down_added"), sem("y_zeroed")
        st_full = [sem(f"st{i}_full") for i in range(14)]
        st_evac = [sem(f"st{i}_evac") for i in range(14)]
        dt_ready, x1_ready = sem("Dt_ready"), sem("X1_ready")
        e_ready = sem("E_ready")
        rhs_full, rhs_sbr, sa_full, sa_sbr, ds_full, s_ready = (sem(n) for n in (
            "rhs_full", "rhs_copied", "sa_full", "sa_copied", "chunk_done", "state_ready"))
        l_in, lg_in, r_in, k_in = sem("l2_loaded"), sem("l2g_loaded"), sem("r_loaded"), sem("k_loaded")
        v_in = [sem("v_loaded0"), sem("v_loaded1")]
        zw_f, za_f, mean_f, ss_f, var_f, g_f, bon_f = (sem(n + "_full") for n in ("zw", "za", "mean", "ss", "var", "g", "bonus"))
        zw_e, za_e, mean_e, ss_e, var_e, g_e, bon_e = (sem(n + "_read") for n in ("zw", "za", "mean", "ss", "var", "g", "bonus"))
        ksq_r, s_r, sm_r, P_r, rinv_r, prep_done, rk_r, sp_ready = (sem(n) for n in (
            "key_square", "decay_sum", "decay_sum_prev", "decays", "key_rnorm", "prep_done", "rk_ready", "state_decayed"))
        y_sb, yc_r, ysq_r, z_r, zhi_r, z_ready = (sem(n) for n in (
            "y_copied", "y_centred", "y_square", "z_ready", "z_hi", "z_split"))
        pq_r = sem("post_params")
        y_tile, pp_r = sem("y_tile_done"), sem("prep_params")
        rot_f, rot_r = sem("rotated_full"), sem("rope_done")
        kd_r, pad_r = sem("keys_ready"), sem("kv_padded")
        s_f, sm_m, nm_r, p_r, p_n, pt_f, pt_r, o_f, o_r = (sem(n) for n in (
            "scores_full", "scores_masked", "max_ready", "probs_ready", "probs_normed",
            "pT_full", "pT_copied", "o_full", "o_hi"))
        oz_r, den_r = sem("o_split"), sem("denominators_ready")
        st_out = sem("out_written")

        class Own:
            def __init__(self, eng, s):
                self.eng, self.s, self.n, self.r = eng, s, 0, 0

            def link(self, ins):
                self.n += 1
                ins.then_inc(self.s, 1)
                self.eng.wait_ge(self.s, self.r + self.n)

        def bank(b):
            return ps[:, b // 2, (b % 2) * HALF:(b % 2) * HALF + HALF]

        def halves():
            return [(0, HALF), (HALF, T)]

        def inv_bank(s, g):
            return (0, 1, 2, 7)[(2 * s + g) % 4]

        def prior(s, g):
            e = 2 * s + g
            return (e - 4) % 28 // 2, g, int(e < 4)

        def xs(kt):
            return (tmp if kt % 4 < 2 else sqb)[:, kt % 2, :]

        def xn(p, hf, kt):
            return 6 * KT + 2 * KT * p + KT * hf + kt

        def wait_x(eng, n):
            eng.wait_ge(x_odd if n % 2 else x_ready, n // 2 + 1)

        B_SC, B_Y, B_AUX0, B_AUX1 = 3, 4, 5, 6
        block = ctx.enter_context(nc.Block())

        @block.sync
        def _(sp):
            sp.dma_start(cb[:], cbase).then_inc(c_in, 16)
            sp.dma_start(pr[:], par).then_inc(c_in, 16)
            sp.wait_ge(x_first[3], 16)
            sp.dma_start(wst[:, 0, :], wt[0]).then_inc(w_dma[0], 16)
            sp.dma_start(wst[:, 1, :], wt[1]).then_inc(w_dma[1], 16)
            with sp.Fori(0, (N_ALL - 3) // 2) as i:
                for u in range(2):
                    sp.wait_ge(w_split, 2 * i + u + 1)
                    sp.dma_start(wst[:, u, :], wt[2 * i + 2 + u]).then_inc(w_dma[u], 16)
            sp.wait_ge(w_split, N_ALL - 2)
            sp.dma_start(wst[:, 0, :], wt[N_ALL - 1]).then_inc(w_dma[0], 16)
            for hf, (lo, hi) in enumerate(halves()):
                for kt in range(KT):
                    sp.wait_ge(res_odd if kt % 2 else res_done, KT * 3 + KT // 2 * hf + kt // 2 + 1)
                    sp.dma_start(out[:, kt, lo:hi], x[:, kt, lo:hi]).then_inc(st_out, 16)
            sp.wait_ge(st_out, 16 * 2 * KT)

        @block.gpsimd
        def _(pool):
            own = Own(pool, pool_own)
            for i in range(4):
                pool.dma_start(h[:, 2 * i:2 * i + 2, 1:T + 1], xT[:, 2 * i:2 * i + 2, :]).then_inc(x_first[i], 16)
            own.link(pool.memset(h[:, :, 0:1], 0.0))

            def lo_part(b, kt):
                pool.wait_ge(xhi_ready, b + kt + 1)
                pool.tensor_tensor(xl[:, kt, :], xs(kt), xh[:, kt, :].bitcast(F32), ALU.subtract).then_inc(x_odd, 1)

            def lo_odd(b):
                for kt in range(1, KT, 2):
                    lo_part(b, kt)

            for kt in range(1, KT, 2):
                pool.wait_ge(h_ready, kt + 1)
                pool.tensor_tensor(xx[:, kt, :], h[:, kt, 0:T], h[:, kt, 1:T + 1], ALU.subtract).then_inc(xx_odd, 1)
                if kt >= 3:
                    lo_part(0, kt - 2)
            lo_part(0, KT - 1)
            for j in range(3):
                def spill(i, u):
                    pool.wait_ge(o_full[u], i + 4 * j + 1)
                    pool.dma_start(rkv_d[j][2 * i + u], ost[:, u, :]).then_inc(o_dma[u], 16)
                with pool.Fori(0, 3) as i:
                    for u in range(2):
                        spill(i, u)
                spill(3, 0)
                lo_odd(KT * (j + 1))
                spill(3, 1)
            pool.wait_ge(o_dma[0], 16 * 12)
            pool.wait_ge(o_dma[1], 16 * 12)
            pool.dma_start(cr[:], crw).then_inc(a_in, 16)

            def load_piece(hp, pc, first):
                r = 2 * hp + pc
                if not first:
                    pool.wait_ge(prep_done, r)
                if pc == 0:
                    if not first:
                        pool.wait_ge(za_f, r)
                    pool.dma_start(l2[:], lora2[hp][:, 0:2, :]).then_inc(l_in, 16)
                if not first:
                    pool.wait_ge(bon_e, r)
                if not (first or (pc == 1 and type(hp) is int and hp == 0)):
                    pool.wait_ge(st_full[2], 8 * hp + 4 * pc - 4)
                cols = slice(pc * HALF, pc * HALF + HALF)
                pool.dma_start(rin[:], rkv_d[0, hp][:, cols]).then_inc(r_in, 16)
                pool.dma_start(kin[:], rkv_d[1, hp][:, cols]).then_inc(k_in, 16)
                pool.dma_start(vin[:, pc, :], rkv_d[2, hp][:, cols]).then_inc(v_in[pc], 16)

            def load_g(hp, first):
                if not first:
                    pool.wait_ge(g_f, 2 * hp)
                pool.dma_start(l2g[:], lora2[hp][:, 2, :]).then_inc(lg_in, 16)

            def merge_masks(k, a, nopr):
                for g in range(2):
                    pool.wait_ge(st_evac[1], 2 * k + g + 1)
                    if not nopr:
                        pool.wait_ge(st_full[12], 2 * k + g - 1)
                    for lv in range(3):
                        ins = pool.tensor_tensor(Et[g][:, lv], Sm[a][g][:, :, 0, :],
                                                 me[lv].unsqueeze(1).to_broadcast([P, 2, P]), ALU.mult)
                    ins.then_inc(e_ready, 1)

            def body(hp, first, last):
                load_piece(hp, 1, False)
                merge_masks(4 * hp + 1, 1, False)
                load_g(hp, first)
                merge_masks(4 * hp + 2, 0, False)
                if not last:
                    load_piece(hp + 1, 0, False)
                merge_masks(4 * hp + 3, 1, False)
                if not last:
                    merge_masks(4 * hp + 4, 0, False)

            load_piece(0, 0, True)
            for j in (4, 5):
                lo_odd(KT * j)
            wait_x(pool, 6 * KT - 2)
            pool.wait_ge(a_in, 16)
            merge_masks(0, 0, True)
            body(0, True, False)
            with pool.Fori(1, NHP - 1) as hp:
                body(hp, False, False)
            body(NHP - 1, False, True)

            pool.wait_ge(z_ready, 16)
            pool.wait_ge(ds_full, 16 * NHP)
            pool.wait_ge(e_ready, 2 * 32)
            pool.dma_start(x[:], xT).then_inc(x_in, 16)

            def residual_odd(i):
                for hf, (lo, hi) in enumerate(halves()):
                    for kt in range(1, KT, 2):
                        pool.wait_ge(scaled, 2 * KT * i + KT * hf + kt)
                        pool.tensor_tensor(x[:, kt, lo:hi], x[:, kt, lo:hi], y[:, kt, lo:hi], ALU.add).then_inc(res_odd, 1)

            def norm_lo(p):
                for hf, (lo, hi) in enumerate(halves()):
                    for kt in range(1, KT, 2):
                        pool.wait_ge(xhi_ready, xn(p, hf, kt) + 1)
                        pool.tensor_tensor(xl[:, kt, lo:hi], xs(kt)[:, lo:hi], xh[:, kt, lo:hi].bitcast(F32),
                                           ALU.subtract).then_inc(x_odd, 1)

            def ffn_zero(i):
                pool.wait_ge(res_done, KT * (i + 1))
                pool.wait_ge(res_odd, KT * (i + 1))
                pool.memset(y[:], 0.0).then_inc(y_zero, 1)

            pool.wait_ge(x_in, 16)
            residual_odd(0)
            norm_lo(0)
            ffn_zero(0)
            residual_odd(1)
            pool.wait_ge(res_done, KT * 2)
            pool.wait_ge(res_odd, KT * 2)
            pool.dma_start(x_d, x[:]).then_inc(x_out, 16)
            pool.dma_start(ca[:], cat).then_inc(a_in, 16)
            norm_lo(1)
            pool.memset(kd[:, :, 0:P], 0.0)
            pool.memset(vt[:, 0, :, :], 0.0).then_inc(pad_r, 1)
            for it in range(NB * NKV):
                pool.wait_ge(den_r, it + 1)
                s3 = sc[:, it % 3, :].rearrange("p (i c) -> p i c", c=2 * P)
                pool.tensor_tensor(s3, s3, st[:, it % 3, 5, :].unsqueeze(2).to_broadcast([P, 4, 2 * P]), ALU.mult).then_inc(p_n, 1)
            pool.wait_ge(oz_r, NB * NKV)
            pool.dma_start(x[:], x_d).then_inc(x_in, 16)
            pool.wait_ge(x_in, 32)
            residual_odd(2)
            norm_lo(2)
            ffn_zero(2)
            residual_odd(3)

        @block.tensor
        def _(pe):
            pe.wait_ge(c_in, 32)

            def dense(n, r, slot, free, xb, count_x=False, before=None):
                pe.wait_ge(w_split, n + r + 1)
                if free is not None:
                    pe.wait_ge(mm_evac, free + r)
                for kt in range(KT):
                    if before:
                        before(kt)
                    if xb is not None:
                        wait_x(pe, xb + kt)
                    for j, (a, b) in enumerate(((wh, xh), (wh, xl), (wl, xh))):
                        for lo, hi in halves():
                            ins = pe.matmul(ps[:, slot, lo:hi], a[:, n % 2, kt * P:(kt + 1) * P],
                                            b[:, kt, lo:hi], start=(kt == 0 and j == 0),
                                            stop=(kt == KT - 1 and j == 2))
                    if count_x and kt < KT - 1:
                        ins.then_inc(x_used, 1)
                ins.then_inc(w_used, 1)

            def stats_y(i, hfs=(0, 1)):
                for hf in hfs:
                    lo, hi = halves()[hf]
                    pe.wait_ge(acc_done, KT * i + KT - 1 + hf)
                    pe.matmul(ps[:, 2, lo:hi], ones, rstd[:, lo:hi], start=True, stop=True).then_inc(sum_full, 1)

            def stats(nn):
                for hf, (lo, hi) in enumerate(halves()):
                    for kt in range(KT):
                        n = 2 * KT * nn - KT + KT * hf + kt
                        pe.wait_ge(sq_ready, n + 1)
                        pe.matmul(ps[:, 2, lo:hi], ones, sqx[:, kt, :], start=(kt == 0), stop=(kt == KT - 1)).then_inc(sq_used, 1)

            def dense_halves(n, s0, norm, i=None):
                for hf, (lo, hi) in enumerate(halves()):
                    for t in range(1 if norm is None else 2):
                        sl = s0 if norm is None else t
                        if hf == 0:
                            pe.wait_ge(w_split, n + t + 1)
                        for kt in range(KT):
                            if norm is None and hf == 1 and kt == 3:
                                stats_y(i, (0,))
                            if norm is not None and t == 0:
                                wait_x(pe, xn(norm, hf, kt))
                            for j, (a, b) in enumerate(((wh, xh), (wh, xl), (wl, xh))):
                                ins = pe.matmul(ps[:, sl, lo:hi], a[:, (n + t) % 2, kt * P:(kt + 1) * P], b[:, kt, lo:hi],
                                                start=(kt == 0 and j == 0), stop=(kt == KT - 1 and j == 2))
                        if hf == 1:
                            ins.then_inc(w_used, 1)
                        elif norm is None:
                            ins.then_inc(half_full, 1)

            pe.wait_ge(sq_used, KT)
            for lo, hi in halves():
                ins = pe.matmul(ps[:, 2, lo:hi], ones, rstd[:, lo:hi], start=True, stop=True)
            ins.then_inc(x_sum_full, 1)
            def rkv(j, t, r):
                n = 8 * j + t
                if n >= 4:
                    pe.wait_ge(o_full[t % 2], (n - 4) // 2 + 1 + 2 * r)
                dense(n, 4 * r, t % 4, None, KT * j, True)

            for t in range(8):
                rkv(0, t, 0)
            for j in (1, 2):
                with pe.Fori(0, 2) as i:
                    for t in range(4):
                        rkv(j, t, i)
            def lora(j, before=None):
                n = N_LORA + j
                if j < 2:
                    pe.wait_ge(o_full[n % 2], (n - 4) // 2 + 1)
                else:
                    pe.wait_ge(lo_ready, 1)
                dense(n, 0, j % 2, None, KT * (3 + j), True, before)

            lora(0)
            lora(1)

            def mm(o, a, b, start, stop=True):
                return pe.matmul(o, a, b, start=start, stop=stop, skip_group_check=True)

            def stage(s, g, k, a, nopr):
                b = bank(inv_bank(s, g))
                ps_, pg, back = prior(s, g)
                if not (back and nopr):
                    pe.wait_ge(st_evac[ps_], 2 * (k - back) + pg + 1)
                cols = slice(a * 256 + g * P, a * 256 + g * P + P)
                if s < 2:
                    hh = slice(HD * s, HD * s + HD)
                    for i, L in enumerate((Bt, Kt)):
                        for j, R in enumerate((At, Rt)):
                            ins = mm(b[:, (2 * i + j) * P:(2 * i + j + 1) * P], L[hh, pcs, cols], R[hh, pcs, cols], i + j == 0)
                elif s == 2:
                    for i, src in enumerate((vin, Bt, Kt)):
                        ins = pe.transpose(b[:, i * P:(i + 1) * P], src[:, pcs, cols], ident)
                elif s == 3:
                    pe.wait_ge(dt_ready, 2 * k + g + 1)
                    for i in range(2):
                        ins = pe.transpose(b[:, i * P:(i + 1) * P], Dt[g][:, i, :], ident)
                elif s == 4:
                    pe.wait_ge(st_evac[3], 2 * k + g + 1)
                    for i in range(2):
                        mm(b[:, i * P:(i + 1) * P], Dn[g][:, i, :], Dt[g][:, i, :], i == 0)
                        ins = mm(b[:, (2 + i) * P:(3 + i) * P], Dt[g][:, i, :], Dn[g][:, i, :], False)
                elif s == 5:
                    pe.wait_ge(st_evac[4], 2 * k + g + 1)
                    pe.wait_ge(x1_ready, 2 * k + g + 1)
                    for i in range(2):
                        mm(b[:, i * P:(i + 1) * P], D2[g][:, 1, i, :], TT[a][g][:, 0, i, :], i == 0)
                        ins = mm(b[:, (2 + i) * P:(3 + i) * P], D2[g][:, 0, i, :], D2[g][:, 1, i, :], False)
                elif s == 6:
                    pe.wait_ge(st_evac[5], 2 * k + g + 1)
                    for i in range(2):
                        ins = mm(b[:, i * P:(i + 1) * P], Dn[g][:, i, :], TT[a][g][:, 0, i, :], i == 0)
                elif s == 7:
                    pe.wait_ge(st_evac[6], 2 * k + g + 1)
                    for i in range(2):
                        ins = pe.transpose(b[:, i * P:(i + 1) * P], TT[a][g][:, 0, i, :], ident)
                elif s % 2 == 0:
                    pe.wait_ge(e_ready, 2 * k + g + 1)
                    pe.wait_ge(st_evac[s - 1], 2 * k + g + 1)
                    for i in range(2):
                        ins = mm(b[:, i * P:(i + 1) * P], Et[g][:, (s - 8) // 2, i, :], TT[a][g][:, 1, i, :], i == 0)
                else:
                    pe.wait_ge(st_evac[s - 1], 2 * k + g + 1)
                    for i in range(2):
                        ins = mm(b[:, i * P:(i + 1) * P], Wm[g][:, i, :], TT[a][g][:, 0, i, :], i == 0)
                        if s < 13:
                            ins = mm(b[:, (2 + i) * P:(3 + i) * P], TT[a][g][:, 0, i, :], Wm[g][:, i, :], False)
                ins.then_inc(st_full[s], 1)

            def scan(f, hp, u, first):
                c, ph = f // 3, f % 3
                g, p = c // 2, c % 2
                a, pc = u % 2, u // 2
                n = 16 * hp + 4 * u + c
                tp = slice(C * p, C * p + C)
                base = a * 256 + g * P
                cols = slice(base + C * p, base + C * p + C)
                sc, yb = bank(B_SC), bank(B_Y)
                sm, tk = Sm[a][g], tok[a][g]
                if ph == 0:
                    if c == 0:
                        pe.wait_ge(st_evac[13], 2 * (4 * hp + u) + 2)
                        if a == 0 and not (first and pc == 0):
                            pe.wait_ge(y_sb, 2 * hp + pc)
                    pe.wait_ge(s_ready, n + 1)
                    mm(sc[tp, 0:P], At[:, pc, cols], S[:], True)
                    for i in range(2):
                        hh = slice(HD * i, HD * i + HD)
                        ins = mm(sc[tp, hh], sm[:, i, 2, tp], tk[:, 0, hh], False)
                    ins.then_inc(rhs_full, 1)
                elif ph == 1:
                    mm(yb[:, cols], S[:], Rt[:, pc, cols], c == 0 and a == 0)
                    pe.wait_ge(rhs_sbr, n + 1)
                    for i in range(2):
                        ins = mm(sc[tp, P + HD * i:P + HD * i + HD], TT[a][g][:, 0, i, tp],
                                 rhs_sb[:, HD * i:HD * i + HD], i == 0)
                    ins.then_inc(sa_full, 1)
                else:
                    pe.wait_ge(sa_sbr, n + 1)
                    mm(sc[:, 2 * P:3 * P], tk[tp, 1, :], SA[g][tp, :], True)
                    mm(sc[:, 2 * P:3 * P], tk[tp, 2, :], tk[tp, 0, :], False).then_inc(ds_full, 1)
                    if p == 1:
                        for L, m in ((SA[g][:], 1), (tk[:, 0, :], 3)):
                            for i in range(2):
                                hh = slice(HD * i, HD * i + HD)
                                ins = mm(yb[hh, base:base + P], L[:, hh], sm[:, i, m, :], False)
                        ins.then_inc(y_tile, 1)

            def is0(v, below=1):
                return type(v) is int and v < below

            def prep(e, r, hp, pc):
                cols = slice(pc * HALF, pc * HALF + HALF)
                if e == 0:
                    if not is0(r):
                        pe.wait_ge(bon_e, r)
                    pe.wait_ge(l_in, 16 * (hp + 1))
                    mm(bank(B_AUX0), l2[:, 0, :], lor[:, 0, cols], True).then_inc(zw_f, 1)
                    if not is0(r):
                        pe.wait_ge(ss_e, r)
                    if not is0(r, 3):
                        pe.wait_ge(z_r, r - 2)
                    mm(bank(B_AUX1), l2[:, 1, :], lor[:, 1, cols], True).then_inc(za_f, 1)
                elif e == 1:
                    pe.wait_ge(za_e, r + 1)
                    pe.wait_ge(ksq_r, r + 1)
                    mm(bank(B_AUX1), blk, T6, True).then_inc(ss_f, 1)
                else:
                    pe.wait_ge(rk_r, r + 1)
                    mm(bank(B_AUX0), blk, T6, True).then_inc(bon_f, 1)

            def post(e, p, hp, pc, alone):
                cols = slice(pc * HALF, pc * HALF + HALF)
                if e == 0:
                    if alone == 0:
                        pe.wait_ge(zw_e, p + 3)
                    elif alone == 1:
                        pe.wait_ge(bon_e, 16)
                    else:
                        pe.wait_ge(var_e, p)
                    pe.wait_ge(y_sb, p + 1)
                    mm(bank(B_AUX0), blk, ysb[:], True).then_inc(mean_f, 1)
                elif e == 1:
                    pe.wait_ge(ysq_r, p + 1)
                    mm(bank(B_AUX0), blk, psq, True).then_inc(var_f, 1)
                else:
                    pe.wait_ge(ss_e, p + 3 if alone == 0 else 16)
                    if not is0(p):
                        pe.wait_ge(z_r, p)
                    pe.wait_ge(lg_in, 16 * (hp + 1))
                    mm(bank(B_AUX1), l2g[:], lor[:, 2, cols], True).then_inc(g_f, 1)

            def rounds(inv, sc, busy, between=None):
                nonlocal pcs
                if inv:
                    k, u, nopr, need = inv
                    pcs = u // 2
                    pe.wait_ge(prep_done, need)
                for s in range(14):
                    if busy and busy[0] and s == 0:
                        prep(0, *busy[0])
                    if inv:
                        if s == 2:
                            pe.wait_ge(bon_e, need)
                        stage(s, 0, k, u % 2, nopr)
                    if sc and s >= 2:
                        scan(s - 2, *sc)
                    if inv:
                        stage(s, 1, k, u % 2, nopr)
                    if between:
                        between(s)
                    if busy:
                        pp, qq, alone = busy
                        if qq and s == 2:
                            post(0, *qq, alone)
                        if pp and s == 3:
                            prep(1, *pp)
                        if qq and s == 6:
                            post(1, *qq, alone)
                        if qq and s == 8:
                            post(2, *qq, alone)
                        if pp and s == 12:
                            if qq:
                                pe.wait_ge(var_e, pp[0] - 1)
                            prep(2, *pp)

            pcs = 0

            def body(hp, first, last):
                rounds((4 * hp + 1, 1, False, 2 * hp + 1), (hp, 0, first),
                       ((2 * hp + 1, hp, 1), None if first else (2 * hp - 1, hp - 1, 1), 0))
                rounds((4 * hp + 2, 2, False, 2 * hp + 2), (hp, 1, first), None)
                rounds((4 * hp + 3, 3, False, 2 * hp + 2), (hp, 2, first),
                       (None if last else (2 * hp + 2, hp + 1, 0), (2 * hp, hp, 0), 1 if last else 0))
                rounds(None if last else (4 * hp + 4, 0, False, 2 * hp + 3), (hp, 3, first), None, project_early if last else None)

            def project_early(s):
                if s >= 3 and s % 2 and (s - 3) // 2 < 6:
                    project_part(0, (s - 3) // 2)

            def project_part(t, kt):
                if kt == 0:
                    pe.wait_ge(z_ready, 14)
                    pe.wait_ge(w_split, N_WO + t + 1)
                for j, (a, b) in enumerate(((wh, xh), (wh, xl), (wl, xh))):
                    for lo, hi in halves():
                        ins = pe.matmul(ps[:, t, lo:hi], a[:, (N_WO + t) % 2, kt * P:(kt + 1) * P], b[:, kt, lo:hi],
                                        start=(kt == 0 and j == 0), stop=(kt == KT - 1 and j == 2))
                if kt == KT - 1:
                    ins.then_inc(w_used, 1)

            def first_prep(kt):
                if kt == KT - 1:
                    pe.wait_ge(lo_ready, 2)
                    pe.wait_ge(o_full[0], 12)
                    pe.wait_ge(o_full[1], 12)
                    prep(0, 0, 0, 0)

            lora(2, first_prep)
            prep(1, 0, 0, 0)
            pe.wait_ge(lo_ready, 3)
            pe.wait_ge(a_in, 16)
            prep(2, 0, 0, 0)
            rounds((0, 0, True, 1), None, None)
            body(0, True, False)
            with pe.Fori(1, NHP - 1) as hp:
                body(hp, False, False)
            body(NHP - 1, False, True)

            def project(i, n0, m0, first):
                for t in range(first, 7):
                    dense(n0 + t, 0, t % 4, m0 + t - 3 if t >= 4 else None, None)
                pe.wait_ge(mm_evac, m0 + 4)
                dense_halves(n0 + 7, 3, None, i)

            post(0, 15, NHP - 1, 1, 2)
            post(2, 15, NHP - 1, 1, 2)
            project_part(0, 6)
            post(1, 15, NHP - 1, 1, 2)
            for kt in range(5):
                project_part(1, kt)
            pe.wait_ge(z_ready, 16)
            project_part(0, KT - 1)
            for kt in range(5, KT):
                project_part(1, kt)
            project(0, N_WO, 0, 2)
            stats_y(0, (1,))
            stats(1)

            def ffn(L, n0, norm):
                s0 = n0 % 2

                def gate_up(n, ws, t):
                    pe.wait_ge(w_split, n + 1)
                    for kt in range(KT):
                        for j, (a, b) in enumerate(((wh, xh), (wh, xl), (wl, xh))):
                            for lo, hi in halves():
                                ins = pe.matmul(ps[:, t, lo:hi], a[:, ws, kt * P:(kt + 1) * P], b[:, kt, lo:hi],
                                                start=(kt == 0 and j == 0), stop=(kt == KT - 1 and j == 2))
                    ins.then_inc(w_used, 1)

                def down(G, n, ws, cc, buf, gated):
                    pe.wait_ge(w_split, n + 1)
                    for m in range(4):
                        if cc == 0 and gated:
                            pe.wait_ge(sg_ready if m % 2 == 0 else up_mul, 2 * (G + 1) + m // 2 + 1)
                        else:
                            pe.wait_ge(dn_evac, 8 * G + 4 * cc + m - 3)
                        for kk in range(2):
                            pe.wait_ge(hid_ready, 2 * G + kk + 1)
                            for j, (a, b) in enumerate(((wh, hidh), (wh, hidl), (wl, hidh))):
                                for lo, hi in halves():
                                    ins = pe.matmul(ps[:, m, lo:hi], a[:, ws, kk * HALF + m * P:kk * HALF + (m + 1) * P],
                                                    b[:, buf, kk, lo:hi], start=(kk == 0 and j == 0),
                                                    stop=(kk == 1 and j == 2))
                        ins.then_inc(dn_full, 1)

                G = FG * L
                dense_halves(n0, None, norm)
                for t in range(2, 4):
                    gate_up(n0 + t, (s0 + t) % 2, t)
                for t in range(4):
                    pe.wait_ge(sg_ready if t % 2 == 0 else up_mul, 2 * G + t // 2 + 1)
                    gate_up(n0 + 4 + t, (s0 + t) % 2, t)
                down(G, n0 + 8, s0, 0, 0, True)
                down(G, n0 + 9, 1 - s0, 1, 0, True)

                def group(g, n, buf):
                    for t in range(4):
                        pe.wait_ge(dn_evac, 8 * (g - 2) + 4 + t + 1)
                        gate_up(n + t, (s0 + t) % 2, t)
                    down(g - 1, n + 4, s0, 0, 1 - buf, True)
                    down(g - 1, n + 5, 1 - s0, 1, 1 - buf, True)

                with pe.Fori(0, (FG - 3) // 2) as i:
                    for v in range(2):
                        group(2 * i + G + 2 + v, 12 * i + n0 + 10 + 6 * v, v)
                group(G + FG - 1, n0 + 4 + 6 * (FG - 2), 0)
                down(G + FG - 1, n0 + 6 * FG - 2, s0, 0, 0, False)
                down(G + FG - 1, n0 + 6 * FG - 1, 1 - s0, 1, 0, False)

            ffn(0, N_F0, 0)
            stats_y(1)
            stats(2)

            def qkv(l):
                if l >= 2:
                    pe.wait_ge(mm_evac, 8 + l - 1)
                dense(N_QKV + l, 0, l % 2, None, None)

            def turn(l):
                sl = 2 + l % 2
                pe.wait_ge(mm_evac, 8 + l + 1)
                if l >= 2:
                    pe.wait_ge(rot_r, l - 1)
                if l < 10:
                    for lo, hi in halves():
                        ins = mm(ps[:, sl, lo:hi], perm, tmp[:, l % 2, lo:hi], True)
                else:
                    for n in range(NB):
                        ins = pe.transpose(ps[:, sl, n * P:(n + 1) * P], tmp[:, l % 2, n * P:(n + 1) * P], ident)
                ins.then_inc(rot_f, 1)

            dense_halves(N_QKV, None, 1)
            pe.wait_ge(a_in, 32)
            turn(0)
            for l in range(2, 12):
                qkv(l)
                turn(l - 1)
            turn(11)
            pe.wait_ge(rot_r, 10)
            pe.wait_ge(kd_r, 3)
            pe.wait_ge(pad_r, 1)

            def scores(it):
                n, kv = it // NKV, it % NKV
                if it >= 2:
                    pe.wait_ge(sm_m, it - 1)
                for i in range(4):
                    hh = slice(HD * (i % 2), HD * (i % 2) + HD)
                    o = (i % 2) * HALF + (i // 2) * 2 * P
                    ins = mm(ps[:, it % 2, o:o + 2 * P], q[hh, 2 * kv + i // 2, n * P:(n + 1) * P],
                             kd[hh, kv, n * P:(n + 2) * P], i < 2)
                ins.then_inc(s_f, 1)

            def probs(it):
                pe.wait_ge(p_n, it + 1)
                if it >= 1:
                    pe.wait_ge(pt_r, it)
                for kk in range(2):
                    for i in range(4):
                        ins = pe.transpose(bank(4 + kk)[:, i * P:(i + 1) * P],
                                           sc[:, it % 3, i * 2 * P + kk * P:i * 2 * P + (kk + 1) * P], ident)
                ins.then_inc(pt_f, 1)

            def values(it):
                n, kv = it // NKV, it % NKV
                pe.wait_ge(pt_r, it + 1)
                if it >= 2:
                    pe.wait_ge(oz_r, it - 1)
                o = bank(6 + it % 2)
                for kk in range(2):
                    for odd in range(2):
                        ins = mm(o[HD * odd:HD * odd + HD, 0:2 * P], vt[:, n + kk, kv, :],
                                 pT[:, kk, odd * 2 * P:(odd + 1) * 2 * P], kk == 0)
                ins.then_inc(o_f, 1)

            IT = NB * NKV
            scores(0)
            scores(1)
            for it in range(IT):
                if it + 2 < IT:
                    scores(it + 2)
                if it == 0:
                    pe.wait_ge(rot_r, 12)
                if it >= 1:
                    values(it - 1)
                probs(it)
            values(IT - 1)
            pe.wait_ge(oz_r, IT)
            project(2, N_AO, 20, 0)
            stats_y(2, (1,))
            stats(3)
            ffn(1, N_F1, 2)
            stats_y(3)

        @block.scalar
        def _(act):
            own = Own(act, act_own)

            def w_round(n, r, after):
                act.wait_ge(w_dma[n % 2], 8 * r + 16 * (n // 2 + 1))
                if after:
                    act.wait_ge(*after)
                act.activation(wh[:, n % 2, :], wst[:, n % 2, :], ACT.Copy).then_inc(w_hi, 1)

            def square_y(i, t, ready, src, bias=None, then=None):
                if t >= 3:
                    act.wait_ge(acc_done, KT * i + t - 2)
                for hf, (lo, hi) in enumerate(halves()) if t == KT - 1 else ((0, (0, T)),):
                    act.wait_ge(*ready[hf])
                    dst = sqb[:, t % 2, lo:hi] if t else rstd[:]
                    if bias is None:
                        ins = act.activation(dst, src[:, lo:hi], ACT.Square)
                    else:
                        ins = act.activation(dst, src[:, lo:hi], ACT.Square, bias=bias)
                    ins.then_inc(acc_sq, 1)
                    if then:
                        then(lo, hi)

            def root(summed, after, lo=0, hi=T):
                act.wait_ge(*summed)
                if after:
                    act.wait_ge(*after)
                own.link(act.activation(rstd[:, lo:hi], ps[:, 2, lo:hi], ACT.Ln, bias=pr[:, EPS_RMS:EPS_RMS + 1], scale=1.0 / D))
                act.activation(rstd[:, lo:hi], rstd[:, lo:hi], ACT.Exp, scale=-0.5).then_inc(rs_ready, 1)

            def norms(i, p, second=None):
                if i % 2:
                    act.preload_act_table_set(LN_EXP)
                    root((sum_full, 2 * i + 1), None, 0, HALF)
                root((sum_full, 2 * i + 2), None, HALF, T)
                if p is None:
                    return
                w_round(second[0], 0, second[1])
                q0 = KT + 2 * KT * i

                def square_x(hf, kt):
                    lo, hi = halves()[hf]
                    act.wait_ge(res_odd if kt % 2 else res_done, KT * i + KT // 2 * hf + kt // 2 + 1)
                    n = q0 + KT * hf + kt
                    if hf == 1:
                        act.wait_ge(sq_used, n - KT + 1)
                    act.activation(sqx[:, kt, :], x[:, kt, lo:hi], ACT.Square).then_inc(sq_ready, 1)

                def root_x(hf):
                    root((sq_used, q0 + KT * (hf + 1)), (scaled, 2 * KT * i + KT * (hf + 1)), *halves()[hf])

                def round_x(hf, kt):
                    lo, hi = halves()[hf]
                    act.wait_ge(xn_ready, xn(p, hf, kt) + 1)
                    act.activation(xh[:, kt, lo:hi], xs(kt)[:, lo:hi], ACT.Copy).then_inc(xhi_ready, 1)

                for hf in range(2):
                    for kt in range(KT):
                        if hf == 1 and kt == 3:
                            root_x(0)
                        square_x(hf, kt)
                for hf in range(2):
                    for kt in range(KT):
                        if hf == 0 and kt == 2:
                            root_x(1)
                        round_x(hf, kt)

            def x_round(b, used=None):
                for kt in range(KT):
                    act.wait_ge(xn_ready, b + kt + 1)
                    if used is not None:
                        act.wait_ge(*((x_used, (KT - 1) * (used - 1) + kt + 1) if kt < KT - 1 else (w_used, used)))
                    act.activation(xh[:, kt, :], xs(kt), ACT.Copy).then_inc(xhi_ready, 1)

            act.wait_ge(c_in, 32)
            for kt in range(KT):
                act.wait_ge(x_first[kt // 2], 16)
                if kt >= 3:
                    act.wait_ge(sq_used, kt - 1)
                act.activation(sqb[:, kt % 2, :] if kt else rstd[:], h[:, kt, 1:T + 1], ACT.Square).then_inc(sq_ready, 1)
            act.preload_act_table_set(LN_EXP)
            root((x_sum_full, 1), None)
            w_round(0, 0, None)
            x_round(0)
            for n in range(N_LORA + 3):
                w_round(n + 1, 0, (w_used, n) if n >= 1 else None)
                if n in MIX_LAST:
                    x_round(KT * (MIX_LAST.index(n) + 1), n + 1)
                if n < N_LORA + 2:
                    act.wait_ge(w_used, n + 1)
                if n < N_LORA:
                    if n >= 2:
                        act.wait_ge(o_dma[n % 2], 16 * (n // 2))
                    act.activation(ost[:, n % 2, :], ps[:, n % 4, :], ACT.Copy).then_inc(o_full[n % 2], 1)
                elif n < N_LORA + 2:
                    act.activation(lor[:, n - N_LORA, :], ps[:, n % 2, :], (ACT.Tanh, ACT.Copy)[n - N_LORA]).then_inc(lo_ready, 1)

            def gate_out():
                act.wait_ge(w_used, N_LORA + 3)
                act.activation(lor[:, 2, :], ps[:, 0, :], ACT.Sigmoid).then_inc(lo_ready, 1)

            def evac(s, g, k, a):
                if s not in (2, 3, 4, 7, 8, 10, 12):
                    return
                b = bank(inv_bank(s, g))
                act.wait_ge(st_full[s], 2 * k + g + 1)
                if s == 2:
                    if not (type(k) is int and k < 2):
                        act.wait_ge(y_tile, 2 * k - 3 + g)
                    dst, n = tok[a][g][:].rearrange("p a b -> p (a b)"), 3 * P
                elif s == 3:
                    dst, n = Dn[g][:].rearrange("p a b -> p (a b)"), 2 * P
                elif s == 4:
                    dst, n = D2[g][:].rearrange("p a b c -> p (a b c)"), 4 * P
                elif s == 7:
                    dst, n = TT[a][g][:, 1].rearrange("p a b -> p (a b)"), 2 * P
                else:
                    dst, n = Wm[g][:].rearrange("p a b -> p (a b)"), 2 * P
                act.activation(dst, b[:, 0:n], ACT.Copy).then_inc(st_evac[s], 1)

            def scan(f, hp, u, first):
                c, ph = f // 3, f % 3
                g, p = c // 2, c % 2
                n, k = 16 * hp + 4 * u + c, 4 * hp + u
                tp = slice(C * p, C * p + C)
                b = bank(B_SC)
                if ph == 0:
                    act.wait_ge(rhs_full, n + 1)
                    act.activation(rhs_sb[tp, :], b[tp, 0:P], ACT.Copy).then_inc(rhs_sbr, 1)
                elif ph == 1:
                    act.wait_ge(sa_full, n + 1)
                    if p == 0 and not (type(k) is int and k == 0):
                        act.wait_ge(y_tile, 2 * k + g - 1)
                    act.activation(SA[g][tp, :], b[tp, P:2 * P], ACT.Copy).then_inc(sa_sbr, 1)

            def prep(e, r, hp, pc, between=None):
                if e == 0:
                    if pc == 0:
                        act.wait_ge(pp_r, hp + 1)
                    if not (type(r) is int and r == 0):
                        act.wait_ge(prep_done, r)
                        act.wait_ge(bon_f, r)
                    act.wait_ge(zw_f, r + 1)
                    act.activation(T0, bank(B_AUX0), ACT.Sigmoid, bias=pcp[:, 0:1]).then_inc(zw_e, 1)
                    act.wait_ge(za_f, r + 1)
                    act.activation(T5, bank(B_AUX1), ACT.Sigmoid, bias=pcp[:, 1:2]).then_inc(za_e, 1)
                    if between:
                        between()
                    act.preload_act_table_set(LN_EXP)
                    act.wait_ge(k_in, 16 * (r + 1))
                    act.activation(T6, kin[:], ACT.Square, scale=pcp[:, 2:3]).then_inc(ksq_r, 1)
                elif e == 1:
                    act.wait_ge(s_r, r + 1)
                    act.activation(T2, T1, ACT.Exp, scale=-DECAY)
                    act.activation(T3, T1, ACT.Exp, scale=DECAY)
                elif e == 2:
                    act.wait_ge(sm_r, r + 1)
                    act.activation(T4, T0, ACT.Exp, scale=-DECAY).then_inc(P_r, 1)
                else:
                    act.wait_ge(ss_e, r + 1)
                    own.link(act.activation(T6, T6, ACT.Ln, scale=float(2 ** LN_SHIFT)))
                    act.activation(T6, T6, ACT.Exp, scale=-0.5, bias=pr[:, KSH:KSH + 1]).then_inc(rinv_r, 1)

            def post(e, p, hp, pc):
                if e == 0:
                    act.wait_ge(y_tile, 4 * (p + 1))
                    act.activation(ysb[:], bank(B_Y), ACT.Copy).then_inc(y_sb, 1)
                elif e == 1:
                    act.wait_ge(yc_r, p + 1)
                    act.activation(psq, ysb[:], ACT.Square).then_inc(ysq_r, 1)
                elif e == 2:
                    act.wait_ge(var_f, p + 1)
                    own.link(act.activation(psq, bank(B_AUX0), ACT.Ln, bias=pr[:, EPS_GN:EPS_GN + 1], scale=1.0 / HD))
                    act.activation(psq, psq, ACT.Exp, scale=-0.5).then_inc(var_e, 1)
                else:
                    act.wait_ge(z_r, p + 1)
                    act.activation(xh[:, hp, pc * HALF:(pc + 1) * HALF], zt, ACT.Copy).then_inc(zhi_r, 1)

            def rounds(inv, sc, busy):
                for s in range(14):
                    if busy:
                        pp, qq = busy
                        if qq and s == 0:
                            post(0, *qq)
                    if inv:
                        evac(s, 0, inv[0], inv[1] % 2)
                    if sc and s >= 2:
                        scan(s - 2, *sc)
                    if inv:
                        evac(s, 1, inv[0], inv[1] % 2)
                    if busy:
                        if pp and s == 0:
                            prep(0, *pp)
                        if pp and 3 <= s <= 5:
                            prep(s - 2, *pp)
                        if qq and s == 4:
                            post(1, *qq)
                        if qq and s == 7:
                            post(2, *qq)
                        if qq and s == 12:
                            post(3, *qq)

            def body(hp, first, last):
                rounds((4 * hp + 1, 1), (hp, 0, first), ((2 * hp + 1, hp, 1), None if first else (2 * hp - 1, hp - 1, 1)))
                rounds((4 * hp + 2, 2), (hp, 1, first), None)
                rounds((4 * hp + 3, 3), (hp, 2, first), (None if last else (2 * hp + 2, hp + 1, 0), (2 * hp, hp, 0)))
                rounds(None if last else (4 * hp + 4, 0), (hp, 3, first), None)

            wait_x(act, 6 * KT - 2)
            wait_x(act, 6 * KT - 1)
            prep(0, 0, 0, 0, gate_out)
            for e in range(1, 4):
                prep(e, 0, 0, 0)
            rounds((0, 0), None, None)
            body(0, True, False)
            n, per = own.n, 4
            with act.Fori(1, NHP - 1) as hp:
                own.r = per * hp - per
                body(hp, False, False)
            assert own.n == n + per
            own.n, own.r = n + per * (NHP - 2), 0
            body(NHP - 1, False, True)
            w_round(N_WO + 1, 0, (w_used, N_WO))
            for e in range(4):
                post(e, 15, NHP - 1, 1)

            def project(i, n0, used, bias):
                for t in range(8):
                    if i or t:
                        w_round(n0 + t + 1, 0, (w_used, used + t))
                    b = None if bias is None else pr[:, bias + t:bias + t + 1]

                    def empty(lo, hi):
                        if b is None:
                            ins = act.activation(y[:, t, lo:hi], ps[:, t % 4, lo:hi], ACT.Copy)
                        else:
                            ins = act.activation(y[:, t, lo:hi], ps[:, t % 4, lo:hi], ACT.Identity, bias=b)
                        if hi == T:
                            ins.then_inc(mm_evac, 1)
                        else:
                            act.preload_act_table_set(LN_EXP)
                            root((sum_full, 2 * i + 1), None, lo, hi)

                    full = (w_used, used + t + 1)
                    square_y(i, t, ((half_full, i // 2 + 1) if t == 7 else full, full), ps[:, t % 4, :], b, empty)

            project(0, N_WO, N_WO, None)
            norms(0, 0, (N_F0 + 1, (w_used, N_F0)))

            def ffn(L, n0, used):
                s0 = n0 % 2

                def silu(g, i, count):
                    act.wait_ge(w_used, count)
                    if not (type(g) is int and g == 0):
                        act.wait_ge(up_mul, 2 * g + i - 1)
                    act.activation(sqb[:, i, :], ps[:, 2 * i, :], ACT.Silu).then_inc(sg_ready, 1)

                def hidden(g, i, buf):
                    act.wait_ge(up_mul, 2 * g + i + 1)
                    act.activation(hidh[:, buf, i, :], tmp[:, i, :], ACT.Copy).then_inc(hid_hi, 1)

                G = FG * L
                silu(G, 0, used + 1)
                w_round(n0 + 2, 0, (w_used, used + 1))
                w_round(n0 + 3, 0, (w_used, used + 2))
                hidden(G, 0, 0)
                silu(G, 1, used + 3)
                w_round(n0 + 4, 0, (w_used, used + 3))
                hidden(G, 1, 0)

                def group(g, n, r, u, prev, buf):
                    w_round(n + 1, r, prev)
                    silu(g, 0, u + 1)
                    w_round(n + 2, r, (w_used, u + 1))
                    w_round(n + 3, r, (w_used, u + 2))
                    hidden(g, 0, buf)
                    silu(g, 1, u + 3)
                    w_round(n + 4, r, (w_used, u + 3))
                    w_round(n + 5, r, (w_used, u + 4))
                    hidden(g, 1, buf)
                    w_round(n + 6, r, (dn_full, 8 * (g - 1) + 4))

                group(G + 1, n0 + 4, 0, used + 4, (w_used, used + 4), 1)
                with act.Fori(0, (FG - 3) // 2) as i:
                    for v in range(2):
                        g = 2 * i + G + 2 + v
                        group(g, n0 + 10 + 6 * v, 12 * i, 8 * i + used + 8 + 4 * v, (dn_full, 8 * (g - 2) + 8), v)
                g = G + FG - 1
                group(g, n0 + 4 + 6 * (FG - 2), 0, used + 4 * (FG - 1), (dn_full, 8 * (g - 2) + 8), 0)
                w_round(n0 + 6 * FG - 1, 0, (dn_full, 8 * (g - 1) + 8))
                for m in range(8):
                    if m == 4 and L == 0:
                        w_round(n0 + 6 * FG, 0, (dn_full, 8 * g + 4))
                    square_y(2 * L + 1, m, 2 * ((dn_evac, 8 * g + m + 1),), y[:, m, :])

            U0 = N_F0 + 4 * FG
            ffn(0, N_F0, N_F0)
            norms(1, 1, (N_QKV + 1, (dn_full, 8 * FG)))

            def heads_in(l):
                if l >= 1:
                    w_round(N_QKV + l + 1, 0, (w_used, U0 + l))
                act.wait_ge(w_used, U0 + l + 1)
                if l >= 2:
                    act.wait_ge(rot_r, l - 1)
                act.activation(tmp[:, l % 2, :], ps[:, l % 2, :], ACT.Identity,
                               bias=pr[:, BQKV + l:BQKV + l + 1]).then_inc(mm_evac, 1)

            def v_out(l):
                act.wait_ge(rot_f, l + 1)
                kv = 2 * (l - 10)
                act.activation(vt[:, 1:NB + 1, kv:kv + 2, :].rearrange("p n a b -> p n (a b)"),
                               ps[:, 2 + l % 2, :].rearrange("p (n c) -> p n c", c=P), ACT.Copy).then_inc(rot_r, 1)

            for l in range(11):
                heads_in(l)
            act.wait_ge(kd_r, 2)
            act.wait_ge(rot_r, 10)
            for i in range(2):
                act.activation(kd[HD:P, 2 * i, P:], kd[0:HD, 2 * i, P:], ACT.Copy)
                ins = act.activation(kd[0:HD, 2 * i + 1, P:], kd[HD:P, 2 * i + 1, P:], ACT.Copy)
            ins.then_inc(kd_r, 1)
            heads_in(11)
            v_out(10)
            v_out(11)

            def soft(it):
                act.wait_ge(nm_r, it + 1)
                b = it % 3
                act.activation(st[:, b, 3, :], st[:, b, 3, :], ACT.Exp)
                for i in range(4):
                    ins = act.activation(sc[:, b, i * 2 * P:(i + 1) * 2 * P], sc[:, b, i * 2 * P:(i + 1) * 2 * P], ACT.Exp,
                                         bias=st[:, b, 1, i:i + 1], accum_out=st[:, b, 2, i:i + 1])
                ins.then_inc(p_r, 1)

            def turned(it):
                act.wait_ge(pt_f, it + 1)
                if it >= 1:
                    act.wait_ge(o_f, it)
                act.activation(pT[:].rearrange("p a b -> p (a b)"), ps[:, 2, :], ACT.Copy).then_inc(pt_r, 1)

            def o_hi(it):
                n, kv = it // NKV, it % NKV
                act.wait_ge(o_f, it + 1)
                act.activation(xh[:, 2 * kv:2 * kv + 2, n * P:(n + 1) * P],
                               bank(6 + it % 2)[:, 0:2 * P].rearrange("p (a b) -> p a b", b=P), ACT.Copy).then_inc(o_r, 1)

            IT = NB * NKV
            act.preload_act_table_set(LN_EXP)
            soft(0)
            soft(1)
            for it in range(IT):
                if it >= 1:
                    o_hi(it - 1)
                turned(it)
                if it + 2 < IT:
                    soft(it + 2)
            o_hi(IT - 1)
            act.wait_ge(oz_r, IT)
            project(2, N_AO, U0 + 12, BO)
            norms(2, 2, (N_F1 + 1, (w_used, U0 + 20)))
            ffn(1, N_F1, U0 + 20)
            norms(3, None)

        @block.vector
        def _(dve):
            own = Own(dve, dve_own)
            stt = dve.scalar_tensor_tensor

            def w_lo(n, ws):
                dve.wait_ge(w_hi, n + 1)
                dve.tensor_tensor(wl[:, ws, :], wst[:, ws, :], wh[:, ws, :].bitcast(F32), ALU.subtract).then_inc(w_split, 1)

            def x_split(b, make):
                def lo(kt):
                    dve.wait_ge(xhi_ready, b + kt + 1)
                    dve.tensor_tensor(xl[:, kt, :], xs(kt), xh[:, kt, :].bitcast(F32), ALU.subtract).then_inc(x_ready, 1)
                for kt in range(KT):
                    if b + kt >= 4:
                        wait_x(dve, b + kt - 4)
                    make(kt).then_inc(xn_ready, 1)
                    if kt >= 2 and kt % 2 == 0:
                        lo(kt - 2)
                lo(KT - 2)

            def g_col(c, kt):
                return pr[:, c + kt:c + kt + 1]

            def add_square(i, t, hfs=(0, 1)):
                for hf in hfs if t == KT - 1 else (0,):
                    lo, hi = halves()[hf] if t == KT - 1 else (0, T)
                    dve.wait_ge(acc_sq, (KT + 1) * i + t + hf + 1)
                    if t > 1:
                        dve.wait_ge(acc_done, KT * i + t - 1)
                    dve.tensor_tensor(rstd[:, lo:hi], rstd[:, lo:hi], sqb[:, t % 2, lo:hi], ALU.add).then_inc(acc_done, 1)

            def residual(i, gc, ready):
                for hf, (lo, hi) in enumerate(halves()):
                    dve.wait_ge(rs_ready, 4 * i + hf + 2)
                    if ready and hf == 0:
                        dve.wait_ge(*ready)
                    for j in range(KT // 2):
                        for kt in (2 * j + 1, 2 * j):
                            stt(out=y[:, kt, lo:hi], in0=y[:, kt, lo:hi], scalar=g_col(gc, kt), in1=rstd[:, lo:hi],
                                op0=ALU.mult, op1=ALU.mult).then_inc(scaled, 1)
                        dve.wait_ge(scaled, 2 * KT * i + KT * hf + 2 * j + 2)
                        dve.tensor_tensor(x[:, 2 * j, lo:hi], x[:, 2 * j, lo:hi], y[:, 2 * j, lo:hi], ALU.add).then_inc(res_done, 1)

            def normed(i, p, gc, second):
                def lo_part(hf, kt):
                    lo, hi = halves()[hf]
                    dve.wait_ge(xhi_ready, xn(p, hf, kt) + 1)
                    dve.tensor_tensor(xl[:, kt, lo:hi], xs(kt)[:, lo:hi], xh[:, kt, lo:hi].bitcast(F32), ALU.subtract).then_inc(x_ready, 1)

                for hf, (lo, hi) in enumerate(halves()):
                    dve.wait_ge(rs_ready, 4 * i + hf + 4)
                    for kt in range(KT):
                        if kt >= 4:
                            wait_x(dve, xn(p, hf, kt - 4))
                        stt(out=xs(kt)[:, lo:hi], in0=x[:, kt, lo:hi], scalar=g_col(gc, kt), in1=rstd[:, lo:hi],
                            op0=ALU.mult, op1=ALU.mult).then_inc(xn_ready, 1)
                        if kt >= 2 and kt % 2 == 0:
                            lo_part(hf, kt - 2)
                    lo_part(hf, KT - 2)
                    if hf == 0:
                        w_lo(second, second % 2)

            for kt in range(1, KT):
                dve.wait_ge(sq_ready, kt + 1)
                if kt >= 2:
                    dve.wait_ge(sq_used, kt)
                ins = dve.tensor_tensor(rstd[:], rstd[:], sqb[:, kt % 2, :], ALU.add)
                ins.then_inc(sq_used, 2 if kt == 1 else 1)
            dve.wait_ge(rs_ready, 1)
            dve.wait_ge(pool_own, 1)

            def first_norm(kt):
                stt(out=h[:, kt, 1:T + 1], in0=h[:, kt, 1:T + 1], scalar=g_col(G0, kt), in1=rstd[:],
                    op0=ALU.mult, op1=ALU.mult).then_inc(h_ready, 1)
                if kt % 2 == 0:
                    dve.wait_ge(h_ready, kt + 1)
                    dve.tensor_tensor(xx[:, kt, :], h[:, kt, 0:T], h[:, kt, 1:T + 1], ALU.subtract).then_inc(xx_ready, 1)

            def mixed(j):
                def make(kt):
                    if j == 0 and kt + 2 < KT:
                        first_norm(kt + 2)
                    if j == 0:
                        dve.wait_ge(xx_odd if kt % 2 else xx_ready, kt // 2 + 1)
                        dve.wait_ge(h_ready, kt + 1)
                    return stt(out=xs(kt), in0=xx[:, kt, :], scalar=g_col(MIX + KT * j, kt), in1=h[:, kt, 1:T + 1],
                               op0=ALU.mult, op1=ALU.add)
                return make

            first_norm(0)
            first_norm(1)
            w_lo(0, 0)
            x_split(0, mixed(0))
            for n in range(N_LORA + 3):
                w_lo(n + 1, (n + 1) % 2)
                if n in MIX_LAST:
                    j = MIX_LAST.index(n) + 1
                    x_split(KT * j, mixed(j))

            def evac(s, g, k, a):
                b = bank(inv_bank(s, g))
                tt0 = TT[a][g][:, 0].rearrange("p a b -> p (a b)")
                if s < 2:
                    dve.wait_ge(st_full[s], 2 * k + g + 1)
                    if s == 0 and not (type(k) is int and k < 2):
                        dve.wait_ge(y_tile, 2 * k - 3 + g)
                    dve.tensor_tensor(Sm[a][g][:, s].rearrange("p (i j) c -> p i (j c)", i=2),
                                      b.rearrange("p (i c) -> p i c", i=2),
                                      m_si.unsqueeze(1).to_broadcast([P, 2, 2 * P]), ALU.mult).then_inc(st_evac[s], 1)
                    if s == 1:
                        dve.wait_ge(st_evac[0], 2 * k + g + 1)
                        dve.wait_ge(st_evac[1], 2 * k + g + 1)
                        dve.tensor_tensor(Dt[g][:], Sm[a][g][:, :, 0, :], mu8.unsqueeze(1).to_broadcast([P, 2, P]),
                                          ALU.mult).then_inc(dt_ready, 1)
                        if g == 1:
                            for gg in range(2):
                                dve.wait_ge(dt_ready, 2 * k + gg + 1)
                                dve.tensor_tensor(TT[a][gg][:, 0], Dt[gg][:], ident.unsqueeze(1).to_broadcast([P, 2, P]),
                                                  ALU.add).then_inc(x1_ready, 1)
                elif s == 5:
                    dve.wait_ge(st_full[5], 2 * k + g + 1)
                    dve.tensor_tensor(tt0, tt0, b[:, 0:2 * P], ALU.add)
                    dve.tensor_copy(Dn[g][:].rearrange("p a b -> p (a b)"), b[:, 2 * P:4 * P]).then_inc(st_evac[5], 1)
                elif s in (6, 13):
                    dve.wait_ge(st_full[s], 2 * k + g + 1)
                    dve.tensor_tensor(tt0, tt0, b[:, 0:2 * P], ALU.add).then_inc(st_evac[s], 1)
                elif s in (9, 11):
                    dve.wait_ge(st_full[s], 2 * k + g + 1)
                    tt = TT[a][g][:].rearrange("p a b c -> p (a b c)")
                    dve.tensor_tensor(tt, tt, b, ALU.add).then_inc(st_evac[s], 1)

            def reset(hp, first):
                if first:
                    dve.memset(rhs_sb[:], 0.0)
                else:
                    dve.wait_ge(ds_full, 16 * hp)
                    dve.wait_ge(sp_ready, 16 * hp)
                dve.memset(S[:], 0.0).then_inc(s_ready, 1)

            def scan(f, hp, u, first):
                c, ph = f // 3, f % 3
                a, pc = u % 2, u // 2
                n = 16 * hp + 4 * u + c
                pe_col = pend[:, pc, 4 * a + c:4 * a + c + 1]
                if ph == 0:
                    dve.wait_ge(s_ready, n + 1)
                    dve.tensor_scalar(SP[:], S[:], pe_col, None, ALU.mult).then_inc(sp_ready, 1)
                elif ph == 2 and not (u == 3 and c == 3):
                    dve.wait_ge(ds_full, n + 1)
                    dve.wait_ge(sp_ready, n + 1)
                    b = bank(B_SC)
                    for i in range(2):
                        hh = slice(HD * i, HD * i + HD)
                        ins = stt(out=S[hh, hh], in0=b[hh, 2 * P + HD * i:2 * P + HD * i + HD], scalar=pe_col[hh, :], in1=SP[hh, hh],
                                  op0=ALU.mult, op1=ALU.add)
                    ins.then_inc(s_ready, 1)

            def prep(e, r, hp, pc, after):
                if e == 0:
                    if pc == 0:
                        src = pr[:, W0:W0 + 40].rearrange("p (v h) -> p v h", h=NHP)[:, :, hp:hp + 1] if type(hp) is int else \
                            pr[:, W0:W0 + 40].rearrange("p (v h) -> p v h", h=NHP)[:, :, bass.ds(hp, 1)]
                        own.link(dve.tensor_copy(pcp[:, 0:5].unsqueeze(2), src))
                        dve.tensor_scalar(pcp[:, 5:6], pcp[:, 3:4], -1.0, 1.0, ALU.mult, ALU.add).then_inc(pp_r, 1)
                elif e == 1:
                    dve.wait_ge(zw_e, r + 1)
                    dve.tensor_tensor_scan(T1, rst, T0, 0.0, ALU.mult, ALU.add).then_inc(s_r, 1)
                    dve.wait_ge(s_r, r + 1)
                    dve.tensor_tensor(T0, T1, T0, ALU.subtract).then_inc(sm_r, 1)
                elif e == 2:
                    dve.wait_ge(ss_f, r + 1)
                    dve.tensor_scalar(T6, bank(B_AUX1), 1e-24, None, ALU.max).then_inc(ss_e, 1)
                elif e == 3:
                    dve.wait_ge(P_r, r + 1)
                    dve.wait_ge(r_in, 16 * (r + 1))
                    if after is not None:
                        dve.wait_ge(y_tile, after)
                    dve.tensor_tensor(Rt[:, pc, :], rin[:], T2, ALU.mult)
                elif e == 4:
                    dve.wait_ge(rinv_r, r + 1)
                    dve.wait_ge(za_e, r + 1)
                    own.link(stt(out=T7, in0=kin[:], scalar=pcp[:, 2:3], in1=T6, op0=ALU.mult, op1=ALU.mult))
                    stt(out=At[:, pc, :], in0=T7, scalar=-1.0, in1=T4, op0=ALU.mult, op1=ALU.mult)
                elif e == 5:
                    own.link(dve.tensor_tensor(T7, T7, T5, ALU.mult))
                    dve.tensor_tensor(Bt[:, pc, :], T7, T3, ALU.mult)
                elif e == 6:
                    own.link(dve.tensor_scalar(T5, T5, pcp[:, 3:4], pcp[:, 5:6], ALU.mult, ALU.add))
                    own.link(dve.tensor_tensor(T5, T5, kin[:], ALU.mult))
                elif e == 7:
                    dve.tensor_tensor(Kt[:, pc, :], T5, T3, ALU.mult)
                elif e == 8:
                    stt(out=T6, in0=rin[:], scalar=pcp[:, 4:5], in1=T5, op0=ALU.mult, op1=ALU.mult).then_inc(rk_r, 1)
                    dve.tensor_copy(pend[:, pc, :], T2.rearrange("p (n c) -> p n c", c=C)[:, :, C - 1]).then_inc(prep_done, 1)
                else:
                    dve.wait_ge(bon_f, r + 1)
                    dve.wait_ge(v_in[pc], 16 * (hp + 1))
                    dve.tensor_tensor(bon[:, pc, :], bank(B_AUX0), vin[:, pc, :], ALU.mult).then_inc(bon_e, 1)

            def post(e, p, hp, pc):
                if e == 0:
                    if pc == 0:
                        src = pr[:, LNW:LNW + 16].rearrange("p (v h) -> p v h", h=NHP)
                        src = src[:, :, hp:hp + 1] if type(hp) is int else src[:, :, bass.ds(hp, 1)]
                        dve.tensor_copy(pcq[:].unsqueeze(2), src).then_inc(pq_r, 1)
                    dve.wait_ge(mean_f, p + 1)
                    stt(out=ysb[:], in0=bank(B_AUX0), scalar=-1.0 / HD, in1=ysb[:], op0=ALU.mult, op1=ALU.add).then_inc(yc_r, 1)
                elif e == 1:
                    dve.wait_ge(var_e, p + 1)
                    dve.wait_ge(g_f, p + 1)
                    dve.wait_ge(pq_r, hp + 1)
                    own.link(stt(out=zt, in0=ysb[:], scalar=pcq[:, 0:1], in1=psq, op0=ALU.mult, op1=ALU.mult))
                    own.link(stt(out=zt, in0=zt, scalar=pcq[:, 1:2], in1=bon[:, pc, :], op0=ALU.add, op1=ALU.add))
                    dve.tensor_tensor(zt, zt, bank(B_AUX1), ALU.mult).then_inc(z_r, 1)
                else:
                    dve.wait_ge(zhi_r, p + 1)
                    cols = slice(pc * HALF, pc * HALF + HALF)
                    dve.tensor_tensor(xl[:, hp, cols], zt, xh[:, hp, cols].bitcast(F32), ALU.subtract).then_inc(z_ready, 1)

            def rounds(inv, sc, busy):
                if sc and sc[1] == 0:
                    reset(sc[0], sc[2])
                for s in range(14):
                    if busy and busy[0] and s == 0:
                        prep(0, *busy[0])
                    if inv:
                        evac(s, 0, inv[0], inv[1] % 2)
                    if sc and s >= 2:
                        scan(s - 2, *sc)
                    if inv:
                        evac(s, 1, inv[0], inv[1] % 2)
                    if busy:
                        pp, qq = busy
                        if pp and s == 2:
                            prep(1, *pp)
                        if qq and s == 3:
                            post(0, *qq)
                        if pp and s == 4:
                            prep(2, *pp)
                        if pp and 5 <= s <= 10:
                            prep(s - 2, *pp)
                        if qq and s == 11:
                            post(1, *qq)
                        if pp and s == 13:
                            prep(9, *pp)
                        if qq and s == 13:
                            post(2, *qq)

            own.n = own.r = 0
            dve.wait_ge(a_in, 16)
            wait_x(dve, 6 * KT - 1)
            for e in range(10):
                prep(e, 0, 0, 0, None)
            rounds((0, 0), None, None)

            def body(hp, first, last):
                rounds((4 * hp + 1, 1), (hp, 0, first),
                       ((2 * hp + 1, hp, 1, None if first else 8 * hp), None if first else (2 * hp - 1, hp - 1, 1)))
                rounds((4 * hp + 2, 2), (hp, 1, first), None)
                rounds((4 * hp + 3, 3), (hp, 2, first),
                       (None if last else (2 * hp + 2, hp + 1, 0, 8 * hp + 4), (2 * hp, hp, 0)))
                rounds(None if last else (4 * hp + 4, 0), (hp, 3, first), None)

            body(0, True, False)
            n = own.n
            per = 13
            with dve.Fori(1, NHP - 1) as hp:
                own.r = per * hp - per
                body(hp, False, False)
            assert own.n == n + per, own.n - n
            own.n, own.r = n + per * (NHP - 2), 0
            body(NHP - 1, False, True)
            w_lo(N_WO + 1, (N_WO + 1) % 2)
            for e in range(3):
                post(e, 15, NHP - 1, 1)

            for t in range(8):
                if t:
                    w_lo(N_WO + t + 1, (N_WO + t + 1) % 2)
                if t >= 1:
                    add_square(0, t)
            residual(0, G0 + KT, (x_in, 16))
            normed(0, 0, G0 + 2 * KT, N_F0 + 1)

            def ffn(L, n0):
                s0 = n0 % 2
                G = FG * L

                def hidden(g, i):
                    dve.wait_ge(sg_ready, 2 * g + i + 1)
                    dve.wait_ge(w_used, used(g, i))
                    dve.tensor_tensor(tmp[:, i, :], sqb[:, i, :], ps[:, 2 * i + 1, :], ALU.mult).then_inc(up_mul, 1)

                def hidden_lo(g, i, buf):
                    dve.wait_ge(hid_hi, 2 * g + i + 1)
                    dve.tensor_tensor(hidl[:, buf, i, :], tmp[:, i, :], hidh[:, buf, i, :].bitcast(F32),
                                      ALU.subtract).then_inc(hid_ready, 1)

                def used(g, i):
                    return (N_F0 if L == 0 else N_F0 + 4 * FG + 20) + 4 * (g - G) + 2 * i + 2

                def add(g, m):
                    dve.wait_ge(dn_full, 8 * g + m + 1)
                    dve.tensor_tensor(y[:, m, :], y[:, m, :], ps[:, m % 4, :], ALU.add).then_inc(dn_evac, 1)

                for t in (2, 3):
                    w_lo(n0 + t, (s0 + t) % 2)
                hidden(G, 0)
                hidden_lo(G, 0, 0)
                w_lo(n0 + 4, s0)
                hidden(G, 1)
                hidden_lo(G, 1, 0)
                dve.wait_ge(y_zero, L + 1)

                def group(g, n, buf):
                    for t in (1, 2, 3):
                        w_lo(n + t, (s0 + t) % 2)
                    hidden(g, 0)
                    hidden_lo(g, 0, buf)
                    w_lo(n + 4, s0)
                    w_lo(n + 5, 1 - s0)
                    hidden(g, 1)
                    hidden_lo(g, 1, buf)
                    for m in range(4):
                        add(g - 1, m)
                    w_lo(n + 6, s0)
                    for m in range(4, 8):
                        add(g - 1, m)

                group(G + 1, n0 + 4, 1)
                with dve.Fori(0, (FG - 3) // 2) as i:
                    for v in range(2):
                        group(2 * i + G + 2 + v, 12 * i + n0 + 10 + 6 * v, v)
                group(G + FG - 1, n0 + 4 + 6 * (FG - 2), 0)
                w_lo(n0 + 6 * FG - 1, 1 - s0)
                for m in range(8):
                    if m == 4 and L == 0:
                        w_lo(n0 + 6 * FG, s0)
                    add(G + FG - 1, m)
                    if m >= 2:
                        add_square(2 * L + 1, m - 1)
                add_square(2 * L + 1, 7)

            ffn(0, N_F0)
            residual(1, G0 + 3 * KT, None)
            normed(1, 1, G0 + 4 * KT, N_QKV + 1)

            def rotate(l):
                raw, rot, b = tmp[:, l % 2, :], ps[:, 2 + l % 2, :], sqb[:, l % 2, :]
                dve.wait_ge(mm_evac, 8 + l + 1)
                dve.wait_ge(rot_f, l + 1)
                own.link(dve.tensor_tensor(b, rot, sinT, ALU.mult))
                own.link(dve.tensor_tensor(raw, raw, cosT, ALU.mult))
                if l < 8:
                    own.link(dve.tensor_tensor(raw, raw, b, ALU.add))
                    dve.tensor_scalar(q[:, l, :], raw, SCALE, None, ALU.mult).then_inc(rot_r, 1)
                else:
                    kv = 2 * (l - 8)
                    dve.tensor_tensor(kd[0:HD, kv, P:], raw[0:HD, :], b[0:HD, :], ALU.add).then_inc(kd_r, 1)
                    dve.tensor_tensor(kd[HD:P, kv + 1, P:], raw[HD:P, :], b[HD:P, :], ALU.add).then_inc(rot_r, 1)

            for l in range(12):
                if l >= 1:
                    w_lo(N_QKV + l + 1, (N_QKV + l + 1) % 2)
                if l == 1:
                    dve.wait_ge(a_in, 32)
                    dve.wait_ge(pad_r, 1)
                    dve.wait_ge(x_out, 16)
                if 1 <= l <= 10:
                    rotate(l - 1)

            def masked(it):
                n, kv = it // NKV, it % NKV
                b = it % 3
                dve.wait_ge(s_f, it + 1)
                if it >= 3:
                    dve.wait_ge(pt_f, it - 2)
                s3 = sc[:, b, :].rearrange("p (i c) -> p i c", c=2 * P)
                dve.tensor_tensor(s3, ps[:, it % 2, :].rearrange("p (i c) -> p i c", c=2 * P),
                                  msk[min(n, 1)].unsqueeze(1).to_broadcast([P, 4, 2 * P]), ALU.add).then_inc(sm_m, 1)
                dve.wait_ge(sm_m, it + 1)
                own.link(dve.tensor_reduce(st[:, b, 0, :], s3, AX_X, ALU.max))
                sk = pr[:, SINK + 4 * kv:SINK + 4 * kv + 4]
                own.link(dve.tensor_tensor(st[:, b, 0, :], st[:, b, 0, :], sk, ALU.max))
                own.link(dve.tensor_scalar(st[:, b, 1, :], st[:, b, 0, :], -1.0, None, ALU.mult))
                dve.tensor_tensor(st[:, b, 3, :], st[:, b, 1, :], sk, ALU.add).then_inc(nm_r, 1)

            def denominators(it):
                b = it % 3
                dve.wait_ge(p_r, it + 1)
                own.link(dve.tensor_tensor(st[:, b, 4, :], st[:, b, 2, :], st[:, b, 3, :], ALU.add))
                dve.reciprocal(st[:, b, 5, :], st[:, b, 4, :]).then_inc(den_r, 1)

            def o_lo(it):
                n, kv = it // NKV, it % NKV
                dve.wait_ge(o_r, it + 1)
                dst = slice(n * P, (n + 1) * P)
                dve.tensor_tensor(xl[:, 2 * kv:2 * kv + 2, dst], bank(6 + it % 2)[:, 0:2 * P].rearrange("p (a b) -> p a b", b=P),
                                  xh[:, 2 * kv:2 * kv + 2, dst].bitcast(F32), ALU.subtract).then_inc(oz_r, 1)

            IT = NB * NKV
            masked(0)
            masked(1)
            denominators(0)
            for it in range(IT):
                if it + 2 < IT:
                    masked(it + 2)
                if it + 1 < IT:
                    denominators(it + 1)
                if it >= 1:
                    o_lo(it - 1)
            o_lo(IT - 1)
            for t in range(8):
                w_lo(N_AO + t + 1, (N_AO + t + 1) % 2)
                if t >= 1:
                    add_square(2, t)
            residual(2, G0 + 5 * KT, (x_in, 32))
            normed(2, 2, G0 + 6 * KT, N_F1 + 1)
            ffn(1, N_F1)
            residual(3, G0 + 7 * KT, None)


def lay_out(i):
    f = {k: np.asarray(v) for k, v in i.items()}

    def tiles(w):
        k, n = w.shape
        return w.reshape(k // P, P, n // P, P).transpose(2, 1, 0, 3).reshape(n // P, P, -1)

    def wide(w):
        return np.concatenate([w, np.zeros((w.shape[0], P - w.shape[1]), w.dtype)], 1)

    def ffn(L):
        gu, dn = tiles(f["ffn_w_gate_up"][L]), f["ffn_w_down"][L]
        dn = dn.reshape(FG, 2, P, 2, HALF).transpose(0, 3, 2, 1, 4).reshape(FG, 2, P, T)
        seq = []
        for g in range(FG + 1):
            if g < FG:
                for t in (2 * g, 2 * g + 1):
                    seq += [gu[t], gu[D_FF // P + t]]
            if g >= 1:
                seq += [dn[g - 1, 0], dn[g - 1, 1]]
        return np.stack(seq)

    wt = np.concatenate([
        tiles(f["rwkv_w_rkv"][0, 0]), tiles(f["rwkv_w_rkv"][0, 1]), tiles(f["rwkv_w_rkv"][0, 2]),
        tiles(wide(f["rwkv_w1"][0])), tiles(wide(f["rwkv_a1"][0])), tiles(f["rwkv_g1"][0]),
        tiles(f["rwkv_w_o"][0]), ffn(0), tiles(f["attn_w_qkv"][0]), tiles(f["attn_w_o"][0]), ffn(1)])

    def cols(v):
        return v.reshape(-1, P).T

    sinks = f["attn_sinks"][0].reshape(NKV, 2, 2).transpose(0, 2, 1).reshape(1, -1)
    one = np.ones((P, 1), np.float32)
    par = np.concatenate([
        cols(f["norm_g"]), cols(f["rwkv_x_mix"]), cols(f["rwkv_w0"]), cols(f["rwkv_a0"]), cols(f["rwkv_k_k"]),
        cols(f["rwkv_k_a"]), cols(f["rwkv_r_k"]), cols(f["rwkv_lnx_w"]), cols(f["rwkv_lnx_b"]),
        cols(f["attn_b_qkv"]), cols(f["attn_b_o"]), np.repeat(sinks, P, 0),
        np.full((P, 1), RMS_EPS, np.float32), np.full((P, 1), GN_EPS, np.float32),
        np.full((P, 1), 0.5 * LN_SHIFT * np.log(2.0), np.float32)], 1)

    def tall(w):
        w = np.concatenate([w, np.zeros((P - w.shape[0], D), w.dtype)], 0)
        return w.reshape(P, NHP, P).transpose(1, 0, 2)

    lora2 = np.stack([tall(f["rwkv_w2"][0]), tall(f["rwkv_a2"][0]), tall(f["rwkv_g2"][0])], 2)
    xT = f["x"][0].T.reshape(KT, P, T).transpose(1, 0, 2)
    base, rw, at = shape_constants()
    return [np.ascontiguousarray(a) for a in (xT, wt, par, lora2, base, rw, at)]


def kernel(**inputs):
    import concourse.bacc as bacc
    from concourse.bass_utils import run_bass_kernel_spmd

    nc = bacc.Bacc("TRN2", target_bir_lowering=False, num_devices=1)
    names = ("xT", "wt", "par", "lora2", "cbase", "crw", "cat")
    arrays = dict(zip(names, lay_out(inputs)))
    aps = [nc.dram_tensor(n, arrays[n].shape, F32, kind="ExternalInput").ap() for n in names]
    out = nc.dram_tensor("out", [P, KT, T], F32, kind="ExternalOutput").ap()
    build_program(nc, *aps, out)
    r = run_bass_kernel_spmd(nc, [arrays], core_ids=[0])
    got = r.results[0]["out"]
    return np.ascontiguousarray(got.transpose(1, 0, 2).reshape(1, D, T).transpose(0, 2, 1))
```
